# Optimizing a Trainium2 kernel written in Bass

```python
import math
import numpy as np
import jax
import jax.numpy as jnp
from jax import lax

D_MODEL = 1024
BATCH = 1
SEQ = 512
DEPTH = 2

GRID_W = 64
CTX_LEN = 256
N_MIXERS = 4
GROUP_WIDTH = D_MODEL // N_MIXERS
MIX_WIDTH = N_MIXERS * GROUP_WIDTH
HEAD_DIM = 64
D_FF = 4 * D_MODEL
EPS = 1e-6
NEG_INF = -1e30
ROPE_BASE = 10000.0

DA_HEADS = GROUP_WIDTH // HEAD_DIM
DA_QK_DIM = HEAD_DIM // 2
DA_V_DIM = HEAD_DIM
DA_Q_BLOCK = 128
HG_HEADS = 4
HG_DK = GROUP_WIDTH // HG_HEADS
HG_DV = GROUP_WIDTH // HG_HEADS
HG_CHUNK = 64
NA_HEADS = GROUP_WIDTH // HEAD_DIM
NA_KH = 8
NA_KW = 16
NA_Q_BLOCK_W = 16
NA_BAND_W = 2 * NA_KW
SW_HEADS = GROUP_WIDTH // HEAD_DIM
SW_KV_HEADS = 2
SW_GROUPS = SW_HEADS // SW_KV_HEADS
SW_WINDOW = 128
SW_BLOCK = 128

IN_SIZES = (GROUP_WIDTH, GROUP_WIDTH, GROUP_WIDTH,
            GROUP_WIDTH, GROUP_WIDTH, GROUP_WIDTH, GROUP_WIDTH, GROUP_WIDTH,
            GROUP_WIDTH, GROUP_WIDTH, GROUP_WIDTH,
            SW_HEADS * HEAD_DIM, SW_KV_HEADS * HEAD_DIM, SW_KV_HEADS * HEAD_DIM)
IN_COLS = sum(IN_SIZES)

kernel_name = 'hybrid_parallel_head_dit_block'

def rmsnorm(x, g):
    xf = x.astype(jnp.float32)
    y = xf * lax.rsqrt(jnp.mean(xf * xf, axis=-1, keepdims=True) + EPS)
    return (y * g.astype(jnp.float32)).astype(x.dtype)

def split_heads(x, n_heads, head_dim):
    b, s, _ = x.shape
    return x.reshape(b, s, n_heads, head_dim).transpose(0, 2, 1, 3)

def merge_heads(x):
    b, n, s, d = x.shape
    return x.transpose(0, 2, 1, 3).reshape(b, s, n * d)

def split_cols(p):
    idx = np.cumsum(IN_SIZES)[:-1].tolist()
    return jnp.split(p, idx, axis=-1)

def axial_rope_tables(n_tokens, rot_dim, dtype):
    t = jnp.arange(n_tokens, dtype=jnp.int32)
    row = (t // GRID_W).astype(jnp.float32)
    col = (t % GRID_W).astype(jnp.float32)
    axis_dim = rot_dim // 2
    inv_freq = ROPE_BASE ** (-jnp.arange(0, axis_dim, 2, dtype=jnp.float32) / axis_dim)
    ang_r = row[:, None] * inv_freq
    ang_c = col[:, None] * inv_freq
    return tuple(a.astype(dtype) for a in (jnp.cos(ang_r), jnp.sin(ang_r), jnp.cos(ang_c), jnp.sin(ang_c)))

def rotate(x, cos, sin):
    x1, x2 = jnp.split(x, 2, axis=-1)
    return jnp.concatenate([x1 * cos - x2 * sin, x1 * sin + x2 * cos], axis=-1)

def apply_axial_rope(x, tables):
    cos_r, sin_r, cos_c, sin_c = tables
    x_row, x_col = jnp.split(x, 2, axis=-1)
    return jnp.concatenate([rotate(x_row, cos_r, sin_r), rotate(x_col, cos_c, sin_c)], axis=-1)

def adaln_params(cond, w_mod, b_mod):
    return jnp.split(jax.nn.silu(cond) @ w_mod + b_mod, 6, axis=-1)

def modulate(x, g, shift, scale):
    return rmsnorm(x, g) * (1.0 + scale) + shift

def squared_relu_mlp(h, w1, w2):
    return jnp.square(jax.nn.relu(h @ w1)) @ w2

def diff_attention(lat, ctx, q_gain, k_gain, lam_vecs, sub_gain, lam_init, rope_tabs, need_ctx):
    q_l, k_l, v_l = lat
    q_c, k_c, v_c = ctx

    def qk(x, gain, rope):
        b, s, _ = x.shape
        x = rmsnorm(split_heads(x, 2 * DA_HEADS, DA_QK_DIM), gain)
        if rope:
            x = apply_axial_rope(x, rope_tabs)
        return x.reshape(b, DA_HEADS, 2, s, DA_QK_DIM)

    ql, kl = qk(q_l, q_gain, True), qk(k_l, k_gain, True)
    kc = qk(k_c, k_gain, False)
    vl, vc = split_heads(v_l, DA_HEADS, DA_V_DIM), split_heads(v_c, DA_HEADS, DA_V_DIM)
    k_all = jnp.concatenate([kc, kl], axis=3)
    v_all = jnp.concatenate([vc, vl], axis=2)
    lv = lam_vecs.astype(jnp.float32)
    lam = jnp.exp(jnp.sum(lv[0] * lv[1])) - jnp.exp(jnp.sum(lv[2] * lv[3])) + lam_init
    scale = DA_QK_DIM ** -0.5

    def attend(q, k, v):
        s = jnp.einsum('bhmqd,bhmkd->bhmqk', q, k).astype(jnp.float32) * scale
        a = jax.nn.softmax(s, axis=-1)
        a = a[:, :, 0] - lam * a[:, :, 1]
        return jnp.einsum('bhqk,bhkd->bhqd', a.astype(v.dtype), v)

    def finish(o):
        return merge_heads(rmsnorm(o, sub_gain) * (1.0 - lam_init))

    b, _, _, s, _ = ql.shape
    nb = s // DA_Q_BLOCK
    qb = ql.reshape(b, DA_HEADS, 2, nb, DA_Q_BLOCK, DA_QK_DIM).transpose(3, 0, 1, 2, 4, 5)
    o = lax.map(lambda q_blk: attend(q_blk, k_all, v_all), qb)
    o = o.transpose(1, 2, 0, 3, 4).reshape(b, DA_HEADS, s, DA_V_DIM)
    out_c = finish(attend(qk(q_c, q_gain, False), kc, vc)) if need_ctx else None
    return finish(o), out_c

def hgrn2_chunk_scan(q, k, v, log_f, state0, need_out):
    b, h, t, _ = q.shape
    dv = v.shape[-1]
    n = t // HG_CHUNK

    def chunks(a):
        return a.astype(jnp.float32).reshape(b, h, n, HG_CHUNK, a.shape[-1]).transpose(2, 0, 1, 3, 4)

    lower = jnp.tril(jnp.ones((HG_CHUNK, HG_CHUNK), dtype=bool))[:, :, None]

    def step(state, inp):
        qc, kc, vc, gc = inp
        cum = jnp.cumsum(gc, axis=2)
        last = cum[:, :, -1]
        new_state = jnp.exp(last)[..., None] * state + jnp.einsum(
            'bhsk,bhsv->bhkv', kc * jnp.exp(last[:, :, None] - cum), vc)
        if not need_out:
            return new_state, None
        o_inter = jnp.einsum('bhtk,bhkv->bhtv', qc * jnp.exp(cum), state)
        rel = jnp.where(lower, cum[:, :, :, None, :] - cum[:, :, None, :, :], -jnp.inf)
        scores = jnp.einsum('bhtk,bhsk,bhtsk->bhts', qc, kc, jnp.exp(rel))
        o_intra = jnp.einsum('bhts,bhsv->bhtv', scores, vc)
        return new_state, o_inter + o_intra

    state, out = lax.scan(step, state0.astype(jnp.float32),
                          (chunks(q), chunks(k), chunks(v), chunks(log_f)))
    if need_out:
        out = out.transpose(1, 2, 0, 3, 4).reshape(b, h, t, dv).astype(v.dtype)
    return out, state

def hgrn2_mixer(lat, ctx, lower_bound, out_gain, need_ctx):
    def prep(parts):
        q, i, g, f_fw, f_bw = parts
        dirs = []
        for f, lb in ((f_fw, lower_bound[0]), (f_bw, lower_bound[1])):
            f = lb + (1.0 - lb) * jax.nn.sigmoid(f.astype(jnp.float32))
            dirs.append((split_heads(jnp.log(f), HG_HEADS, HG_DK), split_heads(1.0 - f, HG_HEADS, HG_DK)))
        return split_heads(q, HG_HEADS, HG_DK), split_heads(i, HG_HEADS, HG_DV), g, dirs

    ql, vl, gl, dirs_l = prep(lat)
    qc, vc, gc, dirs_c = prep(ctx)
    b = ql.shape[0]
    zero_state = jnp.zeros((b, HG_HEADS, HG_DK, HG_DV), jnp.float32)
    out_l, out_c = 0.0, 0.0
    for d, flip in enumerate((False, True)):
        rev = (lambda a: jnp.flip(a, axis=2)) if flip else (lambda a: a)
        logf_c, k_c = dirs_c[d]
        logf_l, k_l = dirs_l[d]
        o_c, s_c = hgrn2_chunk_scan(rev(qc), rev(k_c), rev(vc), rev(logf_c), zero_state, need_ctx)
        o_l, _ = hgrn2_chunk_scan(rev(ql), rev(k_l), rev(vl), rev(logf_l), s_c, True)
        out_l = out_l + rev(o_l)
        if need_ctx:
            out_c = out_c + rev(o_c)

    def finish(o, g):
        return merge_heads(rmsnorm(o, out_gain)) * jax.nn.silu(g)

    return finish(out_l, gl), (finish(out_c, gc) if need_ctx else None)

def neighbourhood_attention(lat, ctx, q_gain, k_gain, rpb, need_ctx):
    q_l, k_l, v_l = lat
    q_c, k_c, v_c = ctx
    ql = rmsnorm(split_heads(q_l, NA_HEADS, HEAD_DIM), q_gain)
    kl = rmsnorm(split_heads(k_l, NA_HEADS, HEAD_DIM), k_gain)
    vl = split_heads(v_l, NA_HEADS, HEAD_DIM)
    kc = rmsnorm(split_heads(k_c, NA_HEADS, HEAD_DIM), k_gain)
    vc = split_heads(v_c, NA_HEADS, HEAD_DIM)
    b, h, s, d = ql.shape
    rows = s // GRID_W
    kh = min(NA_KH, rows)
    ncb = GRID_W // NA_Q_BLOCK_W
    scale = d ** -0.5
    q_cols = (jnp.arange(ncb) * NA_Q_BLOCK_W)[:, None] + jnp.arange(NA_Q_BLOCK_W)
    win_start = jnp.clip(q_cols - NA_KW // 2, 0, GRID_W - NA_KW)
    band_start = jnp.clip(jnp.arange(ncb) * NA_Q_BLOCK_W - NA_KW // 2, 0, GRID_W - NA_BAND_W)
    key_cols = band_start[:, None] + jnp.arange(NA_BAND_W)
    kcol = key_cols[:, None, :]
    col_valid = (kcol >= win_start[..., None]) & (kcol < win_start[..., None] + NA_KW)
    dj = jnp.clip(kcol - q_cols[..., None], -(NA_KW - 1), NA_KW - 1) + (NA_KW - 1)
    rpb_cols = rpb.astype(jnp.float32)[:, :, dj]
    row_start = jnp.clip(jnp.arange(rows) - NA_KH // 2, 0, rows - kh)
    kl_g = kl.reshape(b, h, rows, GRID_W, d)
    vl_g = vl.reshape(b, h, rows, GRID_W, d)
    q_rows = ql.reshape(b, h, rows, ncb, NA_Q_BLOCK_W, d).transpose(2, 0, 1, 3, 4, 5)
    n_lat = kh * NA_BAND_W

    def one_row(args):
        r, rs, q = args
        k_band = lax.dynamic_slice_in_dim(kl_g, rs, kh, axis=2)[:, :, :, key_cols]
        v_band = lax.dynamic_slice_in_dim(vl_g, rs, kh, axis=2)[:, :, :, key_cols]
        s_lat = jnp.einsum('bhcqd,bhrckd->bhcqrk', q, k_band).astype(jnp.float32) * scale
        di = rs + jnp.arange(kh) - r + (NA_KH - 1)
        bias = rpb_cols[:, di].transpose(0, 2, 3, 1, 4)
        s_lat = jnp.where(col_valid[:, :, None, :], s_lat + bias, NEG_INF)
        s_ctx = jnp.einsum('bhcqd,bhkd->bhcqk', q, kc).astype(jnp.float32) * scale
        a = jax.nn.softmax(jnp.concatenate(
            [s_lat.reshape(b, h, ncb, NA_Q_BLOCK_W, n_lat), s_ctx], axis=-1), axis=-1).astype(q.dtype)
        a_lat = a[..., :n_lat].reshape(b, h, ncb, NA_Q_BLOCK_W, kh, NA_BAND_W)
        return (jnp.einsum('bhcqrk,bhrckd->bhcqd', a_lat, v_band)
                + jnp.einsum('bhcqk,bhkd->bhcqd', a[..., n_lat:], vc))

    o = lax.map(one_row, (jnp.arange(rows), row_start, q_rows))
    o = o.transpose(1, 2, 0, 3, 4, 5).reshape(b, h, s, d)
    out_c = None
    if need_ctx:
        qc = rmsnorm(split_heads(q_c, NA_HEADS, HEAD_DIM), q_gain)
        sc = jnp.einsum('bhqd,bhkd->bhqk', qc, kc).astype(jnp.float32) * scale
        out_c = merge_heads(jnp.einsum('bhqk,bhkd->bhqd', jax.nn.softmax(sc, axis=-1).astype(vc.dtype), vc))
    return merge_heads(o), out_c

def softmax_with_sink(scores, sink_b):
    sink_col = jnp.broadcast_to(sink_b, scores.shape[:-1] + (1,))
    return jax.nn.softmax(jnp.concatenate([sink_col, scores], axis=-1), axis=-1)[..., 1:]

def window_gqa(lat, ctx, q_gain, k_gain, sink, rope_tabs, need_ctx):
    q_l, k_l, v_l = lat
    q_c, k_c, v_c = ctx

    def qheads(x, rope):
        b_, s_, _ = x.shape
        x = rmsnorm(split_heads(x, SW_HEADS, HEAD_DIM), q_gain)
        if rope:
            x = apply_axial_rope(x, rope_tabs)
        return x.reshape(b_, SW_KV_HEADS, SW_GROUPS, s_, HEAD_DIM)

    ql = qheads(q_l, True)
    kl = apply_axial_rope(rmsnorm(split_heads(k_l, SW_KV_HEADS, HEAD_DIM), k_gain), rope_tabs)
    vl = split_heads(v_l, SW_KV_HEADS, HEAD_DIM)
    kc = rmsnorm(split_heads(k_c, SW_KV_HEADS, HEAD_DIM), k_gain)
    vc = split_heads(v_c, SW_KV_HEADS, HEAD_DIM)
    b, _, _, s, d = ql.shape
    n_ctx = kc.shape[2]
    nb = s // SW_BLOCK
    scale = d ** -0.5
    sink_f = sink.astype(jnp.float32).reshape(SW_KV_HEADS, SW_GROUPS)
    qb = ql.reshape(b, SW_KV_HEADS, SW_GROUPS, nb, SW_BLOCK, d)

    def band(a):
        a = jnp.pad(a, ((0, 0), (0, 0), (SW_BLOCK, SW_BLOCK), (0, 0))).reshape(b, SW_KV_HEADS, nb + 2, SW_BLOCK, d)
        return jnp.concatenate([a[:, :, :-2], a[:, :, 1:-1], a[:, :, 2:]], axis=3)

    kw, vw = band(kl), band(vl)
    q_pos = jnp.arange(s).reshape(nb, SW_BLOCK)
    k_pos = (jnp.arange(nb) * SW_BLOCK - SW_BLOCK)[:, None] + jnp.arange(3 * SW_BLOCK)
    valid = ((jnp.abs(k_pos[:, None, :] - q_pos[:, :, None]) <= SW_WINDOW)
             & (k_pos >= 0)[:, None, :] & (k_pos < s)[:, None, :])
    s_win = jnp.where(valid, jnp.einsum('bkgnqd,bknsd->bkgnqs', qb, kw).astype(jnp.float32) * scale, NEG_INF)
    s_ctx = jnp.einsum('bkgnqd,bkcd->bkgnqc', qb, kc).astype(jnp.float32) * scale
    a = softmax_with_sink(jnp.concatenate([s_ctx, s_win], axis=-1),
                          sink_f[None, :, :, None, None, None]).astype(vl.dtype)
    o = (jnp.einsum('bkgnqc,bkcd->bkgnqd', a[..., :n_ctx], vc)
         + jnp.einsum('bkgnqs,bknsd->bkgnqd', a[..., n_ctx:], vw))
    out_l = merge_heads(o.reshape(b, SW_HEADS, s, d))
    out_c = None
    if need_ctx:
        qc = qheads(q_c, False)
        sc = jnp.einsum('bkgqd,bkcd->bkgqc', qc, kc).astype(jnp.float32) * scale
        ac = softmax_with_sink(sc, sink_f[None, :, :, None, None]).astype(vc.dtype)
        out_c = merge_heads(jnp.einsum('bkgqc,bkcd->bkgqd', ac, vc).reshape(b, SW_HEADS, n_ctx, d))
    return out_l, out_c

def setup_inputs(seed: int = 0) -> dict:
    key = jax.random.key(seed)
    ks = jax.random.split(key, 24)

    def nrm(k, shape, s):
        return s * jax.random.normal(k, shape, jnp.float32)

    def gain(k, shape):
        return 1.0 + 0.02 * jax.random.normal(k, shape, jnp.float32)

    L = DEPTH
    return {
        'x': nrm(ks[0], (BATCH, SEQ, D_MODEL), 1.0),
        'c': nrm(ks[1], (BATCH, D_MODEL), 1.0),
        'ctx': nrm(ks[2], (BATCH, CTX_LEN, D_MODEL), 1.0),
        'c_ctx': nrm(ks[3], (D_MODEL,), 1.0),
        'w_mod': nrm(ks[4], (L, D_MODEL, 6 * D_MODEL), 0.5 * D_MODEL ** -0.5),
        'b_mod': nrm(ks[5], (L, 6 * D_MODEL), 0.01),
        'norm1_g': gain(ks[6], (L, D_MODEL)),
        'norm2_g': gain(ks[7], (L, D_MODEL)),
        'w_in': nrm(ks[8], (L, D_MODEL, IN_COLS), D_MODEL ** -0.5),
        'w_out': nrm(ks[9], (L, MIX_WIDTH, D_MODEL), MIX_WIDTH ** -0.5),
        'da_q_gain': gain(ks[10], (L, DA_QK_DIM)),
        'da_k_gain': gain(ks[11], (L, DA_QK_DIM)),
        'da_lambda': nrm(ks[12], (L, 4, DA_QK_DIM), 0.1),
        'da_sub_gain': gain(ks[13], (L, DA_V_DIM)),
        'hg_lb_logits': nrm(ks[14], (L, 2, GROUP_WIDTH), 0.5),
        'hg_out_gain': gain(ks[15], (L, HG_DV)),
        'na_q_gain': gain(ks[16], (L, HEAD_DIM)),
        'na_k_gain': gain(ks[17], (L, HEAD_DIM)),
        'na_rpb': nrm(ks[18], (L, NA_HEADS, 2 * NA_KH - 1, 2 * NA_KW - 1), 0.1),
        'sw_q_gain': gain(ks[19], (L, HEAD_DIM)),
        'sw_k_gain': gain(ks[20], (L, HEAD_DIM)),
        'sw_sink': nrm(ks[21], (L, SW_HEADS), 1.0),
        'w_ff1': nrm(ks[22], (L, D_MODEL, D_FF), D_MODEL ** -0.5),
        'w_ff2': nrm(ks[23], (L, D_FF, D_MODEL), D_FF ** -0.5),
    }

def reference(x, c, ctx, c_ctx, w_mod, b_mod, norm1_g, norm2_g, w_in, w_out,
              da_q_gain, da_k_gain, da_lambda, da_sub_gain, hg_lb_logits, hg_out_gain,
              na_q_gain, na_k_gain, na_rpb, sw_q_gain, sw_k_gain, sw_sink, w_ff1, w_ff2):
    seq = x.shape[1]
    rope_da = axial_rope_tables(seq, DA_QK_DIM, x.dtype)
    rope_sw = axial_rope_tables(seq, HEAD_DIM, x.dtype)
    lb_soft = jax.nn.softmax(hg_lb_logits.astype(jnp.float32), axis=0)
    lower_bounds = jnp.cumsum(lb_soft, axis=0) - lb_soft[0]
    for layer in range(DEPTH):
        need_ctx = layer < DEPTH - 1
        lam_init = 0.8 - 0.6 * math.exp(-0.3 * layer)
        mod_l = [m[:, None, :] for m in adaln_params(c, w_mod[layer], b_mod[layer])]
        mod_c = adaln_params(c_ctx, w_mod[layer], b_mod[layer])
        p_l = split_cols(modulate(x, norm1_g[layer], mod_l[0], mod_l[1]) @ w_in[layer])
        p_c = split_cols(modulate(ctx, norm1_g[layer], mod_c[0], mod_c[1]) @ w_in[layer])
        a_l, a_c = diff_attention(p_l[0:3], p_c[0:3], da_q_gain[layer], da_k_gain[layer], da_lambda[layer],
                                  da_sub_gain[layer], lam_init, rope_da, need_ctx)
        b_l, b_c = hgrn2_mixer(p_l[3:8], p_c[3:8], lower_bounds[layer], hg_out_gain[layer], need_ctx)
        n_l, n_c = neighbourhood_attention(p_l[8:11], p_c[8:11], na_q_gain[layer], na_k_gain[layer],
                                           na_rpb[layer], need_ctx)
        w_l, w_c = window_gqa(p_l[11:14], p_c[11:14], sw_q_gain[layer], sw_k_gain[layer], sw_sink[layer],
                              rope_sw, need_ctx)
        x = x + mod_l[2] * (jnp.concatenate([a_l, b_l, n_l, w_l], axis=-1) @ w_out[layer])
        x = x + mod_l[5] * squared_relu_mlp(modulate(x, norm2_g[layer], mod_l[3], mod_l[4]),
                                            w_ff1[layer], w_ff2[layer])
        if need_ctx:
            ctx = ctx + mod_c[2] * (jnp.concatenate([a_c, b_c, n_c, w_c], axis=-1) @ w_out[layer])
            ctx = ctx + mod_c[5] * squared_relu_mlp(modulate(ctx, norm2_g[layer], mod_c[3], mod_c[4]),
                                                    w_ff1[layer], w_ff2[layer])
    return x


_drawn_inputs = setup_inputs


def setup_inputs(seed=0):
    import zlib

    import numpy as np

    out = dict(_drawn_inputs(seed))
    spreads = {}
    factors = {'norm1_g': 8.0,
     'norm2_g': 4.432,
     'da_q_gain': 8.0,
     'da_k_gain': 8.0,
     'da_lambda': 3.409,
     'da_sub_gain': 64.0,
     'hg_out_gain': 8.0,
     'na_q_gain': 8.0,
     'na_k_gain': 8.0,
     'na_rpb': 23.101,
     'sw_q_gain': 8.0,
     'sw_k_gain': 8.0,
     'sw_sink': 8.0}
    for name, (base, spread) in spreads.items():
        noise = np.random.default_rng([zlib.crc32(name.encode()), seed]).standard_normal(out[name].shape)
        drawn = base * np.exp(spread * noise) if base else spread * noise
        out[name] = jnp.asarray(drawn.astype(out[name].dtype))
    for name, factor in factors.items():
        out[name] = (out[name] * factor).astype(out[name].dtype)
    return out
```

```python
import math
from contextlib import ExitStack

import numpy as np

import concourse.bass as bass
from concourse import mybir

F32 = mybir.dt.float32
F32R = mybir.dt.float32r
U8 = mybir.dt.uint8
ALU = mybir.AluOpType
ACT = mybir.ActivationFunctionType
AX = mybir.AxisListType

P = 128
D = 1024
KT = D // P
LAT, CTX = 512, 256
T = LAT + CTX
DEPTH = 2
GW = 256
UC = 256
GRID = 64
EPS = 1e-6
NEG = -1e30
SEGS = ((0, LAT), (LAT, T))

R_BMOD, R_N1, R_N2, R_C, R_CC, R_LB, R_G = 0, 48, 56, 64, 72, 80, 88
(G_DAQ, G_DAK, G_DAS, G_HGO, G_NAQ, G_NAK, G_SWQ, G_SWK) = range(R_G, R_G + 8)
NROWS = 96

C_ID, C_B32, C_B64, C_ONE, C_P32, C_P64 = (i * P for i in range(6))
C_CA, C_SA, C_CS, C_SS = (6 * P + i * LAT for i in range(4))
C_SW = 6 * P + 4 * LAT
C_NA = C_SW + 2 * P
C_SGN = C_NA + 96
NCF = C_SGN + 2
B_LEV, B_RST, NCB = 0, 7 * P, 7 * P + T


def shape_constants():
    f = np.zeros((P, NCF), np.float32)
    i = np.arange(P)
    f[:, C_ID:C_ID + P] = np.eye(P)
    f[:, C_B32:C_B32 + P] = (i[:, None] // 32 == i // 32) / 32.0
    f[:, C_B64:C_B64 + P] = (i[:, None] // 64 == i // 64) / 64.0
    f[:, C_ONE:C_ONE + P] = 1.0 / D
    t = np.arange(LAT)
    for hd, cp, cc, cs in ((32, C_P32, C_CA, C_SA), (64, C_P64, C_CS, C_SS)):
        axis, half = hd // 2, hd // 4
        inv = (np.float32(10000.0) ** (-np.arange(0, axis, 2, dtype=np.float32) / np.float32(axis))).astype(np.float32)
        within = i % axis
        pos = np.where(((i % hd) // axis == 0)[:, None], (t // GRID)[None], (t % GRID)[None]).astype(np.float32)
        ang = (pos * inv[within % half][:, None]).astype(np.float32)
        f[:, cc:cc + LAT] = np.cos(ang)
        f[:, cs:cs + LAT] = np.sin(ang)
        for o in range(P):
            if o % axis < half:
                f[o + half, cp + o] = -1.0
            else:
                f[o - half, cp + o] = 1.0
    f[:, C_SW:C_SW + P] = np.where(i[None] >= i[:, None], 0.0, NEG)
    f[:, C_SW + P:C_SW + 2 * P] = np.where(i[None] <= i[:, None], 0.0, NEG)
    qc = i // 8
    for v, (band, q0) in enumerate(((0, 0), (8, 16), (32, 48))):
        key = band + np.arange(32)
        start = np.clip(q0 + qc - 8, 0, GRID - 16)[:, None]
        f[:, C_NA + 32 * v:C_NA + 32 * v + 32] = np.where((key >= start) & (key < start + 16), 0.0, NEG)
    f[:, C_SGN] = np.where(i < 64, -1.0, 1.0)
    f[:, C_SGN + 1] = -f[:, C_SGN]
    b = np.zeros((P, NCB), np.float32)
    x = i[:, None] ^ i[None]
    for j in range(6):
        b[:, j * P:(j + 1) * P] = (x >= 2 ** j) & (x < 2 ** (j + 1))
    b[:, 6 * P:7 * P] = x == 0
    t = np.arange(T)
    b[:, B_RST:] = np.where(i[:, None] < 64, t % 64 != 0, t % 64 != 63)
    return f, b


def unit_order():
    units = []
    for l in range(DEPTH):
        units += [("mod", l, j, i) for j in range(6) for i in range(4)]
        units += [("prj", l, n) for n in ("NAq", "NAk", "NAv", "SWq", "SWkv", "DAq", "DAk", "DAv",
                                          "HGq0", "HGq1", "HGf0", "HGf1", "HGi", "HGg")]
        units += [("out", l, j) for j in range(4)]
        for q in range(4):
            units += [("ff1", l, q, j) for j in range(4)] + [("ff2", l, q, j) for j in range(4)]
    return units


COLS = {"DAq": 0, "DAk": 256, "DAv": 512, "HGq": 768, "HGi": 1024, "HGg": 1280, "HGf": 1536,
        "NAq": 2048, "NAk": 2304, "NAv": 2560, "SWq": 2816, "SWkv": 3072}


def build(nc, t):
    units = unit_order()
    index = {u: i for i, u in enumerate(units)}
    split_no, mod_no = {}, {}
    for u in units:
        (mod_no if u[0] == "mod" else split_no).setdefault(u, len(mod_no if u[0] == "mod" else split_no))

    def unit_dmas(u):
        kind, l = u[:2]
        rows = lambda w: w.rearrange("(k p) n -> p k n", p=P)
        if kind == "mod":
            c = u[2] * D + u[3] * UC
            return [((0, UC, 1), rows(t["w_mod"][l])[:, :, c:c + UC])]
        if kind == "out":
            return [((0, UC, 1), rows(t["w_out"][l])[:, :, u[2] * UC:(u[2] + 1) * UC])]
        if kind == "ff1":
            c = u[2] * D + u[3] * UC
            return [((0, UC, 1), rows(t["w_ff1"][l])[:, :, c:c + UC])]
        if kind == "ff2":
            return [((0, UC, 1), rows(t["w_ff2"][l][u[2] * D:(u[2] + 1) * D, :])[:, :, u[3] * UC:(u[3] + 1) * UC])]
        n = u[2]
        w = rows(t["w_in"][l])
        if n in ("HGq0", "HGq1"):
            h = 2 * int(n[3])
            return [((64 * (2 * a + b), 64, 1), w[:, :, 768 + 64 * (h + a):768 + 64 * (h + a) + 64])
                    for a in range(2) for b in range(2)]
        if n in ("HGf0", "HGf1"):
            h = 2 * int(n[3])
            return [((64 * (2 * a + b), 64, 1), w[:, :, 1536 + 256 * b + 64 * (h + a):1536 + 256 * b + 64 * (h + a) + 64])
                    for a in range(2) for b in range(2)]
        if n == "SWq":
            return [((64 * s, 64, 1), w[:, :, 2816 + 64 * h:2816 + 64 * h + 64]) for s, h in enumerate((0, 2, 1, 3))]
        c = COLS[n]
        return [((0, UC, 1), w[:, :, c:c + UC])]

    landed_at, per_slot = {}, [0, 0]
    for i, u in enumerate(units):
        per_slot[i % 2] += 16 * len(unit_dmas(u))
        landed_at[u] = per_slot[i % 2]

    groups, group_no = [], {}

    def chunks_of(u):
        l = u[1]
        lat_only = l == DEPTH - 1
        if u[0] == "mod":
            return ["row"] + (["turn"] if u[3] == 3 else [])
        if u[0] in ("out", "ff1", "ff2"):
            return [(ct, s) for ct in range(2) for s in range(1 if lat_only else 2)]
        n = u[2]
        if n in ("DAv", "HGi"):
            return [("tok", tt) for tt in range(6)]
        if lat_only and n in ("NAq", "SWq", "DAq", "HGg", "HGq0", "HGq1"):
            return [(ct, 0) for ct in range(2)]
        return [(ct, s) for ct in range(2) for s in range(2)]

    for l in range(DEPTH):
        order = [u for u in units if u[1] == l]
        for u in order:
            if u[:3] == ("prj", l, "NAq"):
                for s in range(2):
                    group_no[("ms", l, 1, s)] = len(groups)
                    groups.append(None)
            if u[:4] == ("ff1", l, 0, 0):
                for s in range(1 if l == DEPTH - 1 else 2):
                    group_no[("ms", l, 2, s)] = len(groups)
                    groups.append(None)
            for c in chunks_of(u):
                group_no[(u, c)] = len(groups)
                groups.append(None)

    ctx = ExitStack()
    with ctx:
        def sem(name):
            return ctx.enter_context(nc.semaphore(name))

        base = (nc.sbuf_base + 31) // 32 * 32
        at = [base]

        def place(name, shape, dt=F32, offset=None):
            size = int(np.prod(shape[1:])) * (1 if dt == U8 else 4)
            size = (size + 31) // 32 * 32
            o = at[0] if offset is None else offset
            if offset is None:
                at[0] += size
            assert o + size <= nc.sbuf_usable_end, (name, o + size - nc.sbuf_usable_end)
            tensor = nc.alloc_sbuf_tensor_at(name, shape, dt, offset=o)
            return tensor, o + size

        xT, _ = place("xT", [P, KT, T])
        cf, _ = place("cf", [P, NCF])
        cb, _ = place("cb", [P, NCB], U8)
        raw, _ = place("raw", [P, 2, KT, UC])
        whi, _ = place("whi", [P, 2, KT, UC], F32R)
        wlo, _ = place("wlo", [P, 2, KT, UC], F32R)
        prow, _ = place("prow", [P, DEPTH, P])
        pcol, _ = place("pcol", [P, DEPTH, NROWS])
        mods, _ = place("mods", [P, DEPTH, 48, 2])
        silu_c, _ = place("silu_c", [P, KT, 2])
        siluw, _ = place("siluw", [P, 16])
        amod, _ = place("amod", [P, KT, 2])
        lamv, _ = place("lamv", [P, DEPTH, 4, 32])
        lamt, _ = place("lamt", [P, 2, 32])
        lams, _ = place("lams", [P, 4])
        nlam, _ = place("nlam", [P, 1])
        sink, _ = place("sink", [P, DEPTH, 4])
        gq, _ = place("gq", [P, 4])
        lbt, _ = place("lbt", [P, 6, 4])
        small, _ = place("small", [P, 32])
        epsc, _ = place("epsc", [P, 1])
        x0 = at[0]
        xhi, _ = place("xhi", [P, KT, T], F32R)
        xlo, _ = place("xlo", [P, KT, T], F32R)
        scratch0 = at[0]
        hhi, e = place("hhi", [P, KT, T], F32R, scratch0)
        hlo, e = place("hlo", [P, KT, T], F32R, e)
        frel, _ = place("frel", [P, 2, LAT], F32, e)
        mix, mix_end = place("mix", [P, KT, T], F32, scratch0)
        mrow, _ = place("mrow", [2, D], F32, x0 + KT * T * 4)
        xin, _ = place("xin", [P, 6, D], F32, x0)
        cbf, _ = place("cbf", [P, NCB], F32, scratch0)
        bias, e = place("bias", [P, 3, 4, 256], F32, mix_end)
        na_end = e
        e1, e = place("e1", [8, 4, 8, 31], F32, na_end)
        e2, e = place("e2", [8, 4, 63, 8], F32, e)
        nsq, e = place("nsq", [P, 2, T], F32, e)
        nt1, e = place("nt1", [P, 2, T], F32, e)
        nrs, e = place("nrs", [P, T], F32, e)

        phase_bufs = {}

        def phase(name, start, shapes):
            e = start
            for n, shape in shapes:
                phase_bufs[name, n], e = place(f"{name}_{n}", shape, F32, e)

        phase("NA", na_end, [("xr", [P, 4, T]), ("vt", [P, 2, T]), ("y", [P, 2, T]), ("v", [P, 9, 256])])
        phase("NAp", na_end + 4 * T * 4, [("p", [P, 2, 512]), ("pt", [P, 2, 512])])
        phase("SW", mix_end, [("xr", [P, 3, T]), ("vt", [P, 1, T]), ("y", [P, 2, T]), ("rot", [P, 2, LAT]),
                              ("v", [P, 6, P]), ("p", [P, 2, 640]), ("pt", [P, 2, 640])])
        phase("DA", mix_end, [("xr", [P, 4, T]), ("v", [P, 6, 256]), ("y", [P, 2, T]), ("rot", [P, 2, LAT]),
                              ("p", [P, 2, 2, T]), ("pt", [P, 2, T])])
        phase("HG", mix_end, [("q", [P, 4, T]), ("cum", [P, 4, T]), ("k", [P, 4, T]), ("v", [P, 6, 256]),
                              ("tmp", [P, 2, T]), ("ref", [P, 4, 64]), ("at", [P, 2, 4, P]), ("gate", [P, 2, T])])
        phase("HGx", x0, [("qd", [P, 6, 4, P]), ("kd", [P, 6, 4, P]), ("u", [P, 12, 256]), ("s", [P, 12, 256])])
        buf = lambda a, b: phase_bufs[a, b]

        gp = ctx.enter_context(nc.psum_tensor("gp", [P, 2, 512], F32))
        sp_ = ctx.enter_context(nc.psum_tensor("sp", [P, 4, 512], F32))
        tp = ctx.enter_context(nc.psum_tensor("tp", [P, 512], F32))
        op_ = ctx.enter_context(nc.psum_tensor("op", [P, 512], F32))

        consts_in = sem("consts_in")
        params_in = sem("params_in")
        x_in = sem("x_in")
        landed = [sem("landed0"), sem("landed1")]
        hi_done = sem("hi_done")
        lo_done = sem("lo_done")
        group_done = sem("group_done")
        bank_free = [sem("bank_free0"), sem("bank_free1")]
        dve_step = sem("dve_step")
        act_step = sem("act_step")
        out_done = sem("out_done")
        S = {}
        counts = {}
        PER_LAYER = {"HG_" + n: c for n, c in dict(
            tot=1, kready=4, interread=4, ke=4, cumdone=4, oms=2, a=42, decay=1, osq=2, fa=4, qexp=4, eg=4, lev=36,
            ktcopied=6, kexp=4, dexp=36, oread=6, d=36, kt=6, state=22, orstd=2, aused=42, uread=12, u=12, inter=2,
            lastd=4, lnf=4, qe=4, sc=42).items()}
        for which in (1, 2):
            PER_LAYER.update({f"sq{which}": KT, f"sq{which}_read": KT - 1, f"rstd{which}": 1, f"y{which}": KT,
                              f"xhi{which}": KT, f"xn{which}": KT})
        PER_LAYER.update(h_sq=64, h_hi=64, h_split=64, mixhi=KT, mixsplit=KT, rpb_in=16 * 8, bias_in=16 * 48,
                         e2_zero=1, e2_done=1, mix_ready=1, DA_final=1, DA_oms=2, DA_orstd=2, DA_osq=2)

        def ls(l, name):
            key = name if name in PER_LAYER else f"{name}_{l}"
            if key not in S:
                S[key] = sem(key)
            return S[key]

        def upto(l, name, value):
            return ls(l, name), value + l * PER_LAYER.get(name, 0)

        N = lambda u, c: group_no[u, c]

        def wait_used(eng, u):
            eng.wait_ge(group_done, N(u, [c for c in chunks_of(u) if c != "turn"][-1]) + 1)

        def wait_read(eng, u, n=None):
            if n is None:
                for c in chunks_of(u)[-2:]:
                    wait_read(eng, u, N(u, c))
            else:
                eng.wait_ge(bank_free[n % 2], n // 2 + 1)

        bank = lambda n: gp[:, n % 2, :]
        ident = cf[:, C_ID:C_ID + P]

        def jobs_of(m, l):
            jobs = []
            last = l == DEPTH - 1
            if m == "NA":
                for h in range(4):
                    rows = slice(64 * (h % 2), 64 * (h % 2) + 64)
                    q, k = buf("NA", "xr")[rows, h // 2, :], buf("NA", "xr")[rows, 2 + h // 2, :]
                    v = lambda i, h=h: buf("NA", "v")[:, i, 64 * h:64 * h + 64]
                    for cbk in range(4):
                        band = (0, 8, 24, 32)[cbk]
                        jobs.append(dict(q=[q[:, P * cbk:P * cbk + P]], segs=[(0, 256, [k[:, 8 * band:8 * band + 256]], 0),
                                                                              (256, 256, [k[:, LAT:T]], 256)],
                                         bias=(0, 256, bias[:, (0, 1, 1, 2)[cbk], h, :]), rest=(256, 256, 256), n=512,
                                         v=[v(i) for i in ((0, 1), (4, 5), (5, 6), (2, 3))[cbk]] + [v(7), v(8)],
                                         head=h, out=("grid", cbk), rows=rows))
                    for qt in range(0 if last else 2):
                        c = LAT + P * qt
                        jobs.append(dict(q=[q[:, c:c + P]], segs=[(0, 256, [k[:, LAT:T]], 0)], bias=None,
                                         rest=(0, 256, 0), n=256, v=[v(7), v(8)], head=h, out=("plain", c), rows=rows))
            if m == "SW":
                for h in range(4):
                    rows = slice(64 * (h // 2), 64 * (h // 2) + 64)
                    q, k = buf("SW", "xr")[rows, h % 2, :], buf("SW", "xr")[rows, 2, :]
                    v = lambda i, h=h: buf("SW", "v")[:, i, 64 * (h // 2):64 * (h // 2) + 64]
                    orow = slice(64 * (h % 2), 64 * (h % 2) + 64)
                    for n in range(4):
                        a, b = max(n - 1, 0), min(n + 2, 4)
                        w = P * (b - a)
                        masks = []
                        if n > 0:
                            masks.append((0, cf[:, C_SW:C_SW + P]))
                        if n < 3:
                            masks.append((w - P, cf[:, C_SW + P:C_SW + 2 * P]))
                        jobs.append(dict(q=[q[:, P * n:P * n + P]], segs=[(0, w, [k[:, P * a:P * b]], 0), (512, 256, [k[:, LAT:T]], w)],
                                         masks=masks, plain=P * (n - a), n=w + 256, w=w,
                                         v=[v(i) for i in range(a, b)] + [v(4), v(5)], head=h, out=("plain", P * n), rows=orow))
                    for qt in range(0 if last else 2):
                        c = LAT + P * qt
                        jobs.append(dict(q=[q[:, c:c + P]], segs=[(0, 256, [k[:, LAT:T]], 0)], masks=[], plain=None, w=0,
                                         n=256, v=[v(4), v(5)], head=h, out=("plain", c), rows=orow))
            if m == "DA":
                for h in range(4):
                    rows = slice(64 * (h % 2), 64 * (h % 2) + 64)
                    v = lambda i, h=h: buf("DA", "v")[:, i, 64 * h:64 * h + 64]
                    for qt in range(4 if last else 6):
                        qs, ks = [], []
                        for mp in range(2):
                            s = 2 * h + mp
                            r = slice(32 * (s % 4), 32 * (s % 4) + 32)
                            qs.append(buf("DA", "xr")[r, s // 4, P * qt:P * qt + P])
                            ks.append(buf("DA", "xr")[r, 2 + s // 4, :])
                        if qt < 4:
                            segs = [(0, 512, [k[:, 0:LAT] for k in ks], 0), (512, 256, [k[:, LAT:T] for k in ks], 512)]
                            jobs.append(dict(q=qs, segs=segs, n=T, v=[v(i) for i in range(6)], head=h,
                                             out=("plain", P * qt), rows=rows))
                        else:
                            jobs.append(dict(q=qs, segs=[(0, 256, [k[:, LAT:T] for k in ks], 0)], n=256,
                                             v=[v(4), v(5)], head=h, out=("plain", P * qt), rows=rows))
            return jobs

        MIXT = {"DA": 0, "HG": 2, "NA": 4, "SW": 6}
        JOBS = {(m, l): jobs_of(m, l) for m in ("NA", "SW", "DA") for l in range(DEPTH)}

        def pieces(job):
            nk = job["n"] // P
            return [(a, min(a + 4, nk)) for a in range(0, nk, 4)]

        def piece_base(m, l, n):
            return sum(len(pieces(j)) for j in JOBS[m, l][:n])

        def probs(m, n, mp=0):
            if m == "DA":
                return buf("DA", "p")[:, n % 2, mp, :]
            return buf("NAp" if m == "NA" else "SW", "p")[:, n % 2, :]

        def probs_t(m, n):
            return buf("NAp" if m == "NA" else m, "pt")[:, n % 2, :]

        def tiles_of(m):
            if m == "NA":
                return [("NAq", 0, 0), ("NAq", 1, 1), ("NAk", 0, 2), ("NAk", 1, 3)]
            if m == "SW":
                return [("SWq", 0, 0), ("SWq", 1, 1), ("SWkv", 0, 2)]
            return [("DAq", 0, 0), ("DAq", 1, 1), ("DAk", 0, 2), ("DAk", 1, 3)]

        GAIN = {"NAq": 0, "SWq": 1, "DAq": 2}
        AVG = {"NA": C_B64, "SW": C_B64, "DA": C_B32}
        ROPE = {"SW": (C_P64, C_CS, C_SS), "DA": (C_P32, C_CA, C_SA)}

        for m in ("NA", "SW", "DA"):
            jobs0, nt0 = JOBS[m, 0], len(tiles_of(m))
            scored = len(jobs0) * (2 if m == "DA" else 1)
            turned = sum(len(pieces(j)) for j in jobs0)
            PER_LAYER.update({m + "_" + n: c for n, c in dict(
                sqseg=2 * nt0, ln=nt0, ms=nt0, rstd=nt0, scaled=nt0, rot=nt0, rotread=nt0, ready=1, s=scored, max=scored,
                exp=scored, sfree=len(jobs0), p=len(jobs0), o=len(jobs0), oread=len(jobs0), pt=turned,
                ptcopied=turned).items()})
        PER_LAYER.update(NA_vturn=9, NA_vfree=9, SW_vturn=6, SW_vfree=6, x_final=1, lamdot=1, lamexp=1, silu_done=1)

        def tile_len(l, n):
            return LAT if l == DEPTH - 1 and n[2:] == "q" else T

        def tile_segs(l, n):
            return SEGS[:1] if tile_len(l, n) == LAT else SEGS

        def ff_index(l, q, j, c):
            s = 1 if l == DEPTH - 1 else 2
            return ((q * 4 + j) * 2 + c[0]) * s + c[1]

        block = ctx.enter_context(nc.Block())

        @block.sync
        def _(sp):
            sp.dma_start(prow[0:48, :, :], t["b_mod"].rearrange("l (r c) -> r l c", c=P)).then_inc(params_in, 16)
            sp.dma_start(prow[48:56, :, :], t["norm1_g"].rearrange("l (r c) -> r l c", c=P)).then_inc(params_in, 16)
            sp.dma_start(prow[56:64, :, :], t["norm2_g"].rearrange("l (r c) -> r l c", c=P)).then_inc(params_in, 16)
            n = 3
            for l in range(DEPTH):
                sp.dma_start(prow[64:72, l, :], t["c"].rearrange("o (r c) -> (o r) c", c=P)).then_inc(params_in, 16)
                sp.dma_start(prow[72:80, l, :], t["c_ctx"].rearrange("(r c) -> r c", c=P)).then_inc(params_in, 16)
                n += 2
                for l2 in range(DEPTH):
                    for d in range(2):
                        sp.dma_start(prow[80 + 4 * l2:84 + 4 * l2, l, 64 * d:64 * d + 64],
                                     t["hg_lb_logits"][l2, d].rearrange("(h k) -> h k", k=64)).then_inc(params_in, 16)
                        n += 1
                for r, name in enumerate(("da_q_gain", "da_k_gain", "da_sub_gain", "hg_out_gain", "na_q_gain",
                                          "na_k_gain", "sw_q_gain", "sw_k_gain")):
                    g = t[name][l:l + 1, :]
                    w = g.shape[1]
                    for rep in range(P // w):
                        sp.dma_start(prow[88 + r:89 + r, l, rep * w:rep * w + w], g).then_inc(params_in, 16)
                        n += 1
                sp.dma_start(lamv[:, l, :, :], t["da_lambda"][l].partition_broadcast(P)).then_inc(params_in, 16)
                sp.dma_start(sink[:, l, :], t["sw_sink"][l].partition_broadcast(P)).then_inc(params_in, 16)
                n += 2
            counts["params"] = n * 16
            sp.dma_start(cf[:, :], t["cf"]).then_inc(consts_in, 16)
            sp.dma_start(cbf[:, :], t["cb"]).then_inc(consts_in, 16)
            sp.dma_start(xin[:, 0:4, :], t["x"][0].rearrange("(a p) d -> p a d", p=P)).then_inc(x_in, 16)
            sp.dma_start(xin[:, 4:6, :], t["ctx"][0].rearrange("(a p) d -> p a d", p=P)).then_inc(x_in, 16)

            def bias_load(l):
                if l > 0:
                    sp.wait_ge(*upto(l - 1, "x_final", 1))
                else:
                    sp.wait_ge(*upto(0, "start_done", 1))
                sp.wait_ge(*upto(l, "e2_zero", 1))
                for r in range(8):
                    sp.dma_start(e1[r:r + 1, :, :, :], t["na_rpb"][l:l + 1, :, 7 - r:15 - r, :]).then_inc(ls(l, "rpb_in"), 16)
                sp.wait_ge(*upto(l, "e2_done", 1))
                for v, off in enumerate((0, -8, -16)):
                    for qc in range(16):
                        j0 = off - qc + 15 + 16
                        sp.dma_start(bias[8 * qc:8 * qc + 8, v, :, :],
                                     e2[:, :, j0:j0 + 32, :].rearrange("p h j r -> p h (j r)")).then_inc(ls(l, "bias_in"), 16)

            for i, u in enumerate(units):
                if i >= 2:
                    w = units[i - 2]
                    if w[0] == "mod":
                        wait_used(sp, w)
                    else:
                        sp.wait_ge(lo_done, split_no[w] + 1)
                for (c, n, s), src in unit_dmas(u):
                    sp.dma_start(raw[:, i % 2, :, c:c + n], src).then_inc(landed[i % 2], 16)
                if u[0] == "mod" and u[2:] == (0, 1):
                    bias_load(u[1])
            for tt in range(4):
                sp.wait_ge(*upto(0, "y_copied", 2 * tt + 2))
                sp.dma_start(t["out"][0, P * tt:P * tt + P, :], xin[:, tt, :]).then_inc(out_done, 16)
            sp.wait_ge(out_done, 64)

        @block.gpsimd
        def _(pool):
            nc.gpsimd.memset(epsc[:, :], EPS).then_inc(ls(0, "eps_set"), 1)
            for u in units:
                if u[0] == "mod":
                    continue
                s = split_no[u]
                pool.wait_ge(hi_done, s + 1)
                nc.gpsimd.tensor_tensor(wlo[:, s % 2, :, :], raw[:, index[u] % 2, :, :],
                                        whi[:, s % 2, :, :].bitcast(F32), ALU.subtract).then_inc(lo_done, 1)

        @block.tensor
        def _(pe):
            def start_group(n):
                if n >= 2:
                    pe.wait_ge(bank_free[n % 2], n // 2)

            def dense(u, c):
                n = N(u, c)
                s = split_no[u] % 2
                start_group(n)
                hi, lo = (hhi, hlo) if u[0] == "ff2" else (xhi, xlo)
                for k in range(KT):
                    if c[0] == "tok":
                        a, b = P * c[1], P * c[1] + P
                        out = bank(n)[:, 0:UC]
                        trips = ((hi[:, k, a:b], whi[:, s, k, :]), (hi[:, k, a:b], wlo[:, s, k, :]), (lo[:, k, a:b], whi[:, s, k, :]))
                    else:
                        ct, (a, b) = c[0], SEGS[c[1]]
                        out = bank(n)[:, 0:b - a]
                        w0, w1 = P * ct, P * ct + P
                        trips = ((whi[:, s, k, w0:w1], hi[:, k, a:b]), (whi[:, s, k, w0:w1], lo[:, k, a:b]),
                                 (wlo[:, s, k, w0:w1], hi[:, k, a:b]))
                    for j, (lhs, rhs) in enumerate(trips):
                        mm = pe.matmul(out, lhs, rhs, start=(k == 0 and j == 0), stop=(k == KT - 1 and j == 2))
                mm.then_inc(group_done, 1)
                return mm

            def start_unit(u):
                pe.wait_ge(lo_done, split_no[u] + 1)

            def modulation(l, j):
                if j == 0:
                    pe.wait_ge(*upto(l, "silu_done", 1))
                for i in range(4):
                    u = ("mod", l, j, i)
                    n = N(u, "row")
                    start_group(n)
                    pe.wait_ge(landed[index[u] % 2], landed_at[u])
                    for k in range(KT):
                        mm = pe.matmul(bank(n)[0:2, 0:UC], silu_c[:, k, :], raw[:, index[u] % 2, k, :],
                                       start=(k == 0), stop=(k == KT - 1))
                    mm.then_inc(group_done, 1)
                n = N(u, "turn")
                start_group(n)
                for i in range(4):
                    wait_read(pe, None, N(("mod", l, j, i), "row"))
                for i in range(8):
                    mm = pe.transpose(bank(n)[:, 2 * i:2 * i + 2], mrow[0:2, P * i:P * i + P], cf[0:2, C_ID:C_ID + 2])
                mm.then_inc(group_done, 1)

            def norm_sums(l, which):
                segs = SEGS[:1] if (which == 2 and l == DEPTH - 1) else SEGS
                for s, _ in enumerate(segs):
                    start_group(group_no["ms", l, which, s])
                for k in range(KT):
                    pe.wait_ge(*upto(l, f"sq{which}", k + 1))
                    for s, (a, b) in enumerate(segs):
                        n = group_no["ms", l, which, s]
                        mm = pe.matmul(bank(n)[:, 0:b - a], cf[:, C_ONE:C_ONE + P], nsq[:, k % 2, a:b],
                                       start=(k == 0), stop=(k == KT - 1))
                        if k == KT - 1:
                            mm.then_inc(group_done, 1)
                    if k < KT - 1:
                        mm.then_inc(ls(l, f"sq{which}_read"), 1)

            def head_norms(m, l):
                tiles = tiles_of(m)

                def project(i):
                    n, ct, _ = tiles[i]
                    u = ("prj", l, n)
                    if ct == 0:
                        start_unit(u)
                    for s, _ in enumerate(tile_segs(l, n)):
                        mm = dense(u, (ct, s))

                def average(i):
                    pe.wait_ge(*upto(l, m + "_sqseg", sum(len(tile_segs(l, x[0])) for x in tiles[:i + 1])))
                    if i >= 2:
                        pe.wait_ge(*upto(l, m + "_ln", i - 1))
                    for (a, b) in tile_segs(l, tiles[i][0]):
                        mm = pe.matmul(sp_[:, 2 * (i % 2) + (1 if a else 0), 0:b - a], cf[:, AVG[m]:AVG[m] + P],
                                       buf(m, "y")[:, i % 2, a:b], start=True, stop=True)
                    mm.then_inc(ls(l, m + "_ms"), 1)

                def turn(i):
                    if m == "NA":
                        return
                    pe.wait_ge(*upto(l, m + "_scaled", i + 1))
                    if i >= 2:
                        pe.wait_ge(*upto(l, m + "_rotread", i - 1))
                    perm = ROPE[m][0]
                    pe.matmul((tp, op_)[i % 2][:, :], cf[:, perm:perm + P], buf(m, "xr")[:, tiles[i][2], 0:LAT],
                              start=True, stop=True).then_inc(ls(l, m + "_rot"), 1)

                for i in range(len(tiles) + 2):
                    if i < len(tiles):
                        project(i)
                    if 1 <= i <= len(tiles):
                        average(i - 1)
                    if i >= 2:
                        turn(i - 2)
                if m == "NA":
                    u = ("prj", l, "NAv")
                    start_unit(u)
                    for ct in range(2):
                        for s in range(2):
                            mm = dense(u, (ct, s))
                    wait_read(pe, u)
                    for i in range(9):
                        o = 8 * (0, 16, 32, 48, 8, 24, 40)[i] if i < 7 else LAT + P * (i - 7)
                        if i >= 2:
                            pe.wait_ge(*upto(l, "NA_vfree", i - 1))
                        for ct in range(2):
                            mm = pe.transpose((tp, op_)[i % 2][:, P * ct:P * ct + P], buf("NA", "vt")[:, ct, o:o + P], ident)
                        mm.then_inc(ls(l, "NA_vturn"), 1)
                if m == "SW":
                    u = ("prj", l, "SWkv")
                    for s in range(2):
                        mm = dense(u, (1, s))
                    wait_read(pe, u)
                    pe.wait_ge(*upto(l, "SW_rotread", 3))
                    for i in range(6):
                        if i >= 2:
                            pe.wait_ge(*upto(l, "SW_vfree", i - 1))
                        pe.transpose((tp, op_)[i % 2][:, 0:P], buf("SW", "vt")[:, 0, P * i:P * i + P], ident)\
                          .then_inc(ls(l, "SW_vturn"), 1)
                if m == "DA":
                    u = ("prj", l, "DAv")
                    start_unit(u)
                    for tt in range(6):
                        mm = dense(u, ("tok", tt))

            def attention(m, l):
                jobs = JOBS[m, l]
                nm = 2 if m == "DA" else 1
                pe.wait_ge(*upto(l, m + "_ready", 1))

                def scores(n):
                    j = jobs[n]
                    for mp in range(nm):
                        unit = nm * n + mp
                        if unit >= 2:
                            pe.wait_ge(*upto(l, m + ("_exp" if m == "DA" else "_sfree"), unit - 1))
                        for (o, w, ks, _) in j["segs"]:
                            mm = pe.matmul(sp_[:, 2 * (unit % 2) + o // 512, o % 512:o % 512 + w], j["q"][mp], ks[mp],
                                           start=True, stop=True)
                        mm.then_inc(ls(l, m + "_s"), 1)

                def turn_and_weigh(n):
                    j = jobs[n]
                    pe.wait_ge(*upto(l, m + "_p", n + 1))
                    b = piece_base(m, l, n)
                    for i, (k0, k1) in enumerate(pieces(j)):
                        if b + i >= 2:
                            pe.wait_ge(*upto(l, m + "_ptcopied", b + i - 1))
                        for k in range(k0, k1):
                            mm = pe.transpose((tp, op_)[(b + i) % 2][:, P * (k - k0):P * (k - k0) + P], probs(m, n)[:, P * k:P * k + P], ident)
                        mm.then_inc(ls(l, m + "_pt"), 1)
                    pe.wait_ge(*upto(l, m + "_ptcopied", b + len(pieces(j))))
                    if n >= 2:
                        pe.wait_ge(*upto(l, m + "_oread", n - 1))
                    nk = j["n"] // P
                    for k in range(nk):
                        mm = pe.matmul(gp[j["rows"], n % 2, 0:P], j["v"][k], probs_t(m, n)[:, P * k:P * k + P],
                                       start=(k == 0), stop=(k == nk - 1))
                    mm.then_inc(ls(l, m + "_o"), 1)

                scores(0)
                for n in range(len(jobs)):
                    if n + 1 < len(jobs):
                        scores(n + 1)
                    turn_and_weigh(n)
                pe.wait_ge(*upto(l, m + "_oread", len(jobs)))
                if m == "DA":
                    for i in range(2):
                        pe.wait_ge(*upto(l, "DA_osq", i + 1))
                        for s, (a, b) in enumerate(SEGS[:1] if l == DEPTH - 1 else SEGS):
                            mm = pe.matmul(sp_[:, 2 * i + s, 0:b - a], cf[:, C_B64:C_B64 + P], buf("DA", "y")[:, i, a:b],
                                           start=True, stop=True)
                        mm.then_inc(ls(l, "DA_oms"), 1)

            def hgrn(l):
                last = l == DEPTH - 1
                g = lambda name: ls(l, "HG_" + name)
                gupto = lambda name, value: upto(l, "HG_" + name, value)
                q, cum, k_, v = buf("HG", "q"), buf("HG", "cum"), buf("HG", "k"), buf("HG", "v")
                for name in ("HGq0", "HGq1", "HGf0", "HGf1"):
                    u = ("prj", l, name)
                    start_unit(u)
                    for c in chunks_of(u):
                        mm = dense(u, c)
                u = ("prj", l, "HGi")
                start_unit(u)
                for tt in range(6):
                    mm = dense(u, ("tok", tt))
                u = ("prj", l, "HGg")
                start_unit(u)
                for c in chunks_of(u):
                    mm = dense(u, c)
                ntile = 4 if last else 6
                for name in ("HGq0", "HGq1", "HGi"):
                    wait_read(pe, ("prj", l, name))
                pe.wait_ge(*gupto("kready", 4))
                idx = 0

                def weigh(tt, j, i):
                    pe.wait_ge(*gupto("a", i + 1))
                    if j == 0 and tt >= 1:
                        pe.wait_ge(*gupto("oread", tt))
                    for h in range(4):
                        mm = pe.matmul((tp, op_)[h // 2][64 * (h % 2):64 * (h % 2) + 64, 0:P],
                                       v[:, tt, 64 * h:64 * h + 64], buf("HG", "at")[:, i % 2, h, :],
                                       start=(j == 0), stop=(j == 6))
                    mm.then_inc(g("aused"), 1)

                pend = None
                for tt in range(ntile):
                    for j in range(7):
                        if j < 6:
                            pe.wait_ge(*gupto("lev", 6 * tt + j + 1))
                        if idx >= 4:
                            pe.wait_ge(*gupto("a", idx - 3))
                        for h in range(4):
                            if j < 6:
                                kk, qq = buf("HGx", "kd")[:, j, h, :], buf("HGx", "qd")[:, j, h, :]
                            else:
                                kk, qq = k_[:, h, P * tt:P * tt + P], q[:, h, P * tt:P * tt + P]
                            mm = pe.matmul(sp_[:, idx % 4, P * h:P * h + P], kk, qq, start=True, stop=True)
                        mm.then_inc(g("sc"), 1)
                        if pend:
                            weigh(*pend)
                        pend = (tt, j, idx)
                        idx += 1
                weigh(*pend)
                pe.wait_ge(*gupto("a", idx))
                pe.wait_ge(*gupto("oread", ntile))
                for tt in range(6):
                    pe.wait_ge(*gupto("ke", 4))
                    if tt >= 1:
                        pe.wait_ge(*gupto("ktcopied", tt))
                    for h in range(4):
                        mm = pe.transpose(tp[:, P * h:P * h + P], k_[:, h, P * tt:P * tt + P], ident)
                    mm.then_inc(g("kt"), 1)
                    pe.wait_ge(*gupto("ktcopied", tt + 1))
                    if tt >= 2:
                        pe.wait_ge(*gupto("uread", 2 * (tt - 1)))
                    for half in range(2):
                        for h in range(4):
                            r = slice(64 * half, 64 * half + 64)
                            mm = pe.matmul(sp_[:, 2 * (tt % 2) + half, 64 * h:64 * h + 64], buf("HG", "at")[r, tt % 2, h, :],
                                           v[r, tt, 64 * h:64 * h + 64], start=True, stop=True)
                        mm.then_inc(g("u"), 1)
                pe.wait_ge(*gupto("state", 22))
                pe.wait_ge(*gupto("uread", 12))
                for s in range(1 if last else 2):
                    if s:
                        pe.wait_ge(*gupto("interread", 2))
                    for c in range(8 * s, 8 if s == 0 else 12):
                        for h in range(4):
                            mm = pe.matmul((tp, op_)[h // 2][64 * (h % 2):64 * (h % 2) + 64, 64 * (c - 8 * s):64 * (c - 8 * s) + 64],
                                           buf("HGx", "s")[:, c, 64 * h:64 * h + 64], q[:, h, 64 * c:64 * c + 64],
                                           start=True, stop=True)
                    mm.then_inc(g("inter"), 1)
                for i in range(2):
                    pe.wait_ge(*gupto("osq", i + 1))
                    for s, (a, b) in enumerate(SEGS[:1] if last else SEGS):
                        mm = pe.matmul(sp_[:, 2 * i + s, 0:b - a], cf[:, C_B64:C_B64 + P], buf("HG", "tmp")[:, i, a:b],
                                       start=True, stop=True)
                    mm.then_inc(g("oms"), 1)

            pe.wait_ge(consts_in, 32)
            pe.wait_ge(params_in, counts["params"])
            for l in range(DEPTH):
                mm = pe.transpose(tp[:, P * l:P * l + NROWS], prow[0:NROWS, l, :], cf[0:NROWS, C_ID:C_ID + NROWS])
            mm.then_inc(ls(0, "pturn"), 1)
            pe.wait_ge(x_in, 32)
            for k in range(KT):
                for s, (a, b) in enumerate(SEGS):
                    i = 2 * k + s
                    if i >= 4:
                        pe.wait_ge(*upto(0, "xt_copied", i - 3))
                    for tt in range(a // P, b // P):
                        mm = pe.transpose(sp_[:, i % 4, P * tt - a:P * tt - a + P], xin[:, tt, P * k:P * k + P], ident)
                    mm.then_inc(ls(0, "xt_turned"), 1)

            for l in range(DEPTH):
                last = l == DEPTH - 1
                for j in range(6):
                    modulation(l, j)
                norm_sums(l, 1)
                pe.wait_ge(*upto(l, "xn1", KT))
                for m in ("NA", "SW", "DA"):
                    head_norms(m, l)
                    attention(m, l)
                hgrn(l)
                pe.wait_ge(*upto(l, "mixsplit", KT))
                for j in range(4):
                    u = ("out", l, j)
                    start_unit(u)
                    for c in chunks_of(u):
                        mm = dense(u, c)
                norm_sums(l, 2)
                pe.wait_ge(*upto(l, "xn2", KT))
                for q in range(4):
                    for j in range(4):
                        u = ("ff1", l, q, j)
                        start_unit(u)
                        for c in chunks_of(u):
                            mm = dense(u, c)
                    pe.wait_ge(*upto(l, "h_split", (q + 1) * 8 * (1 if last else 2)))
                    for j in range(4):
                        u = ("ff2", l, q, j)
                        start_unit(u)
                        for c in chunks_of(u):
                            mm = dense(u, c)
            pe.wait_ge(*upto(DEPTH - 1, "x_final", 1))
            for tt in range(4):
                for half in range(2):
                    i = 2 * tt + half
                    if i >= 4:
                        pe.wait_ge(*upto(0, "y_copied", i - 3))
                    for k in range(4):
                        mm = pe.transpose(sp_[:, i % 4, P * k:P * k + P], xT[:, 4 * half + k, P * tt:P * tt + P], ident)
                    mm.then_inc(ls(0, "yt"), 1)

        @block.scalar
        def _(act):
            steps = [0]

            def link(ins):
                steps[0] += 1
                ins.then_inc(act_step, 1)
                act.wait_ge(act_step, steps[0])

            splits = [u for u in units if u[0] != "mod"]
            nexts = [0]

            def split_high():
                if nexts[0] >= len(splits):
                    return
                s = nexts[0]
                u = splits[s]
                nexts[0] += 1
                if s >= 2:
                    wait_used(act, splits[s - 2])
                act.wait_ge(landed[index[u] % 2], landed_at[u])
                nc.scalar.activation(whi[:, s % 2, :, :], raw[:, index[u] % 2, :, :], ACT.Copy).then_inc(hi_done, 1)

            def norm(l, which):
                segs = SEGS[:1] if (which == 2 and l == DEPTH - 1) else SEGS
                end = segs[-1][1]
                if which == 2:
                    wait_read(act, ("out", l, 3))
                elif l > 0:
                    act.wait_ge(*upto(l - 1, "x_final", 1))
                else:
                    act.wait_ge(*upto(0, "xt_copied", 16))
                for k in range(KT):
                    if k >= 2:
                        act.wait_ge(*upto(l, f"sq{which}_read", k - 1))
                    nc.scalar.activation(nsq[:, k % 2, 0:end], xT[:, k, 0:end], ACT.Square).then_inc(ls(l, f"sq{which}"), 1)
                for s, (a, b) in enumerate(segs):
                    n = group_no["ms", l, which, s]
                    act.wait_ge(group_done, n + 1)
                    ins = nc.scalar.activation(nrs[:, a:b], bank(n)[:, 0:b - a], ACT.Ln, bias=epsc[:, 0:1])
                    ins.then_inc(bank_free[n % 2], 1)
                for s, _ in enumerate(segs):
                    wait_read(act, None, group_no["ms", l, which, s])
                nc.scalar.activation(nrs[:, 0:end], nrs[:, 0:end], ACT.Exp, scale=-0.5).then_inc(ls(l, f"rstd{which}"), 1)
                for k in range(KT):
                    act.wait_ge(*upto(l, f"y{which}", k + 1))
                    nc.scalar.activation(xhi[:, k, 0:end], nt1[:, k % 2, 0:end], ACT.Copy).then_inc(ls(l, f"xhi{which}"), 1)

            def head_norms(m, l):
                tiles = tiles_of(m)

                before = {"SW": "NA", "DA": "SW"}.get(m)
                if before:
                    act.wait_ge(*upto(l, before + "_oread", len(JOBS[before, l])))

                def square(i):
                    n, ct, slot = tiles[i]
                    if i >= 2:
                        act.wait_ge(*upto(l, m + "_scaled", i - 1))
                    for s, (a, b) in enumerate(tile_segs(l, n)):
                        g = N(("prj", l, n), (ct, s))
                        act.wait_ge(group_done, g + 1)
                        out, src = buf(m, "y")[:, i % 2, a:b], bank(g)[:, 0:b - a]
                        if m == "NA" and s == 0:
                            out = out.rearrange("p (c r) -> p r c", r=8)
                            src = src.rearrange("p (r c) -> p r c", c=GRID)
                        ins = nc.scalar.activation(out, src, ACT.Square)
                        ins.then_inc(ls(l, m + "_sqseg"), 1)
                    if ct == 1:
                        split_high()

                def factor(i):
                    end = tile_len(l, tiles[i][0])
                    act.wait_ge(*upto(l, m + "_ms", i + 1))
                    y = buf(m, "y")[:, i % 2, 0:end]
                    src = sp_[:, 2 * (i % 2):2 * (i % 2) + 2, :].rearrange("p b c -> p (b c)")[:, 0:end]
                    ins = nc.scalar.activation(y, src, ACT.Ln, bias=epsc[:, 0:1])
                    ins.then_inc(ls(l, m + "_ln"), 1)
                    act.wait_ge(*upto(l, m + "_ln", i + 1))
                    nc.scalar.activation(y, y, ACT.Exp, scale=-0.5).then_inc(ls(l, m + "_rstd"), 1)

                for i in range(len(tiles) + 1):
                    if i < len(tiles):
                        square(i)
                    if i >= 1:
                        factor(i - 1)
                if m == "NA":
                    split_high()
                    for i in range(9):
                        act.wait_ge(*upto(l, "NA_vturn", i + 1))
                        nc.scalar.activation(buf("NA", "v")[:, i, :], (tp, op_)[i % 2][:, 0:256], ACT.Copy)\
                          .then_inc(ls(l, "NA_vfree"), 1)
                if m == "SW":
                    split_high()
                    for i in range(6):
                        act.wait_ge(*upto(l, "SW_vturn", i + 1))
                        nc.scalar.activation(buf("SW", "v")[:, i, :], (tp, op_)[i % 2][:, 0:P], ACT.Copy)\
                          .then_inc(ls(l, "SW_vfree"), 1)
                if m == "DA":
                    for tt in range(6):
                        g = N(("prj", l, "DAv"), ("tok", tt))
                        act.wait_ge(group_done, g + 1)
                        ins = nc.scalar.activation(buf("DA", "v")[:, tt, :], bank(g)[:, 0:UC], ACT.Copy)
                        ins.then_inc(bank_free[g % 2], 1)
                    split_high()

            def attention(m, l):
                jobs = JOBS[m, l]
                nm = 2 if m == "DA" else 1

                def expo(n):
                    j = jobs[n]
                    for mp in range(nm):
                        unit = nm * n + mp
                        act.wait_ge(*upto(l, m + "_max", unit + 1))
                        if m == "SW":
                            nc.scalar.activation(small[:, 8 + unit % 4:9 + unit % 4], sink[:, l, j["head"]:j["head"] + 1],
                                                 ACT.Exp, bias=small[:, unit % 4:unit % 4 + 1])
                        if m == "DA":
                            if n >= 2:
                                act.wait_ge(*upto(l, m + "_pt", piece_base(m, l, n - 1)))
                            src = sp_[:, 2 * (unit % 2):2 * (unit % 2) + 2, :].rearrange("p b c -> p (b c)")[:, 0:j["n"]]
                        else:
                            src = probs(m, n)[:, 0:j["n"]]
                        ins = nc.scalar.activation(probs(m, n, mp)[:, 0:j["n"]], src, ACT.Exp,
                                                   bias=small[:, unit % 4:unit % 4 + 1],
                                                   accum_out=small[:, 4 + unit % 4:5 + unit % 4])
                        ins.then_inc(ls(l, m + "_exp"), 1)

                def copy_turned(n):
                    b = piece_base(m, l, n)
                    if n >= 2:
                        act.wait_ge(*upto(l, m + "_o", n - 1))
                    for i, (k0, k1) in enumerate(pieces(jobs[n])):
                        act.wait_ge(*upto(l, m + "_pt", b + i + 1))
                        nc.scalar.activation(probs_t(m, n)[:, P * k0:P * k1], (tp, op_)[(b + i) % 2][:, 0:P * (k1 - k0)], ACT.Copy)\
                          .then_inc(ls(l, m + "_ptcopied"), 1)

                expo(0)
                for n in range(len(jobs)):
                    if n + 1 < len(jobs):
                        expo(n + 1)
                    copy_turned(n)
                if m == "DA":
                    end = LAT if l == DEPTH - 1 else T
                    act.wait_ge(*upto(l, "DA_oread", len(jobs)))
                    for i in range(2):
                        nc.scalar.activation(buf("DA", "y")[:, i, 0:end], mix[:, i, 0:end], ACT.Square)\
                          .then_inc(ls(l, "DA_osq"), 1)
                    for i in range(2):
                        act.wait_ge(*upto(l, "DA_oms", i + 1))
                        y = buf("DA", "y")[:, i, 0:end]
                        link(nc.scalar.activation(y, sp_[:, 2 * i:2 * i + 2, :].rearrange("p b c -> p (b c)")[:, 0:end],
                                                  ACT.Ln, bias=epsc[:, 0:1]))
                        nc.scalar.activation(y, y, ACT.Exp, scale=-0.5).then_inc(ls(l, "DA_orstd"), 1)

            def hgrn(l):
                last = l == DEPTH - 1
                g = lambda name: ls(l, "HG_" + name)
                gupto = lambda name, value: upto(l, "HG_" + name, value)
                q, cum, k_ = buf("HG", "q"), buf("HG", "cum"), buf("HG", "k")
                tmp = buf("HG", "tmp")
                act.wait_ge(*upto(l, "DA_final", 1))
                for name in ("HGq0", "HGq1"):
                    u = ("prj", l, name)
                    for c in chunks_of(u):
                        n = N(u, c)
                        a, b = SEGS[c[1]]
                        act.wait_ge(group_done, n + 1)
                        ins = nc.scalar.activation(q[:, 2 * int(name[3]) + c[0], a:b], bank(n)[:, 0:b - a], ACT.Copy)
                        ins.then_inc(bank_free[n % 2], 1)
                    split_high()
                for name in ("HGf0", "HGf1"):
                    u = ("prj", l, name)
                    for c in chunks_of(u):
                        n = N(u, c)
                        h = 2 * int(name[3]) + c[0]
                        a, b = SEGS[c[1]]
                        act.wait_ge(group_done, n + 1)
                        ins = nc.scalar.activation(cum[:, h, a:b], bank(n)[:, 0:b - a], ACT.Exp, scale=-1.0)
                        ins.then_inc(bank_free[n % 2], 1)
                        if c[1] == 1 and h > 0:
                            lns(l, h - 1)
                    split_high()
                lns(l, 3)
                for tt in range(6):
                    n = N(("prj", l, "HGi"), ("tok", tt))
                    act.wait_ge(group_done, n + 1)
                    ins = nc.scalar.activation(buf("HG", "v")[:, tt, :], bank(n)[:, 0:UC], ACT.Copy)
                    ins.then_inc(bank_free[n % 2], 1)
                split_high()
                u = ("prj", l, "HGg")
                for i, c in enumerate(chunks_of(u)):
                    n = N(u, c)
                    a, b = SEGS[c[1]]
                    act.wait_ge(group_done, n + 1)
                    if i == 0:
                        act.wait_ge(*gupto("cumdone", 4))
                    nc.scalar.activation(tmp[:, c[0], a:b], bank(n)[:, 0:b - a], ACT.Exp, scale=-1.0)\
                      .then_inc(g("eg"), 1)
                split_high()
                ntile = 4 if last else 6
                wait_read(act, u)
                dbuf = [tmp[:, i, 0:512] for i in range(2)]
                idx = 0

                def read_out(tt):
                    act.wait_ge(*gupto("aused", 7 * (tt + 1)))
                    for i in range(2):
                        ins = nc.scalar.activation(mix[:, 2 + i, P * tt:P * tt + P], (tp, op_)[i][:, 0:P], ACT.Copy)
                    ins.then_inc(g("oread"), 1)

                for tt in range(ntile):
                    for j in range(6):
                        B = 1 << j
                        act.wait_ge(*gupto("d", idx + 1))
                        dv = dbuf[idx % 2].rearrange("p (n two b) -> p n two b", two=2, b=B)
                        nc.scalar.activation(dv[:, :, 0, :], dv[:, :, 0, :], ACT.Exp, scale=cf[:, C_SGN:C_SGN + 1])
                        nc.scalar.activation(dv[:, :, 1, :], dv[:, :, 1, :], ACT.Exp, scale=cf[:, C_SGN + 1:C_SGN + 2])\
                          .then_inc(g("dexp"), 1)
                        idx += 1
                        if tt >= 1 and j == 3:
                            read_out(tt - 1)
                read_out(ntile - 1)
                end = LAT if last else T
                for h in range(4):
                    act.wait_ge(*gupto("lastd", h + 1))
                    nc.scalar.activation(tmp[:, h % 2, :], tmp[:, h % 2, :], ACT.Exp, scale=-1.0).then_inc(g("kexp"), 1)
                for h in range(4):
                    act.wait_ge(*gupto("ke" if h < 2 else "qe", h + 3 if h < 2 else h - 1))
                    nc.scalar.activation(tmp[:, h % 2, 0:end], cum[:, h, 0:end], ACT.Exp).then_inc(g("qexp"), 1)
                act.wait_ge(*gupto("tot", 1))
                nc.scalar.activation(buf("HG", "ref")[:, :, 16:28], buf("HG", "ref")[:, :, 0:12], ACT.Exp).then_inc(g("decay"), 1)
                for tt in range(6):
                    act.wait_ge(*gupto("kt", tt + 1))
                    if tt >= 2:
                        act.wait_ge(*gupto("u", 2 * (tt - 1)))
                    nc.scalar.activation(buf("HG", "at")[:, tt % 2, :, :], tp[:, :].rearrange("p (h c) -> p h c", c=P), ACT.Copy)\
                      .then_inc(g("ktcopied"), 1)
                    for half in range(2):
                        act.wait_ge(*gupto("u", 2 * tt + half + 1))
                        nc.scalar.activation(buf("HGx", "u")[:, 2 * tt + half, :], sp_[:, 2 * (tt % 2) + half, 0:256], ACT.Copy)\
                          .then_inc(g("uread"), 1)
                act.wait_ge(*gupto("interread", 2 * (1 if last else 2)))
                for i in range(2):
                    nc.scalar.activation(tmp[:, i, 0:end], mix[:, 2 + i, 0:end], ACT.Square).then_inc(g("osq"), 1)
                for i in range(2):
                    act.wait_ge(*gupto("oms", i + 1))
                    y = tmp[:, i, 0:end]
                    link(nc.scalar.activation(y, sp_[:, 2 * i:2 * i + 2, :].rearrange("p b c -> p (b c)")[:, 0:end],
                                              ACT.Ln, bias=epsc[:, 0:1]))
                    nc.scalar.activation(y, y, ACT.Exp, scale=-0.5).then_inc(g("orstd"), 1)

            def lns(l, h):
                g = lambda name: ls(l, "HG_" + name)
                gupto = lambda name, value: upto(l, "HG_" + name, value)
                act.wait_ge(*gupto("fa", h + 1))
                tmp = buf("HG", "tmp")
                nc.scalar.activation(tmp[:, 0, :], tmp[:, 0, :], ACT.Ln)
                nc.scalar.activation(tmp[:, 1, :], tmp[:, 1, :], ACT.Ln).then_inc(g("lnf"), 1)

            act.wait_ge(*upto(0, "eps_set", 1))
            for i in range(16):
                k, s = i // 2, i % 2
                if i % 2:
                    a, b = SEGS[s]
                    act.wait_ge(*upto(0, "xt_turned", i + 1))
                    act.wait_ge(*upto(0, "xt_copied", i))
                    nc.scalar.activation(xT[:, k, a:b], sp_[:, i % 4, 0:b - a], ACT.Copy).then_inc(ls(0, "xt_copied"), 1)
            for l in range(DEPTH):
                last = l == DEPTH - 1
                if l == 0:
                    act.wait_ge(*upto(0, "pcol_done", 1))
                    nc.scalar.activation(siluw[:, :], pcol[:, 0, R_C:R_C + 16], ACT.Exp, scale=-1.0).then_inc(ls(0, "esilu"), 1)
                    act.wait_ge(*upto(0, "lbdiff", 1))
                    nc.scalar.activation(lbt[:, 1:3, :], lbt[:, 1:3, :], ACT.Exp).then_inc(ls(0, "lbexp"), 1)
                act.wait_ge(*upto(l, "lamdot", 1))
                nc.scalar.activation(lams[:, 2:4], lams[:, 0:2], ACT.Exp).then_inc(ls(l, "lamexp"), 1)
                split_high()
                split_high()
                norm(l, 1)
                for m in ("NA", "SW", "DA"):
                    head_norms(m, l)
                    attention(m, l)
                hgrn(l)
                end = LAT if last else T
                act.wait_ge(*upto(l, "mix_ready", 1))
                for k in range(KT):
                    nc.scalar.activation(xhi[:, k, 0:end], mix[:, k, 0:end], ACT.Copy).then_inc(ls(l, "mixhi"), 1)
                for j in range(4):
                    split_high()
                norm(l, 2)
                for q in range(4):
                    for j in range(4):
                        u = ("ff1", l, q, j)
                        for c in chunks_of(u):
                            n = N(u, c)
                            e = ff_index(l, q, j, c)
                            a, b = SEGS[c[1]]
                            act.wait_ge(group_done, n + 1)
                            if e >= 2:
                                act.wait_ge(*upto(l, "h_split", e - 1))
                            ins = nc.scalar.activation(frel[:, e % 2, 0:b - a], bank(n)[:, 0:b - a], ACT.Relu)
                            ins.then_inc(bank_free[n % 2], 1)
                            act.wait_ge(*upto(l, "h_sq", e + 1))
                            if q > 0:
                                wait_used(act, ("ff2", l, q - 1, 3))
                            nc.scalar.activation(hhi[:, 2 * j + c[0], a:b], frel[:, e % 2, 0:b - a], ACT.Copy)\
                              .then_inc(ls(l, "h_hi"), 1)
                        split_high()
                    for j in range(2 if q == 3 else 4):
                        split_high()

        @block.vector
        def _(dve):
            steps = [0]

            def link(ins):
                steps[0] += 1
                ins.then_inc(dve_step, 1)
                dve.wait_ge(dve_step, steps[0])

            V = nc.vector

            def modulation(l, j):
                for i in range(4):
                    n = N(("mod", l, j, i), "row")
                    dve.wait_ge(group_done, n + 1)
                    ins = V.tensor_copy(mrow[0:2, UC * i:UC * i + UC], bank(n)[0:2, 0:UC])
                    ins.then_inc(bank_free[n % 2], 1)
                n = N(("mod", l, j, 3), "turn")
                dve.wait_ge(group_done, n + 1)
                ins = V.tensor_tensor(mods[:, l, 8 * j:8 * j + 8, :], bank(n)[:, 0:16].rearrange("p (a b) -> p a b", b=2),
                                      pcol[:, l, R_BMOD + 8 * j:R_BMOD + 8 * j + 8].unsqueeze(2).to_broadcast([P, 8, 2]), ALU.add)
                ins.then_inc(bank_free[n % 2], 1)
                wait_read(dve, None, n)

            def norm(l, which):
                segs = SEGS[:1] if (which == 2 and l == DEPTH - 1) else SEGS
                end = segs[-1][1]
                sh, sc = (0, 1) if which == 1 else (3, 4)
                grow = R_N1 if which == 1 else R_N2
                link(V.tensor_scalar(amod[:, :, :], mods[:, l, 8 * sc:8 * sc + 8, :], 1.0, None, ALU.add))
                link(V.tensor_tensor(amod[:, :, :], amod[:, :, :],
                                     pcol[:, l, grow:grow + 8].unsqueeze(2).to_broadcast([P, 8, 2]), ALU.mult))
                dve.wait_ge(*upto(l, f"rstd{which}", 1))

                def low(k):
                    dve.wait_ge(*upto(l, f"xhi{which}", k + 1))
                    V.tensor_tensor(xlo[:, k, 0:end], nt1[:, k % 2, 0:end], xhi[:, k, 0:end].bitcast(F32), ALU.subtract)\
                     .then_inc(ls(l, f"xn{which}"), 1)

                for k in range(KT):
                    if k >= 2:
                        dve.wait_ge(*upto(l, f"xn{which}", k - 1))
                    link(V.tensor_tensor(nt1[:, k % 2, 0:end], xT[:, k, 0:end], nrs[:, 0:end], ALU.mult))
                    for s, (a, b) in enumerate(segs):
                        ins = V.tensor_scalar(nt1[:, k % 2, a:b], nt1[:, k % 2, a:b], amod[:, k, s:s + 1],
                                              mods[:, l, 8 * sh + k, s:s + 1], ALU.mult, ALU.add)
                    ins.then_inc(ls(l, f"y{which}"), 1)
                    if k >= 1:
                        low(k - 1)
                low(KT - 1)

            def head_norms(m, l):
                tiles = tiles_of(m)
                xr = buf(m, "xr")
                seg_count = [0]

                def copy(i):
                    n, ct, slot = tiles[i]
                    for s, (a, b) in enumerate(tile_segs(l, n)):
                        g = N(("prj", l, n), (ct, s))
                        seg_count[0] += 1
                        dve.wait_ge(*upto(l, m + "_sqseg", seg_count[0]))
                        out, src = xr[:, slot, a:b], bank(g)[:, 0:b - a]
                        if m == "NA" and s == 0:
                            out = out.rearrange("p (c r) -> p r c", r=8)
                            src = src.rearrange("p (r c) -> p r c", c=GRID)
                        ins = V.tensor_copy(out, src)
                        ins.then_inc(bank_free[g % 2], 1)
                        wait_read(dve, None, g)

                def scale(i):
                    n, ct, slot = tiles[i]
                    end = tile_len(l, n)
                    gain = gq[:, GAIN[n]:GAIN[n] + 1] if n in GAIN else \
                        pcol[:, l, {"NAk": G_NAK, "SWkv": G_SWK, "DAk": G_DAK}[n]:][:, 0:1]
                    dve.wait_ge(*upto(l, m + "_rstd", i + 1))
                    ins = V.scalar_tensor_tensor(out=xr[:, slot, 0:end], in0=xr[:, slot, 0:end], scalar=gain,
                                                 in1=buf(m, "y")[:, i % 2, 0:end], op0=ALU.mult, op1=ALU.mult)
                    ins.then_inc(ls(l, m + "_scaled"), 1)
                    dve.wait_ge(*upto(l, m + "_scaled", i + 1))

                def rope(i):
                    if m == "NA":
                        return
                    slot = tiles[i][2]
                    _, cc, cs = ROPE[m]
                    rot = buf(m, "rot")[:, i % 2, :]
                    dve.wait_ge(*upto(l, m + "_rot", i + 1))
                    V.tensor_tensor(rot, (tp, op_)[i % 2][:, :], cf[:, cs:cs + LAT], ALU.mult).then_inc(ls(l, m + "_rotread"), 1)
                    link(V.tensor_tensor(xr[:, slot, 0:LAT], xr[:, slot, 0:LAT], cf[:, cc:cc + LAT], ALU.mult))
                    ins = V.tensor_tensor(xr[:, slot, 0:LAT], xr[:, slot, 0:LAT], rot, ALU.add)
                    link(ins)
                    return ins

                for i in range(len(tiles) + 2):
                    if i < len(tiles):
                        copy(i)
                    if 1 <= i <= len(tiles):
                        scale(i - 1)
                    if i >= 2:
                        rope(i - 2)
                if m == "NA":
                    for ct in range(2):
                        for s, (a, b) in enumerate(SEGS):
                            g = N(("prj", l, "NAv"), (ct, s))
                            dve.wait_ge(group_done, g + 1)
                            out, src = buf("NA", "vt")[:, ct, a:b], bank(g)[:, 0:b - a]
                            if s == 0:
                                out = out.rearrange("p (c r) -> p r c", r=8)
                                src = src.rearrange("p (r c) -> p r c", c=GRID)
                            ins = V.tensor_copy(out, src)
                            ins.then_inc(bank_free[g % 2], 1)
                if m == "SW":
                    for s, (a, b) in enumerate(SEGS):
                        g = N(("prj", l, "SWkv"), (1, s))
                        dve.wait_ge(group_done, g + 1)
                        ins = V.tensor_copy(buf("SW", "vt")[:, 0, a:b], bank(g)[:, 0:b - a])
                        ins.then_inc(bank_free[g % 2], 1)
                if m == "NA":
                    dve.wait_ge(*upto(l, "NA_vfree", 9))
                if m == "SW":
                    dve.wait_ge(*upto(l, "SW_vfree", 6))
                if m == "DA":
                    wait_read(dve, ("prj", l, "DAv"))
                V.memset(small[:, 16:17], 0.0).then_inc(ls(l, m + "_ready"), 1)

            def attention(m, l):
                jobs = JOBS[m, l]
                nm = 2 if m == "DA" else 1

                def maxima(n):
                    j = jobs[n]
                    for mp in range(nm):
                        unit = nm * n + mp
                        c = small[:, unit % 4:unit % 4 + 1]
                        dve.wait_ge(*upto(l, m + "_s", unit + 1))
                        full = sp_[:, 2 * (unit % 2):2 * (unit % 2) + 2, :].rearrange("p b c -> p (b c)")
                        if m == "DA":
                            V.tensor_reduce(c, full[:, 0:j["n"]], AX.X, ALU.max, negate=True).then_inc(ls(l, m + "_max"), 1)
                            continue
                        p = probs(m, n)
                        if n >= 2:
                            dve.wait_ge(*upto(l, m + "_pt", piece_base(m, l, n - 1)))
                        if m == "NA":
                            if j["bias"]:
                                V.tensor_tensor(p[:, 0:256], full[:, 0:256], j["bias"][2], ALU.add)
                            o, w, d = j["rest"]
                            sfree(V.tensor_copy(p[:, d:d + w], full[:, o:o + w]), unit)
                            V.tensor_reduce(c, p[:, 0:j["n"]], AX.X, ALU.max, negate=True).then_inc(ls(l, m + "_max"), 1)
                        else:
                            w = j["w"]
                            for o, mask in j["masks"]:
                                V.tensor_tensor(p[:, o:o + P], full[:, o:o + P], mask, ALU.add)
                            if j["plain"] is not None:
                                V.tensor_copy(p[:, j["plain"]:j["plain"] + P], full[:, j["plain"]:j["plain"] + P])
                            o = 512 if w else 0
                            sfree(V.tensor_copy(p[:, w:w + 256], full[:, o:o + 256]), unit)
                            link(V.tensor_reduce(c, p[:, 0:j["n"]], AX.X, ALU.max))
                            V.tensor_scalar(c, c, sink[:, l, j["head"]:j["head"] + 1], -1.0, ALU.max, ALU.mult)\
                             .then_inc(ls(l, m + "_max"), 1)

                def sfree(ins, unit):
                    ins.then_inc(ls(l, m + "_sfree"), 1)
                    dve.wait_ge(*upto(l, m + "_sfree", unit + 1))

                def finish(n):
                    j = jobs[n]
                    u0 = nm * n
                    dve.wait_ge(*upto(l, m + "_exp", u0 + nm))
                    sums = small[:, 4 + u0 % 4:4 + u0 % 4 + nm]
                    if m == "SW":
                        link(V.tensor_tensor(sums, sums, small[:, 8 + u0 % 4:9 + u0 % 4], ALU.add))
                    link(V.reciprocal(sums, sums))
                    p = probs(m, n)[:, 0:j["n"]]
                    if m == "DA":
                        s1 = small[:, 5 + u0 % 4:6 + u0 % 4]
                        V.tensor_tensor(s1, s1, nlam[:, :], ALU.mult)
                        link(V.tensor_scalar(p, p, small[:, 4 + u0 % 4:5 + u0 % 4], None, ALU.mult))
                        V.scalar_tensor_tensor(out=p, in0=probs(m, n, 1)[:, 0:j["n"]], scalar=s1, in1=p,
                                               op0=ALU.mult, op1=ALU.add).then_inc(ls(l, m + "_p"), 1)
                    else:
                        V.tensor_scalar(p, p, sums, None, ALU.mult).then_inc(ls(l, m + "_p"), 1)

                def output(n):
                    j = jobs[n]
                    dve.wait_ge(*upto(l, m + "_o", n + 1))
                    src = gp[j["rows"], n % 2, 0:P]
                    dst = mix[j["rows"], MIXT[m] + j["head"] // 2, :]
                    if j["out"][0] == "grid":
                        dst = dst[:, 0:LAT].rearrange("p (r c) -> p c r", c=GRID)[:, 16 * j["out"][1]:16 * j["out"][1] + 16, :]
                        src = src.rearrange("p (c r) -> p c r", r=8)
                    else:
                        dst = dst[:, j["out"][1]:j["out"][1] + P]
                    ins = V.tensor_copy(dst, src)
                    ins.then_inc(ls(l, m + "_oread"), 1)

                maxima(0)
                for n in range(len(jobs)):
                    if n + 1 < len(jobs):
                        maxima(n + 1)
                    finish(n)
                    if n >= 1:
                        output(n - 1)
                output(len(jobs) - 1)
                if m == "DA":
                    end = LAT if l == DEPTH - 1 else T
                    for i in range(2):
                        dve.wait_ge(*upto(l, "DA_orstd", i + 1))
                        ins = V.scalar_tensor_tensor(out=mix[:, i, 0:end], in0=mix[:, i, 0:end], scalar=gq[:, 3:4],
                                                     in1=buf("DA", "y")[:, i, 0:end], op0=ALU.mult, op1=ALU.mult)
                    ins.then_inc(ls(l, "DA_final"), 1)

            def hgrn(l):
                last = l == DEPTH - 1
                g = lambda name: ls(l, "HG_" + name)
                gupto = lambda name, value: upto(l, "HG_" + name, value)
                q, cum, k_ = buf("HG", "q"), buf("HG", "cum"), buf("HG", "k")
                tmp, ref = buf("HG", "tmp"), buf("HG", "ref")
                qd, kd = buf("HGx", "qd"), buf("HGx", "kd")
                FW, BW = slice(0, 64), slice(64, 128)
                for h in range(4):
                    c = cum[:, h, :]
                    for s in range(2):
                        wait_read(dve, None, N(("prj", l, f"HGf{h // 2}"), (h % 2, s)))
                    link(V.tensor_scalar(c, c, 1.0, None, ALU.add))
                    link(V.reciprocal(c, c))
                    if l > 0:
                        link(V.tensor_scalar(c, c, lbt[:, 4, h:h + 1], lbt[:, 3, h:h + 1], ALU.mult, ALU.add))
                    V.tensor_scalar(k_[:, h, :], c, -1.0, 1.0, ALU.mult, ALU.add).then_inc(g("kready"), 1)
                    V.tensor_scalar(tmp[:, 0, :], c, 2.0 ** -60, None, ALU.max)
                    V.tensor_scalar(tmp[:, 1, :], c, 2.0 ** -124, 2.0 ** 60, ALU.max, ALU.mult).then_inc(g("fa"), 1)
                    dve.wait_ge(*gupto("lnf", h + 1))
                    link(V.scalar_tensor_tensor(out=c, in0=tmp[:, 1, :], scalar=0.0, in1=tmp[:, 0, :], op0=ALU.min, op1=ALU.add))
                    V.tensor_tensor_scan(cum[FW, h, :], cb[FW, B_RST:B_RST + T], cum[FW, h, :], 0.0, ALU.mult, ALU.add)
                    ins = V.tensor_tensor_scan(cum[BW, h, ::-1], cb[BW, B_RST:B_RST + T][:, ::-1], cum[BW, h, ::-1],
                                               0.0, ALU.mult, ALU.add)
                    ins.then_inc(g("cumdone"), 1)
                    dve.wait_ge(*gupto("cumdone", h + 1))
                gate = buf("HG", "gate")
                u = ("prj", l, "HGg")
                for i, c in enumerate(chunks_of(u)):
                    n = N(u, c)
                    a, b = SEGS[c[1]]
                    dve.wait_ge(*gupto("eg", i + 1))
                    e = tmp[:, c[0], a:b]
                    link(V.tensor_scalar(e, e, 1.0, None, ALU.add))
                    link(V.reciprocal(e, e))
                    ins = V.tensor_tensor(gate[:, c[0], a:b], e, bank(n)[:, 0:b - a], ALU.mult)
                    ins.then_inc(bank_free[n % 2], 1)
                    wait_read(dve, None, n)
                wait_used(dve, u)
                V.memset(qd[:, :, :, :], 0.0)
                link(V.memset(kd[:, :, :, :], 0.0))
                ntile = 4 if last else 6
                dbuf = [tmp[:, i, 0:512] for i in range(2)]
                todo = []
                for name in ("HGq0", "HGq1"):
                    wait_read(dve, ("prj", l, name))

                def products(tt, j, idx):
                    B = 1 << j
                    dve.wait_ge(*gupto("dexp", idx + 1))
                    if tt >= 1:
                        dve.wait_ge(*gupto("sc", 7 * (tt - 1) + j + 1))
                    dv = dbuf[idx % 2].rearrange("p (h n two b) -> p h n two b", h=4, two=2, b=B)
                    for (r, qs, ks) in ((FW, 1, 0), (BW, 0, 1)):
                        for dst, src, side in ((qd, q, qs), (kd, k_, ks)):
                            o = dst[r, j, :, :].rearrange("p h (n two b) -> p h n two b", two=2, b=B)[:, :, :, side, :]
                            i0 = src[r, :, P * tt:P * tt + P].rearrange("p h (n two b) -> p h n two b", two=2, b=B)[:, :, :, side, :]
                            ins = V.tensor_tensor(o, i0, dv[r, :, :, side, :], ALU.mult)
                    ins.then_inc(g("lev"), 1)

                def differences(tt, j, idx):
                    B = 1 << j
                    nb = P // (2 * B)
                    ct = cum[:, :, P * tt:P * tt + P].rearrange("p h (n w) -> p h n w", w=2 * B)
                    V.tensor_copy(ref[FW, :, 0:nb], ct[FW, :, :, B - 1])
                    link(V.tensor_copy(ref[BW, :, 0:nb], ct[BW, :, :, B]))
                    if idx >= 2:
                        dve.wait_ge(*gupto("lev", idx - 1))
                    d = dbuf[idx % 2].rearrange("p (h n w) -> p h n w", h=4, w=2 * B)
                    ins = V.tensor_tensor(d, ct, ref[:, :, 0:nb].unsqueeze(3).to_broadcast([P, 4, nb, 2 * B]), ALU.subtract)
                    ins.then_inc(g("d"), 1)
                    dve.wait_ge(*gupto("d", idx + 1))

                def masked(i):
                    dve.wait_ge(*gupto("sc", i + 1))
                    if i >= 2:
                        dve.wait_ge(*gupto("aused", i - 1))
                    m = cb[:, P * (i % 7):P * (i % 7) + P].unsqueeze(1).to_broadcast([P, 4, P])
                    V.tensor_tensor(buf("HG", "at")[:, i % 2, :, :], sp_[:, i % 4, :].rearrange("p (h c) -> p h c", c=P), m, ALU.mult)\
                     .then_inc(g("a"), 1)

                levels = [(tt, j) for tt in range(ntile) for j in range(6)]
                differences(*levels[0], 0)
                done = 0
                for idx, (tt, j) in enumerate(levels):
                    if idx + 1 < len(levels):
                        differences(*levels[idx + 1], idx + 1)
                    products(tt, j, idx)
                    while done < 7 * tt + j - 1:
                        masked(done)
                        done += 1
                while done < 7 * ntile:
                    masked(done)
                    done += 1
                dve.wait_ge(*gupto("oread", ntile))
                dve.wait_ge(*gupto("sc", 7 * ntile))
                cc = cum[:, :, :].rearrange("p h (c w) -> p h c w", w=64)
                V.tensor_copy(ref[FW, :, 0:12], cc[FW, :, :, 63])
                ins = V.tensor_copy(ref[BW, :, 0:12], cc[BW, :, :, 0])
                ins.then_inc(g("tot"), 1)
                dve.wait_ge(*gupto("tot", 1))
                end = LAT if last else T

                def kdiff(h):
                    V.tensor_tensor(tmp[:, h % 2, :].rearrange("p (c w) -> p c w", w=64), cc[:, h, :, :],
                                    ref[:, h, 0:12].unsqueeze(2).to_broadcast([P, 12, 64]), ALU.subtract)\
                     .then_inc(g("lastd"), 1)

                def kscale(h):
                    dve.wait_ge(*gupto("kexp", h + 1))
                    ins = V.tensor_tensor(k_[:, h, :], k_[:, h, :], tmp[:, h % 2, :], ALU.mult)
                    ins.then_inc(g("ke"), 1)
                    dve.wait_ge(*gupto("ke", h + 1))

                kdiff(0)
                kdiff(1)
                kscale(0)
                kdiff(2)
                kscale(1)
                kdiff(3)
                kscale(2)
                kscale(3)
                for h in range(4):
                    dve.wait_ge(*gupto("qexp", h + 1))
                    V.tensor_tensor(q[:, h, 0:end], q[:, h, 0:end], tmp[:, h % 2, 0:end], ALU.mult).then_inc(g("qe"), 1)
                st, uu = buf("HGx", "s"), buf("HGx", "u")
                dve.wait_ge(*gupto("decay", 1))
                fw = [8, 9, 10, 11] + list(range(8))
                bw = [11, 10, 9, 8] + list(range(7, -1, -1))
                V.memset(st[FW, fw[0], :], 0.0)
                link(V.memset(st[BW, bw[0], :], 0.0))
                dve.wait_ge(*gupto("uread", 12))
                for i in range(11):
                    for r, order in ((FW, fw), (BW, bw)):
                        c, d = order[i], order[i + 1]
                        V.tensor_tensor(st[r, d, :].rearrange("p (h v) -> p h v", v=64), st[r, c, :].rearrange("p (h v) -> p h v", v=64),
                                        ref[r, :, 16 + c].unsqueeze(2).to_broadcast([64, 4, 64]), ALU.mult).then_inc(dve_step, 1)
                        steps[0] += 1
                    dve.wait_ge(dve_step, steps[0])
                    for r, order in ((FW, fw), (BW, bw)):
                        c, d = order[i], order[i + 1]
                        V.tensor_tensor(st[r, d, :], st[r, d, :], uu[r, c, :], ALU.add).then_inc(g("state"), 1)
                    dve.wait_ge(*gupto("state", 2 * (i + 1)))
                for s, (a, b) in enumerate(SEGS[:1] if last else SEGS):
                    dve.wait_ge(*gupto("inter", s + 1))
                    for i in range(2):
                        ins = V.tensor_tensor(mix[:, 2 + i, a:b], mix[:, 2 + i, a:b], (tp, op_)[i][:, 0:b - a], ALU.add)
                        ins.then_inc(g("interread"), 1)
                for i in range(2):
                    dve.wait_ge(*gupto("orstd", i + 1))
                    m = mix[:, 2 + i, 0:end]
                    link(V.scalar_tensor_tensor(out=m, in0=m, scalar=pcol[:, l, G_HGO:G_HGO + 1], in1=tmp[:, i, 0:end],
                                                op0=ALU.mult, op1=ALU.mult))
                    ins = V.tensor_tensor(m, m, gate[:, i, 0:end], ALU.mult)
                ins.then_inc(ls(l, "mix_ready"), 1)

            def add_back(u, gate_chunk, l, link_last=False):
                for c in chunks_of(u):
                    n = N(u, c)
                    j = u[-1]
                    k = 2 * j + c[0]
                    a, b = SEGS[c[1]]
                    dve.wait_ge(group_done, n + 1)
                    ins = V.scalar_tensor_tensor(out=xT[:, k, a:b], in0=bank(n)[:, 0:b - a],
                                                 scalar=mods[:, l, 8 * gate_chunk + k, c[1]:c[1] + 1], in1=xT[:, k, a:b],
                                                 op0=ALU.mult, op1=ALU.add)
                    ins.then_inc(bank_free[n % 2], 1)
                return ins

            dve.wait_ge(consts_in, 32)
            link(V.tensor_copy(cb[:, :], cbf[:, :]))
            dve.wait_ge(*upto(0, "pturn", 1))
            ins = V.tensor_copy(pcol[:, :, :], tp[:, 0:2 * P].rearrange("p (l r) -> p l r", r=P)[:, :, 0:NROWS])
            ins.then_inc(ls(0, "pcol_done"), 1)
            dve.wait_ge(*upto(0, "pcol_done", 1))
            link(V.tensor_tensor(lbt[:, 0, :], pcol[:, 0, R_LB:R_LB + 4], pcol[:, 0, R_LB + 4:R_LB + 8], ALU.max))
            V.tensor_tensor(lbt[:, 1:3, :], pcol[:, 0, R_LB:R_LB + 8].rearrange("p (a b) -> p a b", b=4),
                            lbt[:, 0, :].unsqueeze(1).to_broadcast([P, 2, 4]), ALU.subtract).then_inc(ls(0, "lbdiff"), 1)
            for k in range(KT):
                i = 2 * k
                dve.wait_ge(*upto(0, "xt_turned", i + 1))
                if i:
                    dve.wait_ge(*upto(0, "xt_copied", i))
                ins = V.tensor_copy(xT[:, k, 0:LAT], sp_[:, i % 4, :])
                ins.then_inc(ls(0, "xt_copied"), 1)
            dve.wait_ge(*upto(0, "xt_copied", 16))
            for l in range(DEPTH):
                last = l == DEPTH - 1
                if l == 0:
                    dve.wait_ge(*upto(0, "esilu", 1))
                    link(V.tensor_scalar(siluw[:, :], siluw[:, :], 1.0, None, ALU.add))
                    link(V.reciprocal(siluw[:, :], siluw[:, :]))
                    V.tensor_tensor(silu_c[:, :, :], siluw[:, :].rearrange("p (j k) -> p k j", j=2),
                                    pcol[:, 0, R_C:R_C + 16].rearrange("p (j k) -> p k j", j=2), ALU.mult)\
                     .then_inc(ls(0, "silu_done"), 1)
                    dve.wait_ge(*upto(0, "lbexp", 1))
                    link(V.tensor_tensor(lbt[:, 0, :], lbt[:, 1, :], lbt[:, 2, :], ALU.add))
                    link(V.reciprocal(lbt[:, 0, :], lbt[:, 0, :]))
                    link(V.tensor_tensor(lbt[:, 1:3, :], lbt[:, 1:3, :], lbt[:, 0, :].unsqueeze(1).to_broadcast([P, 2, 4]), ALU.mult))
                    link(V.tensor_tensor(lbt[:, 3, :], lbt[:, 1, :], lbt[:, 2, :], ALU.add))
                    link(V.tensor_tensor(lbt[:, 3, :], lbt[:, 3, :], lbt[:, 1, :], ALU.subtract))
                    link(V.tensor_scalar(lbt[:, 4, :], lbt[:, 3, :], -1.0, 1.0, ALU.mult, ALU.add))
                else:
                    V.memset(small[:, 17:18], 0.0).then_inc(ls(l, "silu_done"), 1)
                lam_init = 0.8 - 0.6 * math.exp(-0.3 * l)
                link(V.tensor_tensor(lamt[:, :, :], lamv[:, l, 0:4:2, :], lamv[:, l, 1:4:2, :], ALU.mult))
                V.tensor_reduce(lams[:, 0:2], lamt[:, :, :], AX.X, ALU.add).then_inc(ls(l, "lamdot"), 1)
                V.tensor_scalar(gq[:, 0:1], pcol[:, l, G_NAQ:G_NAQ + 1], 64 ** -0.5, None, ALU.mult)
                V.tensor_scalar(gq[:, 1:2], pcol[:, l, G_SWQ:G_SWQ + 1], 64 ** -0.5, None, ALU.mult)
                V.tensor_scalar(gq[:, 2:3], pcol[:, l, G_DAQ:G_DAQ + 1], 32 ** -0.5, None, ALU.mult)
                link(V.tensor_scalar(gq[:, 3:4], pcol[:, l, G_DAS:G_DAS + 1], 1.0 - lam_init, None, ALU.mult))
                dve.wait_ge(*upto(l, "lamexp", 1))
                link(V.tensor_tensor(lams[:, 0:1], lams[:, 3:4], lams[:, 2:3], ALU.subtract))
                link(V.tensor_scalar(nlam[:, :], lams[:, 0:1], -lam_init, None, ALU.add))
                if l == 0:
                    V.memset(small[:, 18:19], 0.0).then_inc(ls(0, "start_done"), 1)
                V.memset(e2[:, :, :, :], 0.0).then_inc(ls(l, "e2_zero"), 1)
                dve.wait_ge(*upto(l, "e2_zero", 1))
                dve.wait_ge(*upto(l, "rpb_in", 16 * 8))
                V.tensor_copy(e2[:, :, 16:47, :], e1[:, :, :, :].rearrange("p h r j -> p h j r")).then_inc(ls(l, "e2_done"), 1)
                for j in range(6):
                    modulation(l, j)
                dve.wait_ge(*upto(l, "bias_in", 16 * 48))
                for v in range(3):
                    bv = bias[:, v, :, :].rearrange("p h (j r) -> p h j r", r=8)
                    for h in range(4):
                        V.tensor_tensor(bv[:, h], bv[:, h], cf[:, C_NA + 32 * v:C_NA + 32 * v + 32].unsqueeze(2)
                                        .to_broadcast([P, 32, 8]), ALU.add)
                norm(l, 1)
                for m in ("NA", "SW", "DA"):
                    head_norms(m, l)
                    attention(m, l)
                hgrn(l)
                end = LAT if last else T
                for k in range(KT):
                    dve.wait_ge(*upto(l, "mixhi", k + 1))
                    V.tensor_tensor(xlo[:, k, 0:end], mix[:, k, 0:end], xhi[:, k, 0:end].bitcast(F32), ALU.subtract)\
                     .then_inc(ls(l, "mixsplit"), 1)
                for j in range(4):
                    add_back(("out", l, j), 2, l)
                wait_read(dve, ("out", l, 3))
                norm(l, 2)
                for q in range(4):
                    for j in range(4):
                        u = ("ff1", l, q, j)
                        for c in chunks_of(u):
                            e = ff_index(l, q, j, c)
                            a, b = SEGS[c[1]]
                            r = frel[:, e % 2, 0:b - a]
                            wait_read(dve, None, N(u, c))
                            V.tensor_tensor(r, r, r, ALU.mult).then_inc(ls(l, "h_sq"), 1)
                            dve.wait_ge(*upto(l, "h_hi", e + 1))
                            V.tensor_tensor(hlo[:, 2 * j + c[0], a:b], r, hhi[:, 2 * j + c[0], a:b].bitcast(F32), ALU.subtract)\
                             .then_inc(ls(l, "h_split"), 1)
                    for j in range(4):
                        add_back(("ff2", l, q, j), 5, l)
                    wait_read(dve, ("ff2", l, q, 3))
                V.memset(small[:, 19:20], 0.0).then_inc(ls(l, "x_final"), 1)
            for i in range(8):
                tt, half = i // 2, i % 2
                dve.wait_ge(*upto(0, "yt", i + 1))
                ins = V.tensor_copy(xin[:, tt, 512 * half:512 * half + 512], sp_[:, i % 4, :])
                ins.then_inc(ls(0, "y_copied"), 1)


INPUTS = ("x", "c", "ctx", "c_ctx", "w_mod", "b_mod", "norm1_g", "norm2_g", "w_in", "w_out", "da_q_gain", "da_k_gain",
          "da_lambda", "da_sub_gain", "hg_lb_logits", "hg_out_gain", "na_q_gain", "na_k_gain", "na_rpb", "sw_q_gain",
          "sw_k_gain", "sw_sink", "w_ff1", "w_ff2")


def program(nc, shapes):
    t = {n: nc.dram_tensor(f"in_{n}", shape, F32, kind="ExternalInput").ap() for n, shape in shapes.items()}
    t["cf"] = nc.dram_tensor("const_f", (P, NCF), F32, kind="ExternalInput").ap()
    t["cb"] = nc.dram_tensor("const_b", (P, NCB), F32, kind="ExternalInput").ap()
    t["out"] = nc.dram_tensor("out", (1, LAT, D), F32, kind="ExternalOutput").ap()
    build(nc, t)


def kernel(**inputs):
    import concourse.bacc as bacc
    from concourse.bass_utils import run_bass_kernel_spmd

    nc = bacc.Bacc("TRN2", target_bir_lowering=False, num_devices=1, dynamic_dma_scratch_size=1024)
    arrays = {n: np.ascontiguousarray(inputs[n]) for n in INPUTS}
    program(nc, {n: a.shape for n, a in arrays.items()})
    f, b = shape_constants()
    sent = {f"in_{n}": a for n, a in arrays.items()}
    sent["const_f"], sent["const_b"] = f, b
    r = run_bass_kernel_spmd(nc, [sent], core_ids=[0])
    return r.results[0]["out"]
```

```python
import math
from contextlib import ExitStack

import numpy as np

import concourse.bass as bass
from concourse import mybir

F32 = mybir.dt.float32
F32R = mybir.dt.float32r
U8 = mybir.dt.uint8
ALU = mybir.AluOpType
ACT = mybir.ActivationFunctionType
AX = mybir.AxisListType

P = 128
D = 1024
KT = D // P
LAT, CTX = 512, 256
T = LAT + CTX
DEPTH = 2
UC = 256
GRID = 64
FW_ORDER = (8, 9, 10, 11, 0, 1, 2, 3, 4, 5, 6, 7)
BW_ORDER = (11, 10, 9, 8, 7, 6, 5, 4, 3, 2, 1, 0)
FW, BW = slice(0, 64), slice(64, 128)
MIX_ORDER = (0, 1, 4, 5, 6, 7, 2, 3)
STATE_TILES = (4, 5, 0, 3, 1, 2)
EPS = 1e-6
NEG = -1e30
SEGS = ((0, LAT), (LAT, T))

R_BMOD, R_N1, R_N2, R_C, R_CC = 0, 48, 56, 64, 72
NROWS = (80, 64)
R_LB, R_G = 0, 8
(G_DAQ, G_DAK, G_DAS, G_HGO, G_NAQ, G_NAK, G_SWQ, G_SWK) = range(R_G, R_G + 8)
NROWS2 = 16

C_ID, C_B32, C_B64, C_ONE, C_P32, C_P64 = (i * P for i in range(6))
C_CA, C_SA, C_CS, C_SS = (6 * P + i * LAT for i in range(4))
C_SW = 6 * P + 4 * LAT
C_NA = C_SW + 2 * P
C_SGN = C_NA + 96
NCF = C_SGN + 2
B_LEV, B_RST, NCB = 0, 7 * P, 7 * P + T


def shape_constants():
    f = np.zeros((P, NCF), np.float32)
    i = np.arange(P)
    f[:, C_ID:C_ID + P] = np.eye(P)
    f[:, C_B32:C_B32 + P] = (i[:, None] // 32 == i // 32) / 32.0
    f[:, C_B64:C_B64 + P] = (i[:, None] // 64 == i // 64) / 64.0
    f[:, C_ONE:C_ONE + P] = 1.0 / D
    t = np.arange(LAT)
    for hd, cp, cc, cs in ((32, C_P32, C_CA, C_SA), (64, C_P64, C_CS, C_SS)):
        axis, half = hd // 2, hd // 4
        inv = (np.float32(10000.0) ** (-np.arange(0, axis, 2, dtype=np.float32) / np.float32(axis))).astype(np.float32)
        within = i % axis
        pos = np.where(((i % hd) // axis == 0)[:, None], (t // GRID)[None], (t % GRID)[None]).astype(np.float32)
        ang = (pos * inv[within % half][:, None]).astype(np.float32)
        f[:, cc:cc + LAT] = np.cos(ang)
        f[:, cs:cs + LAT] = np.sin(ang)
        for o in range(P):
            if o % axis < half:
                f[o + half, cp + o] = -1.0
            else:
                f[o - half, cp + o] = 1.0
    f[:, C_SW:C_SW + P] = np.where(i[None] >= i[:, None], 0.0, NEG)
    f[:, C_SW + P:C_SW + 2 * P] = np.where(i[None] <= i[:, None], 0.0, NEG)
    qc = i // 8
    for v, (band, q0) in enumerate(((0, 0), (8, 16), (32, 48))):
        key = band + np.arange(32)
        start = np.clip(q0 + qc - 8, 0, GRID - 16)[:, None]
        f[:, C_NA + 32 * v:C_NA + 32 * v + 32] = np.where((key >= start) & (key < start + 16), 0.0, NEG)
    f[:, C_SGN] = np.where(i < 64, -1.0, 1.0)
    f[:, C_SGN + 1] = -f[:, C_SGN]
    b = np.zeros((P, NCB), np.float32)
    x = i[:, None] ^ i[None]
    for j in range(6):
        b[:, j * P:(j + 1) * P] = (x >= 2 ** j) & (x < 2 ** (j + 1))
    b[:, 6 * P:7 * P] = x == 0
    t = np.arange(T)
    b[:, B_RST:] = np.where(i[:, None] < 64, t % 64 != 0, t % 64 != 63)
    return f, b


def chunks_of(u):
    l = u[1]
    lat_only = l == DEPTH - 1
    if u[0] == "mod":
        return ["row", "turn"]
    if u[0] in ("out", "ff1", "ff2"):
        return [(ct, s) for ct in range(2) for s in range(1 if lat_only else 2)]
    if u[2] in ("DAv", "HGi"):
        return [("tok", tt) for tt in range(6)]
    if lat_only and u[2] in ("NAq", "SWq", "DAq", "HGg", "HGq"):
        return [(ct, 0) for ct in range(2)]
    return [(ct, s) for ct in range(2) for s in range(2)]


def fill_plan():
    mods = [("mod", 0, j, i) for j in range(2, 6) for i in range(4)] + [("mod", 1, j, i) for j in range(6) for i in range(4)]
    plan = {}
    for l in range(DEPTH):
        jobs = 24 if l < DEPTH - 1 else 16
        for m, names, n_mods in (("NA", ("SWq", "SWkv"), 16), ("SW", ("DAq", "DAk", "DAv"), 8),
                                 ("DA", ("HGq", "HGi"), 6), ("HG", (), 10)):
            items = [[(("prj", l, n), c)] for n in names for c in chunks_of(("prj", l, n))]
            slots = [[] for _ in range((6 * (6 if l < DEPTH - 1 else 4) if m == "HG" else jobs) + 1)]
            todo = [mods.pop(0) for _ in range(n_mods if l == 0 else 0)]
            step = 3 if m == "HG" else 1
            for i, it in enumerate(items):
                slots[i] += it
            for i, u in enumerate(todo):
                a = len(items) + i * step
                slots[a].append((u, "row"))
                slots[a + 1].append((u, "turn"))
            plan[m, l] = slots
    assert not mods
    return plan


FILL = fill_plan()


def dense_order():
    both, one = (0, 1), (1,)
    groups = []

    def whole(u):
        groups.extend((u, c, both) for c in chunks_of(u))

    for l in range(DEPTH):
        if l == 0:
            for j in range(2):
                for i in range(4):
                    whole(("mod", 0, j, i))
        for n in ("NAq", "NAk", "NAv"):
            whole(("prj", l, n))
        for m in ("NA", "SW", "DA"):
            groups.extend((u, c, one) for slot in FILL[m, l] for u, c in slot)
        for n in ("HGf0", "HGf1", "HGg"):
            whole(("prj", l, n))
        groups.extend((u, c, both) for slot in FILL["HG", l] for u, c in slot)
        for j in range(4):
            whole(("out", l, j))
        for q in range(4):
            for kind in ("ff1", "ff2"):
                for j in range(4):
                    whole((kind, l, q, j))
    return groups


COLS = {"DAq": 0, "DAk": 256, "DAv": 512, "HGq": 768, "HGi": 1024, "HGg": 1280, "HGf": 1536,
        "NAq": 2048, "NAk": 2304, "NAv": 2560, "SWq": 2816, "SWkv": 3072}


def build(nc, t):
    group_no, group_bank, group_turn = {}, [], []
    units = []
    used = [0, 0]
    for u, c, banks in dense_order():
        b = banks[0] if len(banks) == 1 else (1 - group_bank[-1] if group_bank else 0)
        group_no[u, c] = len(group_bank)
        group_bank.append(b)
        group_turn.append(used[b])
        used[b] += 1
        if u not in units:
            units.append(u)
    index = {u: i for i, u in enumerate(units)}
    splits = [u for u in units if u[0] != "mod"]
    split_no = {u: i for i, u in enumerate(splits)}

    def unit_dmas(u):
        kind, l = u[:2]
        rows = lambda w: w.rearrange("(k p) n -> p k n", p=P)
        if kind == "mod":
            c = u[2] * D + u[3] * UC
            return [((0, UC, 1), rows(t["w_mod"][l])[:, :, c:c + UC])]
        if kind == "out":
            return [((0, UC, 1), rows(t["w_out"][l])[:, :, u[2] * UC:(u[2] + 1) * UC])]
        if kind == "ff1":
            c = u[2] * D + u[3] * UC
            return [((0, UC, 1), rows(t["w_ff1"][l])[:, :, c:c + UC])]
        if kind == "ff2":
            return [((0, UC, 1), rows(t["w_ff2"][l][u[2] * D:(u[2] + 1) * D, :])[:, :, u[3] * UC:(u[3] + 1) * UC])]
        n = u[2]
        w = rows(t["w_in"][l])
        if n in ("HGf0", "HGf1"):
            h = 2 * int(n[3])
            return [((64 * (2 * a + b), 64, 1), w[:, :, 1536 + 256 * b + 64 * (h + a):1536 + 256 * b + 64 * (h + a) + 64])
                    for a in range(2) for b in range(2)]
        if n == "SWq":
            return [((64 * s, 64, 1), w[:, :, 2816 + 64 * h:2816 + 64 * h + 64]) for s, h in enumerate((0, 2, 1, 3))]
        c = COLS[n]
        return [((0, UC, 1), w[:, :, c:c + UC])]

    landed_at, per_slot = {}, [0, 0]
    for i, u in enumerate(units):
        per_slot[i % 2] += 16 * len(unit_dmas(u))
        landed_at[u] = per_slot[i % 2]

    ctx = ExitStack()
    with ctx:
        def sem(name):
            return ctx.enter_context(nc.semaphore(name))

        base = (nc.sbuf_base + 31) // 32 * 32
        at = [base]

        def place(name, shape, dt=F32, offset=None):
            size = int(np.prod(shape[1:])) * (1 if dt == U8 else 4)
            size = (size + 31) // 32 * 32
            o = at[0] if offset is None else offset
            if offset is None:
                at[0] += size
            assert o + size <= nc.sbuf_usable_end, (name, o + size - nc.sbuf_usable_end)
            tensor = nc.alloc_sbuf_tensor_at(name, shape, dt, offset=o)
            return tensor, o + size

        xT, _ = place("xT", [P, KT, T])
        cf, _ = place("cf", [P, NCF])
        cb, _ = place("cb", [P, NCB], U8)
        raw, _ = place("raw", [P, 2, KT, UC])
        whi, _ = place("whi", [P, 2, KT, UC], F32R)
        wlo, _ = place("wlo", [P, 2, KT, UC], F32R)
        pcol, _ = place("pcol", [P, DEPTH, NROWS[0]])
        pcol2, _ = place("pcol2", [P, DEPTH, NROWS2])
        mods, _ = place("mods", [P, DEPTH, 48, 2])
        mrow, _ = place("mrow", [2, UC])
        silu_c, _ = place("silu_c", [P, KT, 2])
        siluw, _ = place("siluw", [P, 16])
        amod, _ = place("amod", [P, KT, 2])
        lamv, _ = place("lamv", [P, DEPTH, 4, 32])
        lamt, _ = place("lamt", [P, 2, 32])
        lams, _ = place("lams", [P, 4])
        nlam, _ = place("nlam", [P, 1])
        sink, _ = place("sink", [P, DEPTH, 4])
        gq, _ = place("gq", [P, 4])
        lbt, _ = place("lbt", [P, 6, 4])
        small, _ = place("small", [P, 32])
        epsc, _ = place("epsc", [P, 1])
        x0 = at[0]
        xhi, _ = place("xhi", [P, KT, T], F32R)
        xlo, _ = place("xlo", [P, KT, T], F32R)
        scratch0 = at[0]
        hhi, e = place("hhi", [P, KT, T], F32R, scratch0)
        hlo, e = place("hlo", [P, KT, T], F32R, e)
        frel, _ = place("frel", [P, 2, LAT], F32, e)
        mix, _ = place("mix", [P, KT, T], F32, scratch0)
        xin, e = place("xin", [P, 6, D], F32, x0)
        prow, e = place("prow", [P, DEPTH, P], F32, e)
        prow2, e = place("prow2", [NROWS2, DEPTH, P], F32, e)
        cbf, e = place("cbf", [P, NCB], F32, e)

        phase_bufs = {}
        KB = 1024

        def phase(name, start, shapes):
            e = start
            for n, shape in shapes:
                phase_bufs[name, n], e = place(f"{name}_{n}", shape, F32, e)

        s0 = scratch0
        bias, _ = place("bias", [P, 3, 4, 256], F32, s0 + 24 * KB)
        nsq, e = place("nsq", [P, 2, T], F32, s0 + 48 * KB)
        nt1, e = place("nt1", [P, 2, T], F32, e)
        nrs, e = place("nrs", [P, T], F32, e)
        e1, e = place("e1", [8, 4, 8, 31], F32, s0 + 69 * KB)
        e2, e = place("e2", [8, 4, 63, 8], F32, e)
        phase("NA", s0 + 36 * KB, [("xr", [P, 4, T]), ("vt", [P, 2, T]), ("y", [P, 2, T]), ("v", [P, 9, 256])])
        phase("NAp", s0 + 48 * KB, [("p", [P, 2, 512])])
        phase("NAp", s0 + 69 * KB, [("pt", [P, 2, 512])])
        phase("SW", s0, [("xr", [P, 3, T]), ("vt", [P, 1, T])])
        phase("SW", s0 + 24 * KB, [("y", [P, 2, T]), ("rot", [P, 2, LAT]), ("v", [P, 6, P]), ("p", [P, 2, 640]),
                                   ("pt", [P, 2, 640])])
        phase("DA", s0 + 58 * KB, [("xr", [P, 4, T]), ("v", [P, 6, 256])])
        phase("DA", s0 + 24 * KB, [("y", [P, 2, T]), ("rot", [P, 2, LAT]), ("p", [P, 2, 2, T]), ("pt", [P, 2, T])])
        phase("HG", s0 + 6 * KB, [("q1", [P, 2, T])])
        phase("HG", s0 + 24 * KB, [("q", [P, 4, T]), ("cum", [P, 4, T]), ("at", [P, 2, 4, P]), ("v", [P, 6, 256]),
                                   ("k", [P, 4, T]), ("tmp", [P, 2, T]), ("ref", [P, 4, 64]), ("gate", [P, 2, T])])
        phase("HGz", x0 + 12 * KB, [("v", [P, 6, 2, 256])])
        phase("HGx", x0, [("qd", [P, 6, 4, P]), ("kd", [P, 6, 4, P]), ("u", [P, 12, 256]), ("s", [P, 12, 256])])
        buf = lambda a, b: phase_bufs[a, b]
        hi_parts = {}
        for m, o, n_first, o2, n_second in (("NA", 18, 2, 54, 2), ("SW", 47, 3, 0, 0), ("DA", 76, 2, 24, 2)):
            first, _ = place(m + "_hi", [P, n_first, T], F32R, s0 + o * KB)
            hi_parts[m] = [first[:, i, :] for i in range(n_first)]
            if n_second:
                second, _ = place(m + "_hi2", [P, n_second, T], F32R, s0 + o2 * KB)
                hi_parts[m] += [second[:, i, :] for i in range(n_second)]
        lo_parts = {m: place(m + "_lo", [P, n, T], F32R, s0 + o * KB)[0] for m, o, n in (("NA", 36, 4), ("SW", 0, 3), ("DA", 58, 4))}

        def split_part(m, rows, slot):
            return hi_parts[m][slot][rows, :], lo_parts[m][rows, slot, :]

        def cut(parts, a, b):
            return tuple(x[:, a:b] for x in parts)

        gp = ctx.enter_context(nc.psum_tensor("gp", [P, 2, 512], F32))
        sp_ = ctx.enter_context(nc.psum_tensor("sp", [P, 4, 512], F32))
        tp = ctx.enter_context(nc.psum_tensor("tp", [P, 512], F32))
        op_ = ctx.enter_context(nc.psum_tensor("op", [P, 512], F32))

        consts_in = sem("consts_in")
        tables_in = sem("tables_in")
        params_in = sem("params_in")
        params2_in = sem("params2_in")
        x_in = sem("x_in")
        landed = [sem("landed0"), sem("landed1")]
        hi_done = sem("hi_done")
        lo_done = sem("lo_done")
        group_done = sem("group_done")
        bank_free = [sem("bank_free0"), sem("bank_free1")]
        dve_step = sem("dve_step")
        act_step = sem("act_step")
        out_done = sem("out_done")
        S = {}
        counts = {"params2": 16 * (DEPTH * (2 * DEPTH + 2 * 4 + 6 * 2 + 2) + 1)}
        dense_before = {}
        PER_LAYER = {"HG_" + n: c for n, c in dict(
            tot=1, kready=4, interread=4, ke=4, cumdone=4, oms=2, a=42, decay=1, osq=2, fa=4, qexp=4, eg=4, lev=36, levk=36, cleared=1, qcleared=1,
            ktcopied=6, kexp=4, dexp=36, oread=6, d=36, kt=6, state=22, orstd=2, aused=42, uread=6, u=6, apart=2, vclear=1, inter=2,
            lastd=4, lnf=4, qe=4, sc=42, qdup=16 * 8).items()}
        for which in (1, 2):
            PER_LAYER.update({f"sq{which}": KT, f"sq{which}_read": KT - 1, f"rstd{which}": 1, f"ms{which}": 1, f"nx{which}": KT,
                              f"xhi{which}": KT, f"xn{which}": KT})
        PER_LAYER.update(h_sq=64, h_hi=64, h_split=64, mixhi=KT, mixsplit=KT, rpb_in=16 * 8, bias_in=16 * 48,
                         e2_zero=1, e2_done=1, mix_ready=2, bias_masked=12, DA_final=1, DA_oms=2, DA_orstd=2, DA_osq=2)

        def ls(l, name):
            key = name if name in PER_LAYER else f"{name}_{l}"
            if key not in S:
                S[key] = sem(key)
            return S[key]

        def upto(l, name, value):
            return ls(l, name), value + l * PER_LAYER.get(name, 0)

        N = lambda u, c: group_no[u, c]

        def wait_used(eng, u):
            eng.wait_ge(group_done, N(u, "row" if u[0] == "mod" else chunks_of(u)[-1]) + 1)

        def wait_read(eng, u, n=None):
            if n is None:
                for n in sorted(N(u, c) for c in chunks_of(u)[-2:]):
                    wait_read(eng, u, n)
            else:
                eng.wait_ge(bank_free[group_bank[n]], group_turn[n] + 1)

        bank = lambda n: gp[:, group_bank[n], :]
        ident = cf[:, C_ID:C_ID + P]

        def jobs_of(m, l):
            jobs = []
            last = l == DEPTH - 1
            if m == "NA":
                for h in range(4):
                    rows = slice(64 * (h % 2), 64 * (h % 2) + 64)
                    q, k = split_part("NA", rows, h // 2), split_part("NA", rows, 2 + h // 2)
                    v = lambda i, h=h: buf("NA", "v")[:, i, 64 * h:64 * h + 64]
                    for cbk in range(4):
                        band = (0, 8, 24, 32)[cbk]
                        jobs.append(dict(q=[cut(q, P * cbk, P * cbk + P)],
                                         segs=[(0, 256, [cut(k, 8 * band, 8 * band + 256)], 0), (256, 256, [cut(k, LAT, T)], 256)],
                                         bias=(0, 256, bias[:, (0, 1, 1, 2)[cbk], h, :]), rest=(256, 256, 256), n=512,
                                         v=[v(i) for i in ((0, 1), (4, 5), (5, 6), (2, 3))[cbk]] + [v(7), v(8)],
                                         head=h, out=("grid", cbk), rows=rows))
                    for qt in range(0 if last else 2):
                        c = LAT + P * qt
                        jobs.append(dict(q=[cut(q, c, c + P)], segs=[(0, 256, [cut(k, LAT, T)], 0)], bias=None,
                                         rest=(0, 256, 0), n=256, v=[v(7), v(8)], head=h, out=("plain", c), rows=rows))
            if m == "SW":
                for h in range(4):
                    rows = slice(64 * (h // 2), 64 * (h // 2) + 64)
                    q, k = split_part("SW", rows, h % 2), split_part("SW", rows, 2)
                    v = lambda i, h=h: buf("SW", "v")[:, i, 64 * (h // 2):64 * (h // 2) + 64]
                    orow = slice(64 * (h % 2), 64 * (h % 2) + 64)
                    for n in range(4):
                        a, b = max(n - 1, 0), min(n + 2, 4)
                        w = P * (b - a)
                        masks = []
                        if n > 0:
                            masks.append((0, cf[:, C_SW:C_SW + P]))
                        if n < 3:
                            masks.append((w - P, cf[:, C_SW + P:C_SW + 2 * P]))
                        jobs.append(dict(q=[cut(q, P * n, P * n + P)],
                                         segs=[(0, w, [cut(k, P * a, P * b)], 0), (512, 256, [cut(k, LAT, T)], w)],
                                         masks=masks, plain=P * (n - a), n=w + 256, w=w,
                                         v=[v(i) for i in range(a, b)] + [v(4), v(5)], head=h, out=("plain", P * n), rows=orow))
                    for qt in range(0 if last else 2):
                        c = LAT + P * qt
                        jobs.append(dict(q=[cut(q, c, c + P)], segs=[(0, 256, [cut(k, LAT, T)], 0)], masks=[], plain=None, w=0,
                                         n=256, v=[v(4), v(5)], head=h, out=("plain", c), rows=orow))
            if m == "DA":
                for h in range(4):
                    rows = slice(64 * (h % 2), 64 * (h % 2) + 64)
                    v = lambda i, h=h: buf("DA", "v")[:, i, 64 * h:64 * h + 64]
                    for qt in range(4 if last else 6):
                        qs, ks = [], []
                        for mp in range(2):
                            s = 2 * h + mp
                            r = slice(32 * (s % 4), 32 * (s % 4) + 32)
                            qs.append(cut(split_part("DA", r, s // 4), P * qt, P * qt + P))
                            ks.append(split_part("DA", r, 2 + s // 4))
                        if qt < 4:
                            segs = [(0, 512, [cut(k, 0, LAT) for k in ks], 0), (512, 256, [cut(k, LAT, T) for k in ks], 512)]
                            jobs.append(dict(q=qs, segs=segs, n=T, v=[v(i) for i in range(6)], head=h,
                                             out=("plain", P * qt), rows=rows))
                        else:
                            jobs.append(dict(q=qs, segs=[(0, 256, [cut(k, LAT, T) for k in ks], 0)], n=256,
                                             v=[v(4), v(5)], head=h, out=("plain", P * qt), rows=rows))
            return jobs

        MIXT = {"DA": 0, "HG": 2, "NA": 4, "SW": 6}
        JOBS = {(m, l): jobs_of(m, l) for m in ("NA", "SW", "DA") for l in range(DEPTH)}

        def pieces(job):
            nk = job["n"] // P
            return [(a, min(a + 4, nk)) for a in range(0, nk, 4)]

        def piece_base(m, l, n):
            return sum(len(pieces(j)) for j in JOBS[m, l][:n])

        def probs(m, n, mp=0):
            if m == "DA":
                return buf("DA", "p")[:, n % 2, mp, :]
            return buf("NAp" if m == "NA" else "SW", "p")[:, n % 2, :]

        def probs_t(m, n):
            return buf("NAp" if m == "NA" else m, "pt")[:, n % 2, :]

        def tiles_of(m):
            if m == "NA":
                return [("NAq", 0, 0), ("NAq", 1, 1), ("NAk", 0, 2), ("NAk", 1, 3)]
            if m == "SW":
                return [("SWq", 0, 0), ("SWq", 1, 1), ("SWkv", 0, 2)]
            return [("DAq", 0, 0), ("DAq", 1, 1), ("DAk", 0, 2), ("DAk", 1, 3)]

        GAIN = {"NAq": 0, "SWq": 1, "DAq": 2}
        AVG = {"NA": C_B64, "SW": C_B64, "DA": C_B32}
        ROPE = {"SW": (C_P64, C_CS, C_SS), "DA": (C_P32, C_CA, C_SA)}

        for m in ("NA", "SW", "DA"):
            jobs0, nt0 = JOBS[m, 0], len(tiles_of(m))
            scored = len(jobs0) * (2 if m == "DA" else 1)
            turned = sum(len(pieces(j)) for j in jobs0)
            PER_LAYER.update({m + "_" + n: c for n, c in dict(
                sq=nt0, copied=nt0, ms=nt0, rstd=nt0, scaled=nt0, rot=nt0, rotread=nt0, roped=nt0, high=nt0, low=nt0, ready=1, s=scored, max=scored,
                exp=scored, sfree=len(jobs0), p=len(jobs0), o=len(jobs0), oread=len(jobs0), pt=turned,
                ptcopied=turned).items()})
        PER_LAYER.update(NA_vturn=9, NA_vfree=9, SW_vturn=6, SW_vfree=6, x_final=1, lamdot=1, lamexp=1, silu_done=1)

        def tile_len(l, n):
            return LAT if l == DEPTH - 1 and n[2:] == "q" else T

        def tile_segs(l, n):
            return SEGS[:1] if tile_len(l, n) == LAT else SEGS

        def ff_index(l, q, j, c):
            s = 1 if l == DEPTH - 1 else 2
            return ((q * 4 + j) * 2 + c[0]) * s + c[1]

        for m, l in JOBS:
            last_prj = {"NA": ("prj", l, "NAv"), "SW": ("prj", l, "NAv"), "DA": ("prj", l, "NAv")}[m]
            dense_before[m, l] = sum(group_bank[n] == 0 for n in range(N(last_prj, chunks_of(last_prj)[-1]) + 1))

        block = ctx.enter_context(nc.Block())

        @block.sync
        def _(sp):
            sp.dma_start(cf[:, 0:C_CA], t["cf"][:, 0:C_CA]).then_inc(consts_in, 16)
            sp.dma_start(prow[0:48, :, :], t["b_mod"].rearrange("l (r c) -> r l c", c=P)).then_inc(params_in, 16)
            sp.dma_start(prow[48:56, :, :], t["norm1_g"].rearrange("l (r c) -> r l c", c=P)).then_inc(params_in, 16)
            sp.dma_start(prow[56:64, :, :], t["norm2_g"].rearrange("l (r c) -> r l c", c=P)).then_inc(params_in, 16)
            sp.dma_start(prow[64:72, 0, :], t["c"].rearrange("o (r c) -> (o r) c", c=P)).then_inc(params_in, 16)
            sp.dma_start(prow[72:80, 0, :], t["c_ctx"].rearrange("(r c) -> r c", c=P)).then_inc(params_in, 16)

            rows2 = []
            for l in range(DEPTH):
                for l2 in range(DEPTH):
                    for d in range(2):
                        rows2.append((prow2[R_LB + 4 * l2:R_LB + 4 * l2 + 4, l, 64 * d:64 * d + 64],
                                      t["hg_lb_logits"][l2, d].rearrange("(h k) -> h k", k=64)))
                for r, name in enumerate(("da_q_gain", "da_k_gain", "da_sub_gain", "hg_out_gain", "na_q_gain",
                                          "na_k_gain", "sw_q_gain", "sw_k_gain")):
                    g = t[name][l:l + 1, :]
                    w = g.shape[1]
                    rows2 += [(prow2[R_G + r:R_G + r + 1, l, rep * w:rep * w + w], g) for rep in range(P // w)]
                rows2.append((lamv[:, l, :, :], t["da_lambda"][l].partition_broadcast(P)))
                rows2.append((sink[:, l, :], t["sw_sink"][l].partition_broadcast(P)))
            rows2.append((cbf[:, :], t["cb"]))
            assert 16 * len(rows2) == counts["params2"]

            def bias_load(l):
                sp.wait_ge(*upto(l, "e2_zero", 1))
                for r in range(8):
                    sp.dma_start(e1[r:r + 1, :, :, :], t["na_rpb"][l:l + 1, :, 7 - r:15 - r, :]).then_inc(ls(l, "rpb_in"), 16)
                sp.wait_ge(*upto(l, "e2_done", 1))
                for v, off in enumerate((0, -8, -16)):
                    for qc in range(16):
                        j0 = off - qc + 15 + 16
                        sp.dma_start(bias[8 * qc:8 * qc + 8, v, :, :],
                                     e2[:, :, j0:j0 + 32, :].rearrange("p h j r -> p h (j r)")).then_inc(ls(l, "bias_in"), 16)

            for i, u in enumerate(units):
                if i >= 2:
                    w = units[i - 2]
                    if w[0] == "mod":
                        wait_used(sp, w)
                    else:
                        sp.wait_ge(lo_done, split_no[w] + 1)
                for (c, n, s), src in unit_dmas(u):
                    sp.dma_start(raw[:, i % 2, :, c:c + n], src).then_inc(landed[i % 2], 16)
                if i < 8:
                    for dst, src in rows2[len(rows2) * i // 8:len(rows2) * (i + 1) // 8]:
                        sp.dma_start(dst, src).then_inc(params2_in, 16)
                if i == 7:
                    sp.dma_start(cf[:, C_CA:NCF], t["cf"][:, C_CA:NCF]).then_inc(tables_in, 16)
                if u[0] == "prj" and u[2] == "SWq":
                    bias_load(u[1])
            for tt in range(4):
                sp.wait_ge(*upto(0, "y_copied", 2 * tt + 2))
                sp.dma_start(t["out"][0, P * tt:P * tt + P, :], xin[:, tt, :]).then_inc(out_done, 16)
            sp.wait_ge(out_done, 64)

        @block.gpsimd
        def _(pool):
            nc.gpsimd.memset(epsc[:, :], EPS).then_inc(ls(0, "eps_set"), 1)

            def hgrn(l):
                last = l == DEPTH - 1
                g = lambda name: ls(l, "HG_" + name)
                gupto = lambda name, value: upto(l, "HG_" + name, value)
                q, k_, tmp = buf("HG", "q"), buf("HG", "k"), buf("HG", "tmp")
                kd = buf("HGx", "kd")
                wait_used(pool, ("prj", l, "HGg"))
                nc.gpsimd.memset(kd[:, :, :, :], 0.0).then_inc(g("cleared"), 1)
                pool.wait_ge(*gupto("cleared", 1))
                ntile = 4 if last else 6
                idx = 0
                for tt in range(ntile):
                    for j in range(6):
                        B = 1 << j
                        pool.wait_ge(*gupto("dexp", idx + 1))
                        if tt >= 1:
                            pool.wait_ge(*gupto("sc", 7 * (tt - 1) + j + 1))
                        dv = tmp[:, idx % 2, 0:512].rearrange("p (h n two b) -> p h n two b", h=4, two=2, b=B)
                        for r, side in ((FW, 0), (BW, 1)):
                            o = kd[r, j, :, :].rearrange("p h (n two b) -> p h n two b", two=2, b=B)[:, :, :, side, :]
                            i0 = k_[r, :, P * tt:P * tt + P].rearrange("p h (n two b) -> p h n two b", two=2, b=B)[:, :, :, side, :]
                            ins = nc.gpsimd.tensor_tensor(o, i0, dv[r, :, :, side, :], ALU.mult)
                        ins.then_inc(g("levk"), 1)
                        idx += 1
                pool.wait_ge(*gupto("levk", 6 * ntile))
                pool.wait_ge(*gupto("sc", 7 * ntile))
                apart = buf("HGz", "v")
                nc.gpsimd.memset(apart[:, :, :, :], 0.0).then_inc(g("vclear"), 1)
                pool.wait_ge(*gupto("vclear", 1))
                for half in range(2):
                    r = slice(64 * half, 64 * half + 64)
                    nc.gpsimd.tensor_copy(apart[r, :, half, :], buf("HG", "v")[r, :, :]).then_inc(g("apart"), 1)
                pool.wait_ge(*gupto("apart", 2))
                for i in range(2):
                    low(split_no["out", l, i])
                end = LAT if last else T
                for h in range(4):
                    pool.wait_ge(*gupto("qexp", h + 1))
                    nc.gpsimd.tensor_tensor(q[:, h, 0:end], q[:, h, 0:end], tmp[:, h % 2, 0:end], ALU.mult).then_inc(g("qe"), 1)

            def low(s):
                pool.wait_ge(hi_done, s + 1)
                nc.gpsimd.tensor_tensor(wlo[:, s % 2, :, :], raw[:, index[splits[s]] % 2, :, :],
                                        whi[:, s % 2, :, :].bitcast(F32), ALU.subtract).then_inc(lo_done, 1)

            for s, u in enumerate(splits):
                if u[0] == "out" and u[2] == 0:
                    hgrn(u[1])
                if not (u[0] == "out" and u[2] < 2):
                    low(s)
                if u[0] == "prj" and u[2] == "NAv":
                    pool.wait_ge(tables_in, 16)
                    pool.wait_ge(*upto(u[1], "bias_in", 16 * 48))
                    for v in range(3):
                        bv = bias[:, v, :, :].rearrange("p h (j r) -> p h j r", r=8)
                        for h in range(4):
                            nc.gpsimd.tensor_tensor(bv[:, h], bv[:, h], cf[:, C_NA + 32 * v:C_NA + 32 * v + 32]
                                                    .unsqueeze(2).to_broadcast([P, 32, 8]), ALU.add)\
                              .then_inc(ls(u[1], "bias_masked"), 1)

        @block.tensor
        def _(pe):
            started = [0]

            def start_group(n):
                assert n == started[0], "groups in the planned order"
                started[0] += 1
                if group_turn[n]:
                    pe.wait_ge(bank_free[group_bank[n]], group_turn[n])

            def dense(u, *cs, ready=None):
                s = split_no[u] % 2
                if cs[0] == chunks_of(u)[0]:
                    pe.wait_ge(lo_done, split_no[u] + 1)
                for c in cs:
                    start_group(N(u, c))
                hi, lo = (hhi, hlo) if u[0] == "ff2" else (xhi, xlo)
                for i, k in enumerate(MIX_ORDER if u[0] == "out" else range(KT)):
                    if ready:
                        ready(i)
                    for c in cs:
                        if c[0] == "tok":
                            a, b = P * c[1], P * c[1] + P
                            out = bank(N(u, c))[:, 0:UC]
                            trips = ((hi[:, k, a:b], whi[:, s, k, :]), (hi[:, k, a:b], wlo[:, s, k, :]), (lo[:, k, a:b], whi[:, s, k, :]))
                        else:
                            ct, (a, b) = c[0], SEGS[c[1]]
                            out = bank(N(u, c))[:, 0:b - a]
                            w0, w1 = P * ct, P * ct + P
                            trips = ((whi[:, s, k, w0:w1], hi[:, k, a:b]), (whi[:, s, k, w0:w1], lo[:, k, a:b]),
                                     (wlo[:, s, k, w0:w1], hi[:, k, a:b]))
                        for j, (lhs, rhs) in enumerate(trips):
                            mm = pe.matmul(out, lhs, rhs, start=(i == 0 and j == 0), stop=(i == KT - 1 and j == 2))
                        if i == KT - 1:
                            mm.then_inc(group_done, 1)

            def dense_unit(u, ready):
                cs = chunks_of(u)
                dense(u, *cs[:2], ready=ready)
                for c in cs[2:]:
                    dense(u, c)

            def modulation(u, c):
                n = N(u, c)
                start_group(n)
                if c == "row":
                    if index[u] == 0:
                        pe.wait_ge(*upto(0, "silu_done", 1))
                    pe.wait_ge(landed[index[u] % 2], landed_at[u])
                    for k in range(KT):
                        mm = pe.matmul(bank(n)[0:2, 0:UC], silu_c[:, k, :], raw[:, index[u] % 2, k, :],
                                       start=(k == 0), stop=(k == KT - 1))
                else:
                    wait_read(pe, None, N(u, "row"))
                    for i in range(2):
                        mm = pe.transpose(bank(n)[:, 2 * i:2 * i + 2], mrow[0:2, P * i:P * i + P], cf[0:2, C_ID:C_ID + 2])
                mm.then_inc(group_done, 1)

            def fill(slot):
                for u, c in slot:
                    if u[0] == "mod":
                        modulation(u, c)
                    else:
                        dense(u, c)

            def norm_sums(l, which, ks):
                segs = SEGS[:1] if (which == 2 and l == DEPTH - 1) else SEGS
                for k in ks:
                    pe.wait_ge(*upto(l, f"sq{which}", k + 1))
                    for s, (a, b) in enumerate(segs):
                        mm = pe.matmul(sp_[:, s, 0:b - a], cf[:, C_ONE:C_ONE + P], nsq[:, k % 2, a:b],
                                       start=(k == 0), stop=(k == KT - 1))
                    mm.then_inc(ls(l, f"sq{which}_read" if k < KT - 1 else f"ms{which}"), 1)

            def head_norms(m, l):
                tiles = tiles_of(m)

                def project(i):
                    n, ct, _ = tiles[i]
                    if m == "NA":
                        if i == 0:
                            dense_unit(("prj", l, n), lambda k: pe.wait_ge(*upto(l, "xn1", k + 1)))
                        elif i >= 2:
                            for s, _ in enumerate(tile_segs(l, n)):
                                dense(("prj", l, n), (ct, s))

                def average(i):
                    pe.wait_ge(*upto(l, m + "_sq", i + 1))
                    if i >= 2:
                        pe.wait_ge(*upto(l, m + "_scaled", i - 1))
                    for (a, b) in tile_segs(l, tiles[i][0]):
                        mm = pe.matmul(sp_[:, 2 * (i % 2) + (1 if a else 0), 0:b - a], cf[:, AVG[m]:AVG[m] + P],
                                       buf(m, "y")[:, i % 2, a:b], start=True, stop=True)
                    mm.then_inc(ls(l, m + "_ms"), 1)

                def turn(i):
                    if m == "NA":
                        return
                    pe.wait_ge(*upto(l, m + "_scaled", i + 1))
                    if i >= 2:
                        pe.wait_ge(*upto(l, m + "_rotread", i - 1))
                    perm = ROPE[m][0]
                    pe.matmul((tp, op_)[i % 2][:, :], cf[:, perm:perm + P], buf(m, "xr")[:, tiles[i][2], 0:LAT],
                              start=True, stop=True).then_inc(ls(l, m + "_rot"), 1)

                for i in range(len(tiles) + 2):
                    if i < len(tiles):
                        project(i)
                    if 1 <= i <= len(tiles):
                        average(i - 1)
                    if i >= 2:
                        turn(i - 2)
                if m == "NA":
                    u = ("prj", l, "NAv")
                    for c in chunks_of(u):
                        dense(u, c)
                    wait_read(pe, u)
                    for i in range(9):
                        o = 8 * (0, 16, 32, 48, 8, 24, 40)[i] if i < 7 else LAT + P * (i - 7)
                        if i >= 2:
                            pe.wait_ge(*upto(l, "NA_vfree", i - 1))
                        for ct in range(2):
                            mm = pe.transpose((tp, op_)[i % 2][:, P * ct:P * ct + P], buf("NA", "vt")[:, ct, o:o + P], ident)
                        mm.then_inc(ls(l, "NA_vturn"), 1)
                if m == "SW":
                    wait_read(pe, ("prj", l, "SWkv"))
                    pe.wait_ge(*upto(l, "SW_rotread", 3))
                    for i in range(6):
                        if i >= 2:
                            pe.wait_ge(*upto(l, "SW_vfree", i - 1))
                        pe.transpose((tp, op_)[i % 2][:, 0:P], buf("SW", "vt")[:, 0, P * i:P * i + P], ident)\
                          .then_inc(ls(l, "SW_vturn"), 1)

            def attention(m, l):
                jobs = JOBS[m, l]
                nm = 2 if m == "DA" else 1
                pe.wait_ge(*upto(l, m + "_ready", 1))
                first = dense_before[m, l]
                pe.wait_ge(bank_free[0], first)

                def scores(n):
                    j = jobs[n]
                    for mp in range(nm):
                        unit = nm * n + mp
                        if unit >= 2:
                            pe.wait_ge(*upto(l, m + ("_exp" if m == "DA" else "_sfree"), unit - 1))
                        for (o, w, ks, _) in j["segs"]:
                            (qh, ql), (kh, kl) = j["q"][mp], ks[mp]
                            for i, (lhs, rhs) in enumerate(((qh, kh), (qh, kl), (ql, kh))):
                                mm = pe.matmul(sp_[:, 2 * (unit % 2) + o // 512, o % 512:o % 512 + w], lhs, rhs,
                                               start=(i == 0), stop=(i == 2))
                        mm.then_inc(ls(l, m + "_s"), 1)

                def turn(n):
                    j = jobs[n]
                    pe.wait_ge(*upto(l, m + "_p", n + 1))
                    b = piece_base(m, l, n)
                    for i, (k0, k1) in enumerate(pieces(j)):
                        if b + i >= 2:
                            pe.wait_ge(*upto(l, m + "_ptcopied", b + i - 1))
                        for k in range(k0, k1):
                            mm = pe.transpose((tp, op_)[(b + i) % 2][:, P * (k - k0):P * (k - k0) + P], probs(m, n)[:, P * k:P * k + P], ident)
                        mm.then_inc(ls(l, m + "_pt"), 1)

                def weigh(n):
                    j = jobs[n]
                    pe.wait_ge(*upto(l, m + "_ptcopied", piece_base(m, l, n) + len(pieces(j))))
                    if n >= 1:
                        pe.wait_ge(*upto(l, m + "_oread", n))
                    nk = j["n"] // P
                    for k in range(nk):
                        mm = pe.matmul(gp[j["rows"], 0, 0:P], j["v"][k], probs_t(m, n)[:, P * k:P * k + P],
                                       start=(k == 0), stop=(k == nk - 1))
                    mm.then_inc(ls(l, m + "_o"), 1)

                scores(0)
                if m != "DA":
                    scores(1)
                for n in range(len(jobs)):
                    ahead = n + (1 if m == "DA" else 2)
                    if ahead < len(jobs):
                        scores(ahead)
                    turn(n)
                    fill(FILL[m, l][n])
                    weigh(n)
                fill(FILL[m, l][-1])
                pe.wait_ge(*upto(l, m + "_oread", len(jobs)))
                if m == "DA":
                    for i in range(2):
                        pe.wait_ge(*upto(l, "DA_osq", i + 1))
                        for s, (a, b) in enumerate(SEGS[:1] if l == DEPTH - 1 else SEGS):
                            mm = pe.matmul(sp_[:, 2 * i + s, 0:b - a], cf[:, C_B64:C_B64 + P], buf("DA", "y")[:, i, a:b],
                                           start=True, stop=True)
                        mm.then_inc(ls(l, "DA_oms"), 1)

            def hgrn(l):
                last = l == DEPTH - 1
                g = lambda name: ls(l, "HG_" + name)
                gupto = lambda name, value: upto(l, "HG_" + name, value)
                q, cum, k_, v = buf("HG", "q"), buf("HG", "cum"), buf("HG", "k"), buf("HG", "v")
                for name in ("HGf0", "HGf1", "HGg"):
                    u = ("prj", l, name)
                    for c in chunks_of(u):
                        dense(u, c)
                ntile = 4 if last else 6
                pe.wait_ge(*gupto("qdup", 16 * 8))
                pe.wait_ge(*gupto("kready", 4))
                idx = 0

                def weigh(tt, j, i):
                    pe.wait_ge(*gupto("a", i + 1))
                    if j == 0 and tt >= 1:
                        pe.wait_ge(*gupto("oread", tt))
                    for h in range(4):
                        mm = pe.matmul((tp, op_)[h // 2][64 * (h % 2):64 * (h % 2) + 64, 0:P],
                                       v[:, tt, 64 * h:64 * h + 64], buf("HG", "at")[:, i % 2, h, :],
                                       start=(j == 0), stop=(j == 6))
                    mm.then_inc(g("aused"), 1)

                pend = None
                for tt in range(ntile):
                    for j in range(7):
                        if j < 6:
                            pe.wait_ge(*gupto("lev", 6 * tt + j + 1))
                            pe.wait_ge(*gupto("levk", 6 * tt + j + 1))
                        if idx >= 4:
                            pe.wait_ge(*gupto("a", idx - 3))
                        for h in range(4):
                            if j < 6:
                                kk, qq = buf("HGx", "kd")[:, j, h, :], buf("HGx", "qd")[:, j, h, :]
                            else:
                                kk, qq = k_[:, h, P * tt:P * tt + P], q[:, h, P * tt:P * tt + P]
                            mm = pe.matmul(sp_[:, idx % 4, P * h:P * h + P], kk, qq, start=True, stop=True)
                        mm.then_inc(g("sc"), 1)
                        if j < 6:
                            fill(FILL["HG", l][6 * tt + j])
                        if pend:
                            weigh(*pend)
                        pend = (tt, j, idx)
                        idx += 1
                fill(FILL["HG", l][-1])
                weigh(*pend)
                pe.wait_ge(*gupto("a", idx))
                pe.wait_ge(*gupto("oread", ntile))
                def keys(i):
                    tt = STATE_TILES[i]
                    if i >= 2:
                        pe.wait_ge(*gupto("ktcopied", i - 1))
                    for h in range(4):
                        mm = pe.transpose((tp, op_)[i % 2][:, P * h:P * h + P], k_[:, h, P * tt:P * tt + P], ident)
                    mm.then_inc(g("kt"), 1)

                pe.wait_ge(*gupto("ke", 4))
                keys(0)
                for i, tt in enumerate(STATE_TILES):
                    if i + 1 < 6:
                        keys(i + 1)
                    pe.wait_ge(*gupto("ktcopied", i + 1))
                    if i == 0:
                        pe.wait_ge(*gupto("apart", 2))
                    if i >= 2:
                        pe.wait_ge(*gupto("uread", i - 1))
                    out = sp_[:, i % 2, :].rearrange("p (half h v) -> p half h v", half=2, v=64)
                    for h in range(4):
                        mm = pe.matmul(out[:, :, h, :], buf("HG", "at")[:, i % 2, h, :],
                                       buf("HGz", "v")[:, tt, :, 64 * h:64 * h + 64], start=True, stop=True)
                    mm.then_inc(g("u"), 1)
                pe.wait_ge(*gupto("uread", 6))
                pe.wait_ge(*gupto("qe", 4))
                ready = {c: max(FW_ORDER.index(c), BW_ORDER.index(c)) for c in range(12)}
                for s in ((0,) if last else (1, 0)):
                    for c in sorted(range(8 * s, 8 if s == 0 else 12), key=ready.get):
                        pe.wait_ge(*gupto("state", 2 * ready[c]))
                        for h in range(4):
                            out = (tp, op_)[h // 2] if s == 0 else sp_[:, 2 + h // 2, :]
                            mm = pe.matmul(out[64 * (h % 2):64 * (h % 2) + 64, 64 * (c - 8 * s):64 * (c - 8 * s) + 64],
                                           buf("HGx", "s")[:, c, 64 * h:64 * h + 64], q[:, h, 64 * c:64 * c + 64],
                                           start=True, stop=True)
                    mm.then_inc(g("inter"), 1)
                for i in range(2):
                    pe.wait_ge(*gupto("osq", i + 1))
                    for s, (a, b) in enumerate(SEGS[:1] if last else SEGS):
                        mm = pe.matmul(sp_[:, 2 * i + s, 0:b - a], cf[:, C_B64:C_B64 + P], buf("HG", "tmp")[:, i, a:b],
                                       start=True, stop=True)
                    mm.then_inc(g("oms"), 1)

            pe.wait_ge(consts_in, 16)
            pe.wait_ge(params_in, 16 * 5)
            for l in range(DEPTH):
                n = NROWS[l]
                mm = pe.transpose(tp[:, P * l:P * l + n], prow[0:n, l, :], cf[0:n, C_ID:C_ID + n])
            mm.then_inc(ls(0, "pturn"), 1)
            for k in range(KT):
                modulation(("mod", 0, k // 4, k % 4), "row")
                if k == 0:
                    pe.wait_ge(x_in, 32)
                for s, (a, b) in enumerate(SEGS):
                    i = 2 * k + s
                    if i >= 4:
                        pe.wait_ge(*upto(0, "xt_copied", i - 3))
                    for tt in range(a // P, b // P):
                        mm = pe.transpose(sp_[:, i % 4, P * tt - a:P * tt - a + P], xin[:, tt, P * k:P * k + P], ident)
                    mm.then_inc(ls(0, "xt_turned"), 1)
                modulation(("mod", 0, k // 4, k % 4), "turn")
            pe.wait_ge(params2_in, counts["params2"])
            for l in range(DEPTH):
                mm = pe.transpose(op_[:, P * l:P * l + NROWS2], prow2[:, l, :], cf[0:NROWS2, C_ID:C_ID + NROWS2])
            mm.then_inc(ls(0, "pturn2"), 1)

            for l in range(DEPTH):
                last = l == DEPTH - 1
                if l == 0:
                    norm_sums(0, 1, range(KT))
                for m in ("NA", "SW", "DA"):
                    head_norms(m, l)
                    attention(m, l)
                hgrn(l)
                for j in range(4):
                    u = ("out", l, j)
                    if j == 0:
                        dense_unit(u, lambda i: pe.wait_ge(*upto(l, "mixsplit", i + 1)))
                    else:
                        for c in chunks_of(u):
                            dense(u, c)
                    if j >= 1:
                        norm_sums(l, 2, (2 * j - 2, 2 * j - 1))
                norm_sums(l, 2, (KT - 2, KT - 1))
                for q in range(4):
                    for j in range(4):
                        u = ("ff1", l, q, j)
                        if j == q == 0:
                            dense_unit(u, lambda k: pe.wait_ge(*upto(l, "xn2", k + 1)))
                        else:
                            for c in chunks_of(u):
                                dense(u, c)
                    for j in range(4):
                        u = ("ff2", l, q, j)
                        if j == 0:
                            dense_unit(u, lambda k: pe.wait_ge(*upto(l, "h_split", (8 * q + k + 1) * (1 if last else 2))))
                        else:
                            for c in chunks_of(u):
                                dense(u, c)
                        if q == 3 and not last and j >= 1:
                            norm_sums(l + 1, 1, (2 * j - 2, 2 * j - 1))
                if not last:
                    norm_sums(l + 1, 1, (KT - 2, KT - 1))
            pe.wait_ge(*upto(DEPTH - 1, "x_final", 1))
            for tt in range(4):
                for half in range(2):
                    i = 2 * tt + half
                    if i >= 4:
                        pe.wait_ge(*upto(0, "y_copied", i - 3))
                    for k in range(4):
                        mm = pe.transpose(sp_[:, i % 4, P * k:P * k + P], xT[:, 4 * half + k, P * tt:P * tt + P], ident)
                    mm.then_inc(ls(0, "yt"), 1)

        @block.scalar
        def _(act):
            steps = [0]

            def link(ins):
                steps[0] += 1
                ins.then_inc(act_step, 1)
                act.wait_ge(act_step, steps[0])

            nexts = [0]

            def after_unit(u):
                while nexts[0] < len(splits):
                    s = nexts[0]
                    v = splits[s]
                    if index[v] - 2 > index[u] or (s >= 2 and index[splits[s - 2]] > index[u]):
                        return
                    nexts[0] += 1
                    if s >= 2:
                        wait_used(act, splits[s - 2])
                    act.wait_ge(landed[index[v] % 2], landed_at[v])
                    nc.scalar.activation(whi[:, s % 2, :, :], raw[:, index[v] % 2, :, :], ACT.Copy).then_inc(hi_done, 1)

            def fill(slot):
                for u, c in slot:
                    if c == ("row" if u[0] == "mod" else chunks_of(u)[-1]):
                        after_unit(u)

            def norm(l, which):
                segs = SEGS[:1] if (which == 2 and l == DEPTH - 1) else SEGS
                end = segs[-1][1]
                act.wait_ge(*upto(l, f"ms{which}", 1))
                link(nc.scalar.activation(nrs[:, 0:end], sp_[:, 0:2, :].rearrange("p b c -> p (b c)")[:, 0:end],
                                          ACT.Ln, bias=epsc[:, 0:1]))
                nc.scalar.activation(nrs[:, 0:end], nrs[:, 0:end], ACT.Exp, scale=-0.5).then_inc(ls(l, f"rstd{which}"), 1)
                sh = 0 if which == 1 else 3
                for k in range(KT):
                    act.wait_ge(*upto(l, f"nx{which}", k + 1))
                    for s, (a, b) in enumerate(segs):
                        ins = nc.scalar.activation(nt1[:, k % 2, a:b], nt1[:, k % 2, a:b], ACT.Identity,
                                                   bias=mods[:, l, 8 * sh + k, s:s + 1], scale=amod[:, k, s:s + 1])
                    link(ins)
                    nc.scalar.activation(xhi[:, k, 0:end], nt1[:, k % 2, 0:end], ACT.Copy).then_inc(ls(l, f"xhi{which}"), 1)

            def squares(l, which, ks, before=None):
                end = LAT if (which == 2 and l == DEPTH - 1) else T
                for k in ks:
                    if before:
                        for s in range(1 if end == LAT else 2):
                            wait_read(act, None, N(before, (k % 2, s)))
                    if k >= 2:
                        act.wait_ge(*upto(l, f"sq{which}_read", k - 1))
                    nc.scalar.activation(nsq[:, k % 2, 0:end], xT[:, k, 0:end], ACT.Square).then_inc(ls(l, f"sq{which}"), 1)

            def head_norms(m, l):
                tiles = tiles_of(m)

                before = {"SW": "NA", "DA": "SW"}.get(m)
                if before:
                    act.wait_ge(*upto(l, before + "_oread", len(JOBS[before, l])))
                    wait_read(act, ("prj", l, {"SW": "SWkv", "DA": "DAv"}[m]))

                def square(i):
                    n, ct, slot = tiles[i]
                    if i >= 2:
                        act.wait_ge(*upto(l, m + "_scaled", i - 1))
                    end = tile_len(l, n)
                    if m == "NA":
                        act.wait_ge(*upto(l, "NA_copied", i + 1))
                    nc.scalar.activation(buf(m, "y")[:, i % 2, 0:end], buf(m, "xr")[:, slot, 0:end], ACT.Square)\
                      .then_inc(ls(l, m + "_sq"), 1)
                    if m == "NA" and ct == 1:
                        after_unit(("prj", l, n))

                def factor(i):
                    end = tile_len(l, tiles[i][0])
                    act.wait_ge(*upto(l, m + "_ms", i + 1))
                    y = buf(m, "y")[:, i % 2, 0:end]
                    src = sp_[:, 2 * (i % 2):2 * (i % 2) + 2, :].rearrange("p b c -> p (b c)")[:, 0:end]
                    link(nc.scalar.activation(y, src, ACT.Ln, bias=epsc[:, 0:1]))
                    nc.scalar.activation(y, y, ACT.Exp, scale=-0.5).then_inc(ls(l, m + "_rstd"), 1)

                def high(i):
                    end = tile_len(l, tiles[i][0])
                    act.wait_ge(*upto(l, m + ("_scaled" if m == "NA" else "_roped"), i + 1))
                    nc.scalar.activation(hi_parts[m][i][:, 0:end], buf(m, "xr")[:, tiles[i][2], 0:end], ACT.Copy)\
                      .then_inc(ls(l, m + "_high"), 1)

                for i in range(len(tiles) + 3):
                    if i < len(tiles):
                        square(i)
                    if 1 <= i <= len(tiles):
                        factor(i - 1)
                    if i >= 3:
                        high(i - 3)
                if m == "NA":
                    after_unit(("prj", l, "NAv"))
                    for i in range(9):
                        act.wait_ge(*upto(l, "NA_vturn", i + 1))
                        nc.scalar.activation(buf("NA", "v")[:, i, :], (tp, op_)[i % 2][:, 0:256], ACT.Copy)\
                          .then_inc(ls(l, "NA_vfree"), 1)
                if m == "SW":
                    for i in range(6):
                        act.wait_ge(*upto(l, "SW_vturn", i + 1))
                        nc.scalar.activation(buf("SW", "v")[:, i, :], (tp, op_)[i % 2][:, 0:P], ACT.Copy)\
                          .then_inc(ls(l, "SW_vfree"), 1)

            def attention(m, l):
                jobs = JOBS[m, l]
                nm = 2 if m == "DA" else 1

                def expo(n):
                    j = jobs[n]
                    for mp in range(nm):
                        unit = nm * n + mp
                        act.wait_ge(*upto(l, m + "_max", unit + 1))
                        if m == "SW":
                            nc.scalar.activation(small[:, 8 + unit % 4:9 + unit % 4], sink[:, l, j["head"]:j["head"] + 1],
                                                 ACT.Exp, bias=small[:, unit % 4:unit % 4 + 1])
                        if m == "DA":
                            if n >= 2:
                                act.wait_ge(*upto(l, m + "_pt", piece_base(m, l, n - 1)))
                            src = sp_[:, 2 * (unit % 2):2 * (unit % 2) + 2, :].rearrange("p b c -> p (b c)")[:, 0:j["n"]]
                        else:
                            src = probs(m, n)[:, 0:j["n"]]
                        ins = nc.scalar.activation(probs(m, n, mp)[:, 0:j["n"]], src, ACT.Exp,
                                                   bias=small[:, unit % 4:unit % 4 + 1],
                                                   accum_out=small[:, 4 + unit % 4:5 + unit % 4])
                        ins.then_inc(ls(l, m + "_exp"), 1)

                def copy_turned(n):
                    b = piece_base(m, l, n)
                    if n >= 2:
                        act.wait_ge(*upto(l, m + "_o", n - 1))
                    for i, (k0, k1) in enumerate(pieces(jobs[n])):
                        act.wait_ge(*upto(l, m + "_pt", b + i + 1))
                        nc.scalar.activation(probs_t(m, n)[:, P * k0:P * k1], (tp, op_)[(b + i) % 2][:, 0:P * (k1 - k0)], ACT.Copy)\
                          .then_inc(ls(l, m + "_ptcopied"), 1)

                expo(0)
                for n in range(len(jobs)):
                    if m == "DA":
                        copy_turned(n)
                    if n + 1 < len(jobs):
                        expo(n + 1)
                    if m != "DA":
                        copy_turned(n)
                    if n >= 1:
                        fill(FILL[m, l][n - 1])
                if m == "DA":
                    fill(FILL[m, l][-2])
                    fill(FILL[m, l][-1])
                    end = LAT if l == DEPTH - 1 else T
                    act.wait_ge(*upto(l, "DA_oread", len(jobs)))
                    for i in range(2):
                        nc.scalar.activation(buf("DA", "y")[:, i, 0:end], mix[:, i, 0:end], ACT.Square)\
                          .then_inc(ls(l, "DA_osq"), 1)
                    for i in range(2):
                        act.wait_ge(*upto(l, "DA_oms", i + 1))
                        y = buf("DA", "y")[:, i, 0:end]
                        link(nc.scalar.activation(y, sp_[:, 2 * i:2 * i + 2, :].rearrange("p b c -> p (b c)")[:, 0:end],
                                                  ACT.Ln, bias=epsc[:, 0:1]))
                        nc.scalar.activation(y, y, ACT.Exp, scale=-0.5).then_inc(ls(l, "DA_orstd"), 1)

            def hgrn(l):
                last = l == DEPTH - 1
                g = lambda name: ls(l, "HG_" + name)
                gupto = lambda name, value: upto(l, "HG_" + name, value)
                q, cum, k_ = buf("HG", "q"), buf("HG", "cum"), buf("HG", "k")
                tmp = buf("HG", "tmp")
                act.wait_ge(*upto(l, "DA_final", 1))
                end = LAT if last else T
                for h in range(4):
                    for d in range(2):
                        act.dma_start(q[64 * d:64 * d + 64, h, 0:end],
                                      buf("HG", "q1")[64 * (h % 2):64 * (h % 2) + 64, h // 2, 0:end]).then_inc(g("qdup"), 16)
                for half in range(2):
                    u = ("prj", l, f"HGf{half}")
                    for c in chunks_of(u):
                        n = N(u, c)
                        a, b = SEGS[c[1]]
                        act.wait_ge(group_done, n + 1)
                        nc.scalar.activation(cum[:, 2 * half + c[0], a:b], bank(n)[:, 0:b - a], ACT.Sigmoid)\
                          .then_inc(bank_free[group_bank[n]], 1)
                    after_unit(u)
                    nc.scalar.preload_act_table_set("natural_log_exp_and_others")
                    for h in range(2 * half, 2 * half + 2):
                        act.wait_ge(*gupto("fa", h + 1))
                        fa = (tmp, buf("HG", "q1"))[h % 2]
                        nc.scalar.activation(fa[:, 0, :], fa[:, 0, :], ACT.Ln)
                        nc.scalar.activation(fa[:, 1, :], fa[:, 1, :], ACT.Ln).then_inc(g("lnf"), 1)
                u = ("prj", l, "HGg")
                for c in chunks_of(u):
                    n = N(u, c)
                    a, b = SEGS[c[1]]
                    act.wait_ge(group_done, n + 1)
                    nc.scalar.activation(buf("HG", "gate")[:, c[0], a:b], bank(n)[:, 0:b - a], ACT.Sigmoid)\
                      .then_inc(g("eg"), 1)
                after_unit(u)
                nc.scalar.preload_act_table_set("natural_log_exp_and_others")
                ntile = 4 if last else 6
                dbuf = [tmp[:, i, 0:512] for i in range(2)]
                idx = 0

                def read_out(tt):
                    act.wait_ge(*gupto("aused", 7 * (tt + 1)))
                    for i in range(2):
                        ins = nc.scalar.activation(mix[:, 2 + i, P * tt:P * tt + P], (tp, op_)[i][:, 0:P], ACT.Copy)
                    ins.then_inc(g("oread"), 1)

                for tt in range(ntile):
                    for j in range(6):
                        B = 1 << j
                        act.wait_ge(*gupto("d", idx + 1))
                        dv = dbuf[idx % 2].rearrange("p (n two b) -> p n two b", two=2, b=B)
                        nc.scalar.activation(dv[:, :, 0, :], dv[:, :, 0, :], ACT.Exp, scale=cf[:, C_SGN:C_SGN + 1])
                        nc.scalar.activation(dv[:, :, 1, :], dv[:, :, 1, :], ACT.Exp, scale=cf[:, C_SGN + 1:C_SGN + 2])\
                          .then_inc(g("dexp"), 1)
                        if tt >= 1 and j == 3:
                            read_out(tt - 1)
                        if idx >= 4:
                            fill(FILL["HG", l][idx - 4])
                        idx += 1
                read_out(ntile - 1)
                for slot in FILL["HG", l][-5:]:
                    fill(slot)
                for h in range(4):
                    act.wait_ge(*gupto("lastd", h + 1))
                    nc.scalar.activation(tmp[:, h % 2, :], tmp[:, h % 2, :], ACT.Exp, scale=-1.0).then_inc(g("kexp"), 1)
                def qfactor(h):
                    act.wait_ge(*gupto("ke" if h < 2 else "qe", h + 3 if h < 2 else h - 1))
                    nc.scalar.activation(tmp[:, h % 2, 0:end], cum[:, h, 0:end], ACT.Exp).then_inc(g("qexp"), 1)

                act.wait_ge(*gupto("tot", 1))
                nc.scalar.activation(buf("HG", "ref")[:, :, 16:28], buf("HG", "ref")[:, :, 0:12], ACT.Exp).then_inc(g("decay"), 1)
                def keys(i):
                    act.wait_ge(*gupto("kt", i + 1))
                    if i >= 2:
                        act.wait_ge(*gupto("u", i - 1))
                    nc.scalar.activation(buf("HG", "at")[:, i % 2, :, :], (tp, op_)[i % 2][:, :].rearrange("p (h c) -> p h c", c=P), ACT.Copy)\
                      .then_inc(g("ktcopied"), 1)

                keys(0)
                for i, tt in enumerate(STATE_TILES):
                    if i + 1 < 6:
                        keys(i + 1)
                    act.wait_ge(*gupto("u", i + 1))
                    nc.scalar.activation(buf("HGx", "u")[:, 2 * tt:2 * tt + 2, :],
                                         sp_[:, i % 2, :].rearrange("p (half c) -> p half c", half=2), ACT.Copy)\
                      .then_inc(g("uread"), 1)
                    if i in (0, 3):
                        qfactor(i // 3)
                qfactor(2)
                qfactor(3)
                act.wait_ge(*gupto("sc", 7 * ntile))
                for k in MIX_ORDER[:6]:
                    nc.scalar.activation(xhi[:, k, 0:end], mix[:, k, 0:end], ACT.Copy).then_inc(ls(l, "mixhi"), 1)
                act.wait_ge(*gupto("interread", 2 * (1 if last else 2)))
                for i in range(2):
                    nc.scalar.activation(tmp[:, i, 0:end], mix[:, 2 + i, 0:end], ACT.Square).then_inc(g("osq"), 1)
                for i in range(2):
                    act.wait_ge(*gupto("oms", i + 1))
                    y = tmp[:, i, 0:end]
                    link(nc.scalar.activation(y, sp_[:, 2 * i:2 * i + 2, :].rearrange("p b c -> p (b c)")[:, 0:end],
                                              ACT.Ln, bias=epsc[:, 0:1]))
                    nc.scalar.activation(y, y, ACT.Exp, scale=-0.5).then_inc(g("orstd"), 1)

            nc.scalar.preload_act_table_set("natural_log_exp_and_others")
            act.dma_start(xin[:, 0:4, :], t["x"][0].rearrange("(a p) d -> p a d", p=P)).then_inc(x_in, 16)
            act.dma_start(xin[:, 4:6, :], t["ctx"][0].rearrange("(a p) d -> p a d", p=P)).then_inc(x_in, 16)
            act.wait_ge(*upto(0, "pcol_done", 1))
            nc.scalar.activation(siluw[:, :], pcol[:, 0, R_C:R_C + 16], ACT.Exp, scale=-1.0).then_inc(ls(0, "esilu"), 1)
            act.wait_ge(*upto(0, "eps_set", 1))
            for i in range(16):
                k, s = i // 2, i % 2
                if i % 2:
                    a, b = SEGS[s]
                    act.wait_ge(*upto(0, "xt_turned", i + 1))
                    act.wait_ge(*upto(0, "xt_copied", i))
                    nc.scalar.activation(xT[:, k, a:b], sp_[:, i % 4, 0:b - a], ACT.Copy).then_inc(ls(0, "xt_copied"), 1)
            for l in range(DEPTH):
                last = l == DEPTH - 1
                if l == 0:
                    act.wait_ge(*upto(0, "lbdiff", 1))
                    nc.scalar.activation(lbt[:, 1:3, :], lbt[:, 1:3, :], ACT.Exp).then_inc(ls(0, "lbexp"), 1)
                if l == 0:
                    act.wait_ge(*upto(0, "xt_copied", 16))
                    squares(0, 1, range(0, 4))
                act.wait_ge(*upto(l, "lamdot", 1))
                nc.scalar.activation(lams[:, 2:4], lams[:, 0:2], ACT.Exp).then_inc(ls(l, "lamexp"), 1)
                if l == 0:
                    squares(0, 1, range(4, KT))
                    for i in range(8):
                        after_unit(("mod", 0, i // 4, i % 4))
                    act.wait_ge(tables_in, 16)
                norm(l, 1)
                for m, before in (("NA", None), ("SW", "NA"), ("DA", "SW")):
                    head_norms(m, l)
                    if before:
                        fill(FILL[before, l][-2])
                        fill(FILL[before, l][-1])
                    attention(m, l)
                hgrn(l)
                end = LAT if last else T
                for i in (6, 7):
                    k = MIX_ORDER[i]
                    act.wait_ge(*upto(l, "mix_ready", i - 5))
                    nc.scalar.activation(xhi[:, k, 0:end], mix[:, k, 0:end], ACT.Copy).then_inc(ls(l, "mixhi"), 1)
                for j in range(4):
                    u = ("out", l, j)
                    if j < 3:
                        after_unit(u)
                    squares(l, 2, (2 * j, 2 * j + 1), u)
                after_unit(u)
                norm(l, 2)
                for q in range(4):
                    for j in range(4):
                        u = ("ff1", l, q, j)
                        for c in chunks_of(u):
                            n = N(u, c)
                            e = ff_index(l, q, j, c)
                            a, b = SEGS[c[1]]
                            act.wait_ge(group_done, n + 1)
                            if e >= 2:
                                act.wait_ge(*upto(l, "h_split", e - 1))
                            ins = nc.scalar.activation(frel[:, e % 2, 0:b - a], bank(n)[:, 0:b - a], ACT.Relu)
                            ins.then_inc(bank_free[group_bank[n]], 1)
                            act.wait_ge(*upto(l, "h_sq", e + 1))
                            if q > 0:
                                wait_used(act, ("ff2", l, q - 1, 3))
                            nc.scalar.activation(hhi[:, 2 * j + c[0], a:b], frel[:, e % 2, 0:b - a], ACT.Copy)\
                              .then_inc(ls(l, "h_hi"), 1)
                        after_unit(u)
                    for j in range(4):
                        u = ("ff2", l, q, j)
                        if q < 3 or last:
                            after_unit(u)
                            continue
                        if j < 3:
                            after_unit(u)
                        squares(l + 1, 1, (2 * j, 2 * j + 1), u)
                        if j == 3:
                            after_unit(u)

        @block.vector
        def _(dve):
            steps = [0]

            def link(ins):
                steps[0] += 1
                ins.then_inc(dve_step, 1)
                dve.wait_ge(dve_step, steps[0])

            V = nc.vector

            def fill(slot):
                for u, c in slot:
                    n = N(u, c)
                    dve.wait_ge(group_done, n + 1)
                    if c == "row":
                        ins = V.tensor_copy(mrow[0:2, :], bank(n)[0:2, 0:UC])
                    elif c == "turn":
                        _, l, j, i = u
                        r = 8 * j + 2 * i
                        ins = V.tensor_tensor(mods[:, l, r:r + 2, :], bank(n)[:, 0:4].rearrange("p (a b) -> p a b", b=2),
                                              pcol[:, l, R_BMOD + r:R_BMOD + r + 2].unsqueeze(2).to_broadcast([P, 2, 2]), ALU.add)
                    elif c[0] == "tok":
                        ins = V.tensor_copy(buf(u[2][0:2], "v")[:, c[1], :], bank(n)[:, 0:UC])
                    else:
                        a, b = SEGS[c[1]]
                        name = u[2]
                        if name == "SWkv":
                            dst = buf("SW", "vt")[:, 0, a:b] if c[0] else buf("SW", "xr")[:, 2, a:b]
                        elif name == "HGq":
                            dst = buf("HG", "q1")[:, c[0], a:b]
                        else:
                            dst = buf(name[0:2], "xr")[:, (2 if name[2] == "k" else 0) + c[0], a:b]
                        ins = V.tensor_copy(dst, bank(n)[:, 0:b - a])
                    ins.then_inc(bank_free[group_bank[n]], 1)

            def refine(y, ms):
                link(V.scalar_tensor_tensor(out=ms, in0=ms, scalar=EPS, in1=y, op0=ALU.add, op1=ALU.mult))
                link(V.scalar_tensor_tensor(out=ms, in0=ms, scalar=-0.5, in1=y, op0=ALU.mult, op1=ALU.mult))
                return V.scalar_tensor_tensor(out=y, in0=ms, scalar=1.5, in1=y, op0=ALU.add, op1=ALU.mult)

            averages = lambda i, end: sp_[:, 2 * i:2 * i + 2, :].rearrange("p b c -> p (b c)")[:, 0:end]

            def norm(l, which):
                segs = SEGS[:1] if (which == 2 and l == DEPTH - 1) else SEGS
                end = segs[-1][1]
                if which == 1:
                    wait_read(dve, ("mod", 0, 1, 3) if l == 0 else ("mod", DEPTH - 1, 5, 3))
                sh, sc = (0, 1) if which == 1 else (3, 4)
                grow = R_N1 if which == 1 else R_N2
                link(V.tensor_scalar(amod[:, :, :], mods[:, l, 8 * sc:8 * sc + 8, :], 1.0, None, ALU.add))
                link(V.tensor_tensor(amod[:, :, :], amod[:, :, :],
                                     pcol[:, l, grow:grow + 8].unsqueeze(2).to_broadcast([P, 8, 2]), ALU.mult))
                dve.wait_ge(*upto(l, f"rstd{which}", 1))
                link(refine(nrs[:, 0:end], averages(0, end)))

                def low(k):
                    dve.wait_ge(*upto(l, f"xhi{which}", k + 1))
                    V.tensor_tensor(xlo[:, k, 0:end], nt1[:, k % 2, 0:end], xhi[:, k, 0:end].bitcast(F32), ALU.subtract)\
                     .then_inc(ls(l, f"xn{which}"), 1)

                for k in range(KT):
                    if k >= 2:
                        dve.wait_ge(*upto(l, f"xn{which}", k - 1))
                    V.tensor_tensor(nt1[:, k % 2, 0:end], xT[:, k, 0:end], nrs[:, 0:end], ALU.mult).then_inc(ls(l, f"nx{which}"), 1)
                    if k >= 1:
                        low(k - 1)
                low(KT - 1)

            def head_norms(m, l):
                tiles = tiles_of(m)
                xr = buf(m, "xr")

                def copy(i):
                    n, ct, slot = tiles[i]
                    if m != "NA":
                        return
                    for s, (a, b) in enumerate(tile_segs(l, n)):
                        g = N(("prj", l, n), (ct, s))
                        dve.wait_ge(group_done, g + 1)
                        out, src = xr[:, slot, a:b], bank(g)[:, 0:b - a]
                        if s == 0:
                            out = out.rearrange("p (c r) -> p r c", r=8)
                            src = src.rearrange("p (r c) -> p r c", c=GRID)
                        V.tensor_copy(out, src).then_inc(bank_free[group_bank[g]], 1)
                    wait_read(dve, None, g)
                    V.memset(small[:, 20:21], 0.0).then_inc(ls(l, "NA_copied"), 1)

                def scale(i):
                    n, ct, slot = tiles[i]
                    end = tile_len(l, n)
                    gain = gq[:, GAIN[n]:GAIN[n] + 1] if n in GAIN else \
                        pcol2[:, l, {"NAk": G_NAK, "SWkv": G_SWK, "DAk": G_DAK}[n]:][:, 0:1]
                    dve.wait_ge(*upto(l, m + "_rstd", i + 1))
                    link(refine(buf(m, "y")[:, i % 2, 0:end], averages(i % 2, end)))
                    ins = V.scalar_tensor_tensor(out=xr[:, slot, 0:end], in0=xr[:, slot, 0:end], scalar=gain,
                                                 in1=buf(m, "y")[:, i % 2, 0:end], op0=ALU.mult, op1=ALU.mult)
                    ins.then_inc(ls(l, m + "_scaled"), 1)
                    dve.wait_ge(*upto(l, m + "_scaled", i + 1))

                def rope(i):
                    if m == "NA":
                        return
                    slot = tiles[i][2]
                    _, cc, cs = ROPE[m]
                    rot = buf(m, "rot")[:, i % 2, :]
                    dve.wait_ge(*upto(l, m + "_rot", i + 1))
                    V.tensor_tensor(rot, (tp, op_)[i % 2][:, :], cf[:, cs:cs + LAT], ALU.mult).then_inc(ls(l, m + "_rotread"), 1)
                    link(V.tensor_tensor(xr[:, slot, 0:LAT], xr[:, slot, 0:LAT], cf[:, cc:cc + LAT], ALU.mult))
                    V.tensor_tensor(xr[:, slot, 0:LAT], xr[:, slot, 0:LAT], rot, ALU.add).then_inc(ls(l, m + "_roped"), 1)

                def low(i):
                    slot = tiles[i][2]
                    end = tile_len(l, tiles[i][0])
                    dve.wait_ge(*upto(l, m + "_high", i + 1))
                    V.tensor_tensor(lo_parts[m][:, slot, 0:end], xr[:, slot, 0:end], hi_parts[m][i][:, 0:end].bitcast(F32),
                                    ALU.subtract).then_inc(ls(l, m + "_low"), 1)

                for i in range(len(tiles) + 3):
                    if i < len(tiles):
                        copy(i)
                    if 1 <= i <= len(tiles):
                        scale(i - 1)
                    if 2 <= i < len(tiles) + 2:
                        rope(i - 2)
                    if i >= 3:
                        low(i - 3)
                if m == "NA":
                    for ct in range(2):
                        for s, (a, b) in enumerate(SEGS):
                            g = N(("prj", l, "NAv"), (ct, s))
                            dve.wait_ge(group_done, g + 1)
                            out, src = buf("NA", "vt")[:, ct, a:b], bank(g)[:, 0:b - a]
                            if s == 0:
                                out = out.rearrange("p (c r) -> p r c", r=8)
                                src = src.rearrange("p (r c) -> p r c", c=GRID)
                            ins = V.tensor_copy(out, src)
                            ins.then_inc(bank_free[group_bank[g]], 1)
                dve.wait_ge(*upto(l, m + "_low", len(tiles)))
                if m == "NA":
                    dve.wait_ge(*upto(l, "NA_vfree", 9))
                    dve.wait_ge(*upto(l, "bias_masked", 12))
                if m == "SW":
                    dve.wait_ge(*upto(l, "SW_vfree", 6))
                V.memset(small[:, 16:17], 0.0).then_inc(ls(l, m + "_ready"), 1)

            def attention(m, l):
                jobs = JOBS[m, l]
                nm = 2 if m == "DA" else 1

                def maxima(n):
                    j = jobs[n]
                    for mp in range(nm):
                        unit = nm * n + mp
                        c = small[:, unit % 4:unit % 4 + 1]
                        dve.wait_ge(*upto(l, m + "_s", unit + 1))
                        full = sp_[:, 2 * (unit % 2):2 * (unit % 2) + 2, :].rearrange("p b c -> p (b c)")
                        if m == "DA":
                            V.tensor_reduce(c, full[:, 0:j["n"]], AX.X, ALU.max, negate=True).then_inc(ls(l, m + "_max"), 1)
                            continue
                        p = probs(m, n)
                        if n >= 2:
                            dve.wait_ge(*upto(l, m + "_pt", piece_base(m, l, n - 1)))
                        if m == "NA":
                            if j["bias"]:
                                V.tensor_tensor(p[:, 0:256], full[:, 0:256], j["bias"][2], ALU.add)
                            o, w, d = j["rest"]
                            sfree(V.tensor_copy(p[:, d:d + w], full[:, o:o + w]), unit)
                            V.tensor_reduce(c, p[:, 0:j["n"]], AX.X, ALU.max, negate=True).then_inc(ls(l, m + "_max"), 1)
                        else:
                            w = j["w"]
                            for o, mask in j["masks"]:
                                V.tensor_tensor(p[:, o:o + P], full[:, o:o + P], mask, ALU.add)
                            if j["plain"] is not None:
                                V.tensor_copy(p[:, j["plain"]:j["plain"] + P], full[:, j["plain"]:j["plain"] + P])
                            o = 512 if w else 0
                            sfree(V.tensor_copy(p[:, w:w + 256], full[:, o:o + 256]), unit)
                            link(V.tensor_reduce(c, p[:, 0:j["n"]], AX.X, ALU.max))
                            V.tensor_scalar(c, c, sink[:, l, j["head"]:j["head"] + 1], -1.0, ALU.max, ALU.mult)\
                             .then_inc(ls(l, m + "_max"), 1)

                def sfree(ins, unit):
                    ins.then_inc(ls(l, m + "_sfree"), 1)
                    dve.wait_ge(*upto(l, m + "_sfree", unit + 1))

                def finish(n):
                    j = jobs[n]
                    u0 = nm * n
                    dve.wait_ge(*upto(l, m + "_exp", u0 + nm))
                    sums = small[:, 4 + u0 % 4:4 + u0 % 4 + nm]
                    if m == "SW":
                        link(V.tensor_tensor(sums, sums, small[:, 8 + u0 % 4:9 + u0 % 4], ALU.add))
                    link(V.reciprocal(sums, sums))
                    p = probs(m, n)[:, 0:j["n"]]
                    if m == "DA":
                        s1 = small[:, 5 + u0 % 4:6 + u0 % 4]
                        V.tensor_tensor(s1, s1, nlam[:, :], ALU.mult)
                        link(V.tensor_scalar(p, p, small[:, 4 + u0 % 4:5 + u0 % 4], None, ALU.mult))
                        V.scalar_tensor_tensor(out=p, in0=probs(m, n, 1)[:, 0:j["n"]], scalar=s1, in1=p,
                                               op0=ALU.mult, op1=ALU.add).then_inc(ls(l, m + "_p"), 1)
                    else:
                        V.tensor_scalar(p, p, sums, None, ALU.mult).then_inc(ls(l, m + "_p"), 1)

                def output(n):
                    j = jobs[n]
                    dve.wait_ge(*upto(l, m + "_o", n + 1))
                    src = gp[j["rows"], 0, 0:P]
                    dst = mix[j["rows"], MIXT[m] + j["head"] // 2, :]
                    if j["out"][0] == "grid":
                        dst = dst[:, 0:LAT].rearrange("p (r c) -> p c r", c=GRID)[:, 16 * j["out"][1]:16 * j["out"][1] + 16, :]
                        src = src.rearrange("p (c r) -> p c r", r=8)
                    else:
                        dst = dst[:, j["out"][1]:j["out"][1] + P]
                    ins = V.tensor_copy(dst, src)
                    ins.then_inc(ls(l, m + "_oread"), 1)

                maxima(0)
                for n in range(len(jobs)):
                    if m == "DA":
                        finish(n)
                        if n >= 1:
                            fill(FILL[m, l][n - 1])
                    if n + 1 < len(jobs):
                        maxima(n + 1)
                    if m != "DA":
                        finish(n)
                        if n >= 1:
                            fill(FILL[m, l][n - 1])
                    if n >= 1:
                        output(n - 1)
                fill(FILL[m, l][-2])
                output(len(jobs) - 1)
                fill(FILL[m, l][-1])
                if m == "DA":
                    end = LAT if l == DEPTH - 1 else T
                    for i in range(2):
                        dve.wait_ge(*upto(l, "DA_orstd", i + 1))
                        link(refine(buf("DA", "y")[:, i, 0:end], averages(i, end)))
                        ins = V.scalar_tensor_tensor(out=mix[:, i, 0:end], in0=mix[:, i, 0:end], scalar=gq[:, 3:4],
                                                     in1=buf("DA", "y")[:, i, 0:end], op0=ALU.mult, op1=ALU.mult)
                    ins.then_inc(ls(l, "DA_final"), 1)

            def hgrn(l):
                last = l == DEPTH - 1
                g = lambda name: ls(l, "HG_" + name)
                gupto = lambda name, value: upto(l, "HG_" + name, value)
                q, cum, k_ = buf("HG", "q"), buf("HG", "cum"), buf("HG", "k")
                tmp, ref = buf("HG", "tmp"), buf("HG", "ref")
                qd, kd = buf("HGx", "qd"), buf("HGx", "kd")

                dve.wait_ge(*gupto("qdup", 16 * 8))

                def gates(h):
                    c = cum[:, h, :]
                    fa = (tmp, buf("HG", "q1"))[h % 2]
                    if h >= 2:
                        dve.wait_ge(*gupto("cumdone", h - 1))
                    for s in range(2):
                        wait_read(dve, None, N(("prj", l, f"HGf{h // 2}"), (h % 2, s)))
                    if l > 0:
                        link(V.tensor_scalar(c, c, lbt[:, 4, h:h + 1], lbt[:, 3, h:h + 1], ALU.mult, ALU.add))
                    V.tensor_scalar(k_[:, h, :], c, -1.0, 1.0, ALU.mult, ALU.add).then_inc(g("kready"), 1)
                    V.tensor_scalar(fa[:, 0, :], c, 2.0 ** -60, None, ALU.max)
                    V.tensor_scalar(fa[:, 1, :], c, 2.0 ** -124, 2.0 ** 60, ALU.max, ALU.mult).then_inc(g("fa"), 1)

                def sums(h):
                    c = cum[:, h, :]
                    fa = (tmp, buf("HG", "q1"))[h % 2]
                    dve.wait_ge(*gupto("lnf", h + 1))
                    link(V.scalar_tensor_tensor(out=c, in0=fa[:, 1, :], scalar=0.0, in1=fa[:, 0, :], op0=ALU.min, op1=ALU.add))
                    V.tensor_tensor_scan(cum[FW, h, :], cb[FW, B_RST:B_RST + T], cum[FW, h, :], 0.0, ALU.mult, ALU.add)
                    ins = V.tensor_tensor_scan(cum[BW, h, ::-1], cb[BW, B_RST:B_RST + T][:, ::-1], cum[BW, h, ::-1],
                                               0.0, ALU.mult, ALU.add)
                    ins.then_inc(g("cumdone"), 1)

                gates(0)
                for h in range(4):
                    if h % 2 == 0:
                        gates(h + 1)
                    sums(h)
                    if h == 1:
                        gates(2)
                gate = buf("HG", "gate")
                u = ("prj", l, "HGg")
                for i, c in enumerate(chunks_of(u)):
                    n = N(u, c)
                    a, b = SEGS[c[1]]
                    dve.wait_ge(*gupto("eg", i + 1))
                    ins = V.tensor_tensor(gate[:, c[0], a:b], gate[:, c[0], a:b], bank(n)[:, 0:b - a], ALU.mult)
                    ins.then_inc(bank_free[group_bank[n]], 1)
                wait_used(dve, u)
                V.memset(qd[:, :, :, :], 0.0).then_inc(g("qcleared"), 1)
                dve.wait_ge(*gupto("qcleared", 1))
                dve.wait_ge(*gupto("cumdone", 4))
                ntile = 4 if last else 6
                dbuf = [tmp[:, i, 0:512] for i in range(2)]

                def products(tt, j, idx):
                    B = 1 << j
                    dve.wait_ge(*gupto("dexp", idx + 1))
                    if tt >= 1:
                        dve.wait_ge(*gupto("sc", 7 * (tt - 1) + j + 1))
                    dv = dbuf[idx % 2].rearrange("p (h n two b) -> p h n two b", h=4, two=2, b=B)
                    for r, side in ((FW, 1), (BW, 0)):
                        o = qd[r, j, :, :].rearrange("p h (n two b) -> p h n two b", two=2, b=B)[:, :, :, side, :]
                        i0 = q[r, :, P * tt:P * tt + P].rearrange("p h (n two b) -> p h n two b", two=2, b=B)[:, :, :, side, :]
                        ins = V.tensor_tensor(o, i0, dv[r, :, :, side, :], ALU.mult)
                    ins.then_inc(g("lev"), 1)

                def differences(tt, j, idx):
                    B = 1 << j
                    nb = P // (2 * B)
                    ct = cum[:, :, P * tt:P * tt + P].rearrange("p h (n w) -> p h n w", w=2 * B)
                    V.tensor_copy(ref[FW, :, 0:nb], ct[FW, :, :, B - 1])
                    link(V.tensor_copy(ref[BW, :, 0:nb], ct[BW, :, :, B]))
                    if idx >= 2:
                        dve.wait_ge(*gupto("lev", idx - 1))
                        dve.wait_ge(*gupto("levk", idx - 1))
                    d = dbuf[idx % 2].rearrange("p (h n w) -> p h n w", h=4, w=2 * B)
                    ins = V.tensor_tensor(d, ct, ref[:, :, 0:nb].unsqueeze(3).to_broadcast([P, 4, nb, 2 * B]), ALU.subtract)
                    ins.then_inc(g("d"), 1)
                    dve.wait_ge(*gupto("d", idx + 1))

                def masked(i):
                    dve.wait_ge(*gupto("sc", i + 1))
                    if i >= 2:
                        dve.wait_ge(*gupto("aused", i - 1))
                    m = cb[:, P * (i % 7):P * (i % 7) + P].unsqueeze(1).to_broadcast([P, 4, P])
                    V.tensor_tensor(buf("HG", "at")[:, i % 2, :, :], sp_[:, i % 4, :].rearrange("p (h c) -> p h c", c=P), m, ALU.mult)\
                     .then_inc(g("a"), 1)

                levels = [(tt, j) for tt in range(ntile) for j in range(6)]
                differences(*levels[0], 0)
                done = 0
                for idx, (tt, j) in enumerate(levels):
                    if idx + 1 < len(levels):
                        differences(*levels[idx + 1], idx + 1)
                    products(tt, j, idx)
                    while done < 7 * tt + j - 1:
                        masked(done)
                        done += 1
                    if idx >= 1:
                        fill(FILL["HG", l][idx - 1])
                fill(FILL["HG", l][-2])
                fill(FILL["HG", l][-1])
                while done < 7 * ntile:
                    masked(done)
                    done += 1
                dve.wait_ge(*gupto("levk", 6 * ntile))
                dve.wait_ge(*gupto("oread", ntile))
                dve.wait_ge(*gupto("sc", 7 * ntile))
                cc = cum[:, :, :].rearrange("p h (c w) -> p h c w", w=64)
                V.tensor_copy(ref[FW, :, 0:12], cc[FW, :, :, 63])
                ins = V.tensor_copy(ref[BW, :, 0:12], cc[BW, :, :, 0])
                ins.then_inc(g("tot"), 1)
                dve.wait_ge(*gupto("tot", 1))
                end = LAT if last else T

                def kdiff(h):
                    V.tensor_tensor(tmp[:, h % 2, :].rearrange("p (c w) -> p c w", w=64), cc[:, h, :, :],
                                    ref[:, h, 0:12].unsqueeze(2).to_broadcast([P, 12, 64]), ALU.subtract)\
                     .then_inc(g("lastd"), 1)

                def kscale(h):
                    dve.wait_ge(*gupto("kexp", h + 1))
                    ins = V.tensor_tensor(k_[:, h, :], k_[:, h, :], tmp[:, h % 2, :], ALU.mult)
                    ins.then_inc(g("ke"), 1)
                    dve.wait_ge(*gupto("ke", h + 1))

                kdiff(0)
                kdiff(1)
                kscale(0)
                kdiff(2)
                kscale(1)
                kdiff(3)
                kscale(2)
                kscale(3)
                st, uu = buf("HGx", "s"), buf("HGx", "u")
                dve.wait_ge(*gupto("decay", 1))
                fw, bw = FW_ORDER, BW_ORDER
                V.memset(st[FW, fw[0], :], 0.0)
                link(V.memset(st[BW, bw[0], :], 0.0))
                for i in range(11):
                    if i in (0, 4, 6):
                        dve.wait_ge(*gupto("uread", {0: 2, 4: 4, 6: 6}[i]))
                    for r, order in ((FW, fw), (BW, bw)):
                        c, d = order[i], order[i + 1]
                        V.tensor_tensor(st[r, d, :].rearrange("p (h v) -> p h v", v=64), st[r, c, :].rearrange("p (h v) -> p h v", v=64),
                                        ref[r, :, 16 + c].unsqueeze(2).to_broadcast([64, 4, 64]), ALU.mult).then_inc(dve_step, 1)
                        steps[0] += 1
                    dve.wait_ge(dve_step, steps[0])
                    for r, order in ((FW, fw), (BW, bw)):
                        c, d = order[i], order[i + 1]
                        V.tensor_tensor(st[r, d, :], st[r, d, :], uu[r, c, :], ALU.add).then_inc(g("state"), 1)
                    dve.wait_ge(*gupto("state", 2 * (i + 1)))
                for n, s in enumerate((0,) if last else (1, 0)):
                    a, b = SEGS[s]
                    dve.wait_ge(*gupto("inter", n + 1))
                    for i in range(2):
                        src = (tp, op_)[i][:, 0:b - a] if s == 0 else sp_[:, 2 + i, 0:b - a]
                        V.tensor_tensor(mix[:, 2 + i, a:b], mix[:, 2 + i, a:b], src, ALU.add).then_inc(g("interread"), 1)
                for i in range(6):
                    mix_low(l, i)
                for i in range(2):
                    dve.wait_ge(*gupto("orstd", i + 1))
                    link(refine(tmp[:, i, 0:end], averages(i, end)))
                    m = mix[:, 2 + i, 0:end]
                    link(V.scalar_tensor_tensor(out=m, in0=m, scalar=pcol2[:, l, G_HGO:G_HGO + 1], in1=tmp[:, i, 0:end],
                                                op0=ALU.mult, op1=ALU.mult))
                    V.tensor_tensor(m, m, gate[:, i, 0:end], ALU.mult).then_inc(ls(l, "mix_ready"), 1)

            def mix_low(l, i):
                k = MIX_ORDER[i]
                end = LAT if l == DEPTH - 1 else T
                dve.wait_ge(*upto(l, "mixhi", i + 1))
                V.tensor_tensor(xlo[:, k, 0:end], mix[:, k, 0:end], xhi[:, k, 0:end].bitcast(F32), ALU.subtract)\
                 .then_inc(ls(l, "mixsplit"), 1)

            def add_back(u, gate_chunk, l, link_last=False):
                for c in chunks_of(u):
                    n = N(u, c)
                    j = u[-1]
                    k = 2 * j + c[0]
                    a, b = SEGS[c[1]]
                    dve.wait_ge(group_done, n + 1)
                    ins = V.scalar_tensor_tensor(out=xT[:, k, a:b], in0=bank(n)[:, 0:b - a],
                                                 scalar=mods[:, l, 8 * gate_chunk + k, c[1]:c[1] + 1], in1=xT[:, k, a:b],
                                                 op0=ALU.mult, op1=ALU.add)
                    ins.then_inc(bank_free[group_bank[n]], 1)
                return ins

            dve.wait_ge(*upto(0, "pturn", 1))
            ins = V.tensor_copy(pcol[:, 0, :], tp[:, 0:NROWS[0]])
            ins = V.tensor_copy(pcol[:, 1, 0:NROWS[1]], tp[:, P:P + NROWS[1]])
            ins.then_inc(ls(0, "pcol_done"), 1)
            dve.wait_ge(*upto(0, "pcol_done", 1))
            dve.wait_ge(*upto(0, "esilu", 1))
            link(V.tensor_scalar(siluw[:, :], siluw[:, :], 1.0, None, ALU.add))
            link(V.reciprocal(siluw[:, :], siluw[:, :]))
            V.tensor_tensor(silu_c[:, :, :], siluw[:, :].rearrange("p (j k) -> p k j", j=2),
                            pcol[:, 0, R_C:R_C + 16].rearrange("p (j k) -> p k j", j=2), ALU.mult)\
             .then_inc(ls(0, "silu_done"), 1)
            for k in range(KT):
                i = 2 * k
                fill([(("mod", 0, k // 4, k % 4), "row")])
                dve.wait_ge(*upto(0, "xt_turned", i + 1))
                if i:
                    dve.wait_ge(*upto(0, "xt_copied", i))
                ins = V.tensor_copy(xT[:, k, 0:LAT], sp_[:, i % 4, :])
                ins.then_inc(ls(0, "xt_copied"), 1)
                fill([(("mod", 0, k // 4, k % 4), "turn")])
            dve.wait_ge(*upto(0, "xt_copied", 16))
            dve.wait_ge(*upto(0, "pturn2", 1))
            link(V.tensor_copy(pcol2[:, :, :], op_[:, 0:2 * P].rearrange("p (l r) -> p l r", r=P)[:, :, 0:NROWS2]))
            link(V.tensor_copy(cb[:, :], cbf[:, :]))
            link(V.tensor_tensor(lbt[:, 0, :], pcol2[:, 0, R_LB:R_LB + 4], pcol2[:, 0, R_LB + 4:R_LB + 8], ALU.max))
            V.tensor_tensor(lbt[:, 1:3, :], pcol2[:, 0, R_LB:R_LB + 8].rearrange("p (a b) -> p a b", b=4),
                            lbt[:, 0, :].unsqueeze(1).to_broadcast([P, 2, 4]), ALU.subtract).then_inc(ls(0, "lbdiff"), 1)
            for l in range(DEPTH):
                last = l == DEPTH - 1
                if l == 0:
                    dve.wait_ge(*upto(0, "lbexp", 1))
                    link(V.tensor_tensor(lbt[:, 0, :], lbt[:, 1, :], lbt[:, 2, :], ALU.add))
                    link(V.reciprocal(lbt[:, 0, :], lbt[:, 0, :]))
                    link(V.tensor_tensor(lbt[:, 1:3, :], lbt[:, 1:3, :], lbt[:, 0, :].unsqueeze(1).to_broadcast([P, 2, 4]), ALU.mult))
                    link(V.tensor_tensor(lbt[:, 3, :], lbt[:, 1, :], lbt[:, 2, :], ALU.add))
                    link(V.tensor_tensor(lbt[:, 3, :], lbt[:, 3, :], lbt[:, 1, :], ALU.subtract))
                    link(V.tensor_scalar(lbt[:, 4, :], lbt[:, 3, :], -1.0, 1.0, ALU.mult, ALU.add))
                lam_init = 0.8 - 0.6 * math.exp(-0.3 * l)
                link(V.tensor_tensor(lamt[:, :, :], lamv[:, l, 0:4:2, :], lamv[:, l, 1:4:2, :], ALU.mult))
                V.tensor_reduce(lams[:, 0:2], lamt[:, :, :], AX.X, ALU.add).then_inc(ls(l, "lamdot"), 1)
                V.tensor_scalar(gq[:, 0:1], pcol2[:, l, G_NAQ:G_NAQ + 1], 64 ** -0.5, None, ALU.mult)
                V.tensor_scalar(gq[:, 1:2], pcol2[:, l, G_SWQ:G_SWQ + 1], 64 ** -0.5, None, ALU.mult)
                V.tensor_scalar(gq[:, 2:3], pcol2[:, l, G_DAQ:G_DAQ + 1], 32 ** -0.5, None, ALU.mult)
                link(V.tensor_scalar(gq[:, 3:4], pcol2[:, l, G_DAS:G_DAS + 1], 1.0 - lam_init, None, ALU.mult))
                dve.wait_ge(*upto(l, "lamexp", 1))
                link(V.tensor_tensor(lams[:, 0:1], lams[:, 3:4], lams[:, 2:3], ALU.subtract))
                link(V.tensor_scalar(nlam[:, :], lams[:, 0:1], -lam_init, None, ALU.add))
                dve.wait_ge(tables_in, 16)
                link(V.memset(e2[:, :, :, :], 0.0))
                V.memset(small[:, 18:19], 0.0).then_inc(ls(l, "e2_zero"), 1)
                norm(l, 1)
                dve.wait_ge(*upto(l, "rpb_in", 16 * 8))
                V.tensor_copy(e2[:, :, 16:47, :], e1[:, :, :, :].rearrange("p h r j -> p h j r")).then_inc(ls(l, "e2_done"), 1)
                for m in ("NA", "SW", "DA"):
                    head_norms(m, l)
                    attention(m, l)
                hgrn(l)
                for i in (6, 7):
                    mix_low(l, i)
                for j in range(4):
                    add_back(("out", l, j), 2, l)
                wait_read(dve, ("out", l, 3))
                norm(l, 2)
                for q in range(4):
                    for j in range(4):
                        u = ("ff1", l, q, j)
                        for c in chunks_of(u):
                            e = ff_index(l, q, j, c)
                            a, b = SEGS[c[1]]
                            r = frel[:, e % 2, 0:b - a]
                            wait_read(dve, None, N(u, c))
                            V.tensor_tensor(r, r, r, ALU.mult).then_inc(ls(l, "h_sq"), 1)
                            dve.wait_ge(*upto(l, "h_hi", e + 1))
                            V.tensor_tensor(hlo[:, 2 * j + c[0], a:b], r, hhi[:, 2 * j + c[0], a:b].bitcast(F32), ALU.subtract)\
                             .then_inc(ls(l, "h_split"), 1)
                    for j in range(4):
                        add_back(("ff2", l, q, j), 5, l)
                    wait_read(dve, ("ff2", l, q, 3))
                V.memset(small[:, 19:20], 0.0).then_inc(ls(l, "x_final"), 1)
            for i in range(8):
                tt, half = i // 2, i % 2
                dve.wait_ge(*upto(0, "yt", i + 1))
                ins = V.tensor_copy(xin[:, tt, 512 * half:512 * half + 512], sp_[:, i % 4, :])
                ins.then_inc(ls(0, "y_copied"), 1)


INPUTS = ("x", "c", "ctx", "c_ctx", "w_mod", "b_mod", "norm1_g", "norm2_g", "w_in", "w_out", "da_q_gain", "da_k_gain",
          "da_lambda", "da_sub_gain", "hg_lb_logits", "hg_out_gain", "na_q_gain", "na_k_gain", "na_rpb", "sw_q_gain",
          "sw_k_gain", "sw_sink", "w_ff1", "w_ff2")


def program(nc, shapes):
    t = {n: nc.dram_tensor(f"in_{n}", shape, F32, kind="ExternalInput").ap() for n, shape in shapes.items()}
    t["cf"] = nc.dram_tensor("const_f", (P, NCF), F32, kind="ExternalInput").ap()
    t["cb"] = nc.dram_tensor("const_b", (P, NCB), F32, kind="ExternalInput").ap()
    t["out"] = nc.dram_tensor("out", (1, LAT, D), F32, kind="ExternalOutput").ap()
    build(nc, t)


def kernel(**inputs):
    import concourse.bacc as bacc
    from concourse.bass_utils import run_bass_kernel_spmd

    nc = bacc.Bacc("TRN2", target_bir_lowering=False, num_devices=1, dynamic_dma_scratch_size=1024)
    arrays = {n: np.ascontiguousarray(inputs[n]) for n in INPUTS}
    program(nc, {n: a.shape for n, a in arrays.items()})
    f, b = shape_constants()
    sent = {f"in_{n}": a for n, a in arrays.items()}
    sent["const_f"], sent["const_b"] = f, b
    r = run_bass_kernel_spmd(nc, [sent], core_ids=[0])
    return r.results[0]["out"]
```
